# Optimizing a Trainium2 kernel written in Bass

```python
import math
import jax, jax.numpy as jnp
from jax import lax
import numpy as np

D_MODEL = 1024
BATCH = 1
SEQ = 256
DEPTH = 1

MEM_LEN = 256
D_MIX = D_MODEL
SSD_DIM = D_MIX // 2
SSD_HEAD_DIM = 64
SSD_HEADS = SSD_DIM // SSD_HEAD_DIM
SSD_GROUPS = 2
SSD_STATE = 64
CONV_K = 4
CHUNK = 128
SB_DIM = D_MIX - SSD_DIM
SB_HEAD_DIM = 64
SB_HEADS = SB_DIM // SB_HEAD_DIM
Q_BLOCK = 128
XA_HEADS = 4
XA_HEAD_DIM = 128
XA_DIM = XA_HEADS * XA_HEAD_DIM
D_FF = 4 * D_MODEL
EPS = 1e-5
GN = SSD_GROUPS * SSD_STATE
CONV_DIM = SSD_DIM + 2 * GN
IN_DIM = SSD_DIM + CONV_DIM + SSD_HEADS + 3 * SB_DIM


def rmsnorm(x, g):
    xf = x.astype(jnp.float32)
    y = xf * lax.rsqrt(jnp.mean(xf * xf, axis=-1, keepdims=True) + EPS)
    return (y * g.astype(jnp.float32)).astype(x.dtype)

def causal_dwconv(x, w, b):
    y = lax.conv_general_dilated(
        x, w.astype(x.dtype)[:, None, :], window_strides=(1,), padding=[(CONV_K - 1, 0)],
        dimension_numbers=("NWC", "WIO", "NWC"), feature_group_count=x.shape[-1])
    return y + b.astype(x.dtype)

def ssd_chunked(xh, dt, a, bm, cm):
    b, s, h, p = xh.shape
    g, n = bm.shape[-2:]
    e = h // g
    nc = s // CHUNK
    x_c = (xh * dt[..., None]).reshape(b, nc, CHUNK, g, e, p)
    a_c = (dt * a).reshape(b, nc, CHUNK, g, e)
    b_c = bm.reshape(b, nc, CHUNK, g, n)
    c_c = cm.reshape(b, nc, CHUNK, g, n)
    a_cum = jnp.cumsum(a_c, axis=2)
    seg = a_cum[:, :, :, None] - a_cum[:, :, None, :]
    causal = jnp.tril(jnp.ones((CHUNK, CHUNK), dtype=bool))[:, :, None, None]
    decay = jnp.exp(jnp.where(causal, seg, -jnp.inf))
    cb = jnp.einsum("bclgn,bcsgn->bclsg", c_c, b_c)
    y_diag = jnp.einsum("bclsg,bclsge,bcsgep->bclgep", cb, decay, x_c)
    decay_states = jnp.exp(a_cum[:, :, -1:] - a_cum)
    states = jnp.einsum("bclgn,bclge,bclgep->bcgepn", b_c, decay_states, x_c)
    chunk_decay = jnp.exp(a_cum[:, :, -1])

    def step(prev, inp):
        st, dec = inp
        return prev * dec[..., None, None] + st, prev

    init = jnp.zeros((b, g, e, p, n), jnp.float32)
    _, prev_states = lax.scan(step, init, (jnp.swapaxes(states, 0, 1), jnp.swapaxes(chunk_decay, 0, 1)))
    prev_states = jnp.swapaxes(prev_states, 0, 1)
    y_off = jnp.einsum("bclgn,bcgepn,bclge->bclgep", c_c, prev_states, jnp.exp(a_cum))
    return (y_diag + y_off).reshape(b, s, h, p)

def stick_breaking_attention(q, k, v):
    s_len, dh = q.shape[2], q.shape[3]
    scale = 1.0 / math.sqrt(dh)
    outs = []
    for i in range(s_len // Q_BLOCK):
        start = i * Q_BLOCK
        end = start + Q_BLOCK
        qb = q[:, :, start:end].astype(jnp.float32)
        kb = k[:, :, :end].astype(jnp.float32)
        vb = v[:, :, :end].astype(jnp.float32)
        logits = jnp.einsum("bhqd,bhkd->bhqk", qb, kb) * scale
        t_pos = start + jnp.arange(Q_BLOCK)[:, None]
        s_pos = jnp.arange(end)[None, :]
        mask = s_pos < t_pos
        log_stay = jnp.where(mask, jax.nn.log_sigmoid(-logits), 0.0)
        log_beta = jax.nn.log_sigmoid(logits)
        later = lax.cumsum(log_stay, axis=3, reverse=True) - log_stay
        w = jnp.where(mask, jnp.exp(log_beta + later), 0.0)
        outs.append(jnp.einsum("bhqk,bhkd->bhqd", w, vb))
    return jnp.concatenate(outs, axis=2)

def hybrid_mixer(hn, w_in, conv_w, conv_b, dt_bias, a_log, d_skip, ssd_norm_g, sb_norm_g, w_out):
    b, s, _ = hn.shape
    proj = hn @ w_in.astype(hn.dtype)
    z, xbc, dt_raw, qkv = jnp.split(
        proj, [SSD_DIM, SSD_DIM + CONV_DIM, SSD_DIM + CONV_DIM + SSD_HEADS], axis=-1)
    xbc = jax.nn.silu(causal_dwconv(xbc, conv_w, conv_b))
    xs, bm, cm = jnp.split(xbc, [SSD_DIM, SSD_DIM + GN], axis=-1)
    dt = jax.nn.softplus(dt_raw.astype(jnp.float32) + dt_bias.astype(jnp.float32))
    a = -jnp.exp(a_log.astype(jnp.float32))
    xh = xs.astype(jnp.float32).reshape(b, s, SSD_HEADS, SSD_HEAD_DIM)
    y = ssd_chunked(xh, dt, a,
                    bm.astype(jnp.float32).reshape(b, s, SSD_GROUPS, SSD_STATE),
                    cm.astype(jnp.float32).reshape(b, s, SSD_GROUPS, SSD_STATE))
    y = y + d_skip.astype(jnp.float32)[:, None] * xh
    y = y.reshape(b, s, SSD_DIM) * jax.nn.silu(z.astype(jnp.float32))
    y_ssd = rmsnorm(y, ssd_norm_g)
    q, k, v = jnp.split(qkv, 3, axis=-1)
    to_heads = lambda t: t.reshape(b, s, SB_HEADS, SB_HEAD_DIM).transpose(0, 2, 1, 3)
    o = stick_breaking_attention(to_heads(q), to_heads(k), to_heads(v))
    y_sb = rmsnorm(o.transpose(0, 2, 1, 3).reshape(b, s, SB_DIM), sb_norm_g)
    y_all = jnp.concatenate([y_ssd, y_sb], axis=-1).astype(hn.dtype)
    return y_all @ w_out.astype(hn.dtype)

def memory_cross_attention(hn, mem, g_mem, w_q, w_k, w_v, w_o):
    b, s, _ = hn.shape
    m = rmsnorm(mem, g_mem)
    q = (hn @ w_q.astype(hn.dtype)).reshape(b, s, XA_HEADS, XA_HEAD_DIM).astype(jnp.float32)
    k = (m @ w_k.astype(m.dtype)).reshape(b, -1, XA_HEADS, XA_HEAD_DIM).astype(jnp.float32)
    v = (m @ w_v.astype(m.dtype)).reshape(b, -1, XA_HEADS, XA_HEAD_DIM).astype(jnp.float32)
    logits = jnp.einsum("bshd,bmhd->bhsm", q, k) * (1.0 / math.sqrt(XA_HEAD_DIM))
    p = jax.nn.softmax(logits, axis=-1)
    o = jnp.einsum("bhsm,bmhd->bshd", p, v).reshape(b, s, XA_DIM).astype(hn.dtype)
    return o @ w_o.astype(hn.dtype)

def sqrelu_mlp(hn, w1, w2):
    u = hn @ w1.astype(hn.dtype)
    u = jnp.square(jax.nn.relu(u))
    return u @ w2.astype(hn.dtype)

def first_inputs(seed: int = 0) -> dict:
    key = jax.random.key(seed)
    ks = jax.random.split(key, 24)
    f32 = jnp.float32
    nrm = lambda k, shape, fan_in: jax.random.normal(k, shape, f32) * (fan_in ** -0.5)
    gain = lambda k, shape: 1.0 + 0.02 * jax.random.normal(k, shape, f32)
    u = jax.random.uniform(ks[5], (DEPTH, SSD_HEADS), f32)
    dt0 = jnp.exp(u * (math.log(0.1) - math.log(0.001)) + math.log(0.001))
    dt_bias = dt0 + jnp.log(-jnp.expm1(-dt0))
    a_log = jnp.log(jax.random.uniform(ks[6], (DEPTH, SSD_HEADS), f32, minval=1.0, maxval=16.0))
    return {
        "x": jax.random.normal(ks[0], (BATCH, SEQ, D_MODEL), f32),
        "mem": jax.random.normal(ks[1], (BATCH, MEM_LEN, D_MODEL), f32),
        "norm_mix_g": gain(ks[2], (DEPTH, D_MODEL)),
        "w_in": nrm(ks[3], (DEPTH, D_MODEL, IN_DIM), D_MODEL),
        "conv_w": 0.5 * jax.random.normal(ks[4], (DEPTH, CONV_K, CONV_DIM), f32),
        "conv_b": 0.02 * jax.random.normal(ks[7], (DEPTH, CONV_DIM), f32),
        "dt_bias": dt_bias,
        "a_log": a_log,
        "d_skip": 1.0 + 0.1 * jax.random.normal(ks[8], (DEPTH, SSD_HEADS), f32),
        "ssd_norm_g": gain(ks[9], (DEPTH, SSD_DIM)),
        "sb_norm_g": gain(ks[10], (DEPTH, SB_DIM)),
        "w_out": nrm(ks[11], (DEPTH, D_MIX, D_MODEL), D_MIX),
        "norm_xa_g": gain(ks[12], (DEPTH, D_MODEL)),
        "norm_mem_g": gain(ks[13], (DEPTH, D_MODEL)),
        "w_xq": nrm(ks[14], (DEPTH, D_MODEL, XA_DIM), D_MODEL),
        "w_xk": nrm(ks[15], (DEPTH, D_MODEL, XA_DIM), D_MODEL),
        "w_xv": nrm(ks[16], (DEPTH, D_MODEL, XA_DIM), D_MODEL),
        "w_xo": nrm(ks[17], (DEPTH, XA_DIM, D_MODEL), XA_DIM),
        "norm_ff_g": gain(ks[18], (DEPTH, D_MODEL)),
        "w_ff1": nrm(ks[19], (DEPTH, D_MODEL, D_FF), D_MODEL),
        "w_ff2": nrm(ks[20], (DEPTH, D_FF, D_MODEL), D_FF),
        "final_g": gain(ks[21], (D_MODEL,)),
    }

def first_block(x, mem, norm_mix_g, w_in, conv_w, conv_b, dt_bias, a_log, d_skip, ssd_norm_g,
              sb_norm_g, w_out, norm_xa_g, norm_mem_g, w_xq, w_xk, w_xv, w_xo,
              norm_ff_g, w_ff1, w_ff2, final_g):
    h = x
    for l in range(DEPTH):
        h = h + hybrid_mixer(rmsnorm(h, norm_mix_g[l]), w_in[l], conv_w[l], conv_b[l], dt_bias[l],
                             a_log[l], d_skip[l], ssd_norm_g[l], sb_norm_g[l], w_out[l])
        h = h + memory_cross_attention(rmsnorm(h, norm_xa_g[l]), mem, norm_mem_g[l],
                                       w_xq[l], w_xk[l], w_xv[l], w_xo[l])
        h = h + sqrelu_mlp(rmsnorm(h, norm_ff_g[l]), w_ff1[l], w_ff2[l])
    return rmsnorm(h, final_g)


DEPTH_2 = 2

N_MIXERS = 2
N_CONV_LAYERS = (DEPTH_2 + N_MIXERS - 1) // N_MIXERS
N_NSA_LAYERS = DEPTH_2 // N_MIXERS
CONV_WIDTH = 31
N_HEADS = 16
HEAD_DIM = 64
N_KV = 4
GROUP = N_HEADS // N_KV
ROT_DIM = HEAD_DIM // 4
ROPE_THETA = 500000.0
CMP_LEN = 32
CMP_STRIDE = 16
CMP_HIDDEN = 256
SEL_LEN = 64
SEL_TOPK = 16
WINDOW = 512
D_FF_2 = 2816
FFN_CONV_WIDTH = 3
EPS_2 = 1e-6
PROJ_SIZES = (N_HEADS * HEAD_DIM,) + (N_KV * HEAD_DIM,) * 6 + (3 * N_HEADS,)
PROJ_COLS = sum(PROJ_SIZES)


def rmsnorm_2(x, g):
    xf = x.astype(jnp.float32)
    y = xf * lax.rsqrt(jnp.mean(xf * xf, axis=-1, keepdims=True) + EPS_2)
    return (y * g.astype(jnp.float32)).astype(x.dtype)

def layernorm(x, g, b):
    xf = x.astype(jnp.float32)
    mu = jnp.mean(xf, axis=-1, keepdims=True)
    var = jnp.mean(jnp.square(xf - mu), axis=-1, keepdims=True)
    y = (xf - mu) * lax.rsqrt(var + EPS_2)
    return (y * g.astype(jnp.float32) + b.astype(jnp.float32)).astype(x.dtype)

def causal_dwconv_2(x, w, b):
    width, ch = w.shape
    y = lax.conv_general_dilated(
        x, w[:, None, :].astype(x.dtype), window_strides=(1,),
        padding=[(width - 1, 0)], dimension_numbers=("NWC", "WIO", "NWC"),
        feature_group_count=ch)
    return y + b.astype(x.dtype)

def partial_rope(x):
    seq = x.shape[1]
    half = ROT_DIM // 2
    inv_freq = ROPE_THETA ** (-jnp.arange(half, dtype=jnp.float32) * (2.0 / ROT_DIM))
    ang = jnp.arange(seq, dtype=jnp.float32)[:, None] * inv_freq[None, :]
    cos = jnp.cos(ang)[:, None, :]
    sin = jnp.sin(ang)[:, None, :]
    xf = x.astype(jnp.float32)
    x1 = xf[..., :half]
    x2 = xf[..., half:ROT_DIM]
    out = jnp.concatenate([x1 * cos - x2 * sin, x2 * cos + x1 * sin, xf[..., ROT_DIM:]], axis=-1)
    return out.astype(x.dtype)

def masked_softmax(s, mask):
    s = jnp.where(mask, s.astype(jnp.float32), -1e30)
    m = jnp.max(s, axis=-1, keepdims=True)
    e = jnp.where(mask, jnp.exp(s - m), 0.0)
    return e / jnp.maximum(jnp.sum(e, axis=-1, keepdims=True), 1e-30)

def cmp_to_sel_matrix(n_cmp, n_sel):
    start_c = np.arange(n_cmp)[:, None] * CMP_STRIDE
    start_s = np.arange(n_sel)[None, :] * SEL_LEN
    ov = np.minimum(start_c + CMP_LEN, start_s + SEL_LEN) - np.maximum(start_c, start_s)
    return jnp.asarray(np.maximum(ov, 0).astype(np.float32) / CMP_LEN)

def conformer_conv(h, w_pw1, b_pw1, w_dw, b_dw, ln_g, ln_b, w_pw2, b_pw2):
    u = h @ w_pw1 + b_pw1
    a, gate = jnp.split(u, 2, axis=-1)
    u = a * jax.nn.sigmoid(gate)
    u = causal_dwconv_2(u, w_dw, b_dw)
    u = jax.nn.silu(layernorm(u, ln_g, ln_b))
    return u @ w_pw2 + b_pw2

def compress(blocks, pe, w1, w2):
    b, g, n, l, d = blocks.shape
    z = (blocks + pe).reshape(b, g, n, l * d)
    return jax.nn.silu(z @ w1) @ w2

def nsa_attention(h, w_in, q_g, kc_g, ks_g, kw_g, pe_k, pe_v, ck_w1, ck_w2, cv_w1, cv_w2, w_out):
    bsz, seq, _ = h.shape
    n_cmp = (seq - CMP_LEN) // CMP_STRIDE + 1
    n_sel = seq // SEL_LEN
    k_top = min(SEL_TOPK, n_sel)
    n_qb = seq // Q_BLOCK
    scale = HEAD_DIM ** -0.5

    splits = [int(c) for c in np.cumsum(PROJ_SIZES)[:-1]]
    q, kc, vc, ks, vs, kw, vw, gl = jnp.split(h @ w_in, splits, axis=-1)
    heads = lambda t, n: t.reshape(bsz, seq, n, HEAD_DIM)
    to_groups = lambda t: t.reshape(bsz, seq, N_KV, GROUP, HEAD_DIM).transpose(0, 2, 3, 1, 4)
    q = rmsnorm_2(heads(q, N_HEADS), q_g)
    q_nope = to_groups(q)
    q_rope = to_groups(partial_rope(q))
    gates = jax.nn.sigmoid(gl.astype(jnp.float32)).astype(h.dtype)
    gates = gates.reshape(bsz, seq, N_KV, GROUP, 3).transpose(0, 2, 3, 1, 4)

    blk_idx = np.arange(n_cmp)[:, None] * CMP_STRIDE + np.arange(CMP_LEN)[None, :]
    kc_blk = heads(kc, N_KV)[:, blk_idx].transpose(0, 3, 1, 2, 4)
    vc_blk = heads(vc, N_KV)[:, blk_idx].transpose(0, 3, 1, 2, 4)
    k_cmp = rmsnorm_2(compress(kc_blk, pe_k, ck_w1, ck_w2), kc_g)
    v_cmp = compress(vc_blk, pe_v, cv_w1, cv_w2)
    cmp_end = jnp.asarray(np.arange(n_cmp) * CMP_STRIDE + CMP_LEN - 1)
    cmp_map = cmp_to_sel_matrix(n_cmp, n_sel)

    k_sel = partial_rope(rmsnorm_2(heads(ks, N_KV), ks_g)).transpose(0, 2, 1, 3)
    k_sel = k_sel.reshape(bsz, N_KV, n_sel, SEL_LEN, HEAD_DIM)
    v_sel = heads(vs, N_KV).transpose(0, 2, 1, 3).reshape(bsz, N_KV, n_sel, SEL_LEN, HEAD_DIM)

    pad = ((0, 0), (0, 0), (WINDOW, 0), (0, 0))
    k_win = jnp.pad(partial_rope(rmsnorm_2(heads(kw, N_KV), kw_g)).transpose(0, 2, 1, 3), pad)
    v_win = jnp.pad(heads(vw, N_KV).transpose(0, 2, 1, 3), pad)

    b_ix = jnp.arange(bsz)[:, None, None, None]
    g_ix = jnp.arange(N_KV)[None, :, None, None]
    sel_off = jnp.arange(SEL_LEN)
    win_off = jnp.arange(Q_BLOCK + WINDOW)
    sel_ids = jnp.arange(n_sel)

    def query_block(qb):
        t0 = qb * Q_BLOCK
        pos = t0 + jnp.arange(Q_BLOCK)
        qn = lax.dynamic_slice_in_dim(q_nope, t0, Q_BLOCK, axis=3)
        qr = lax.dynamic_slice_in_dim(q_rope, t0, Q_BLOCK, axis=3)
        gt = lax.dynamic_slice_in_dim(gates, t0, Q_BLOCK, axis=3)

        s_c = jnp.einsum("bgrtd,bgnd->bgrtn", qn, k_cmp) * scale
        p_c = masked_softmax(s_c, cmp_end[None, :] <= pos[:, None])
        o_c = jnp.einsum("bgrtn,bgnd->bgrtd", p_c.astype(v_cmp.dtype), v_cmp)

        cur = pos // SEL_LEN
        imp = jnp.einsum("bgrtn,nj->bgtj", p_c, cmp_map)
        forced = (sel_ids[None, :] == 0) | (sel_ids[None, :] == cur[:, None]) | (sel_ids[None, :] == cur[:, None] - 1)
        imp = jnp.where(sel_ids[None, :] > cur[:, None], -1.0, jnp.where(forced, 1e4, imp))
        _, idx = lax.top_k(imp, k_top)
        k_g = k_sel[b_ix, g_ix, idx]
        v_g = v_sel[b_ix, g_ix, idx]
        s_s = jnp.einsum("bgrtd,bgtkld->bgrtkl", qr, k_g) * scale
        key_pos = idx[..., None] * SEL_LEN + sel_off
        mask_s = (key_pos <= pos[:, None, None]).reshape(bsz, N_KV, 1, Q_BLOCK, k_top * SEL_LEN)
        p_s = masked_softmax(s_s.reshape(bsz, N_KV, GROUP, Q_BLOCK, k_top * SEL_LEN), mask_s)
        o_s = jnp.einsum("bgrtm,bgtmd->bgrtd", p_s.astype(v_g.dtype),
                         v_g.reshape(bsz, N_KV, Q_BLOCK, k_top * SEL_LEN, HEAD_DIM))

        kwb = lax.dynamic_slice_in_dim(k_win, t0, Q_BLOCK + WINDOW, axis=2)
        vwb = lax.dynamic_slice_in_dim(v_win, t0, Q_BLOCK + WINDOW, axis=2)
        kp = t0 - WINDOW + win_off
        mask_w = (kp[None, :] >= 0) & (kp[None, :] <= pos[:, None]) & (kp[None, :] > pos[:, None] - WINDOW)
        s_w = jnp.einsum("bgrtd,bgsd->bgrts", qr, kwb) * scale
        p_w = masked_softmax(s_w, mask_w)
        o_w = jnp.einsum("bgrts,bgsd->bgrtd", p_w.astype(vwb.dtype), vwb)

        return gt[..., 0:1] * o_c + gt[..., 1:2] * o_s + gt[..., 2:3] * o_w

    o = lax.map(query_block, jnp.arange(n_qb))
    o = o.transpose(1, 0, 4, 2, 3, 5).reshape(bsz, seq, N_HEADS * HEAD_DIM)
    return o @ w_out

def conv_ffn(h, w_up, w_dw, b_dw, w_down):
    a, v = jnp.split(h @ w_up, 2, axis=-1)
    return (jax.nn.silu(causal_dwconv_2(a, w_dw, b_dw)) * v) @ w_down

def second_inputs(seed: int = 0) -> dict:
    key = jax.random.key(seed)
    ks = iter(jax.random.split(key, 40))
    f32 = jnp.float32
    D = D_MODEL
    hd = HEAD_DIM
    Lc = N_CONV_LAYERS
    Ln = N_NSA_LAYERS

    def w(shape, fan_in):
        return jax.random.normal(next(ks), shape, f32) * fan_in ** -0.5

    def gain(shape):
        return 1.0 + 0.05 * jax.random.normal(next(ks), shape, f32)

    def small(shape, s=0.02):
        return s * jax.random.normal(next(ks), shape, f32)

    return {
        "x": jax.random.normal(next(ks), (BATCH, SEQ, D), f32),
        "mix_norm_g": gain((DEPTH_2, D)),
        "ffn_norm_g": gain((DEPTH_2, D)),
        "conv_w_pw1": w((Lc, D, 2 * D), D),
        "conv_b_pw1": small((Lc, 2 * D)),
        "conv_w_dw": w((Lc, CONV_WIDTH, D), CONV_WIDTH),
        "conv_b_dw": small((Lc, D)),
        "conv_ln_g": gain((Lc, D)),
        "conv_ln_b": small((Lc, D)),
        "conv_w_pw2": w((Lc, D, D), D),
        "conv_b_pw2": small((Lc, D)),
        "nsa_w_in": w((Ln, D, PROJ_COLS), D),
        "nsa_q_norm": gain((Ln, hd)),
        "nsa_kc_norm": gain((Ln, hd)),
        "nsa_ks_norm": gain((Ln, hd)),
        "nsa_kw_norm": gain((Ln, hd)),
        "nsa_pe_k": small((Ln, CMP_LEN, hd), 0.1),
        "nsa_pe_v": small((Ln, CMP_LEN, hd), 0.1),
        "nsa_ck_w1": w((Ln, CMP_LEN * hd, CMP_HIDDEN), CMP_LEN * hd),
        "nsa_ck_w2": w((Ln, CMP_HIDDEN, hd), CMP_HIDDEN),
        "nsa_cv_w1": w((Ln, CMP_LEN * hd, CMP_HIDDEN), CMP_LEN * hd),
        "nsa_cv_w2": w((Ln, CMP_HIDDEN, hd), CMP_HIDDEN),
        "nsa_w_out": w((Ln, N_HEADS * hd, D), N_HEADS * hd),
        "ffn_w_up": w((DEPTH_2, D, 2 * D_FF_2), D),
        "ffn_w_dw": w((DEPTH_2, FFN_CONV_WIDTH, D_FF_2), FFN_CONV_WIDTH),
        "ffn_b_dw": small((DEPTH_2, D_FF_2)),
        "ffn_w_down": w((DEPTH_2, D_FF_2, D), D_FF_2),
    }

def second_block(x, mix_norm_g, ffn_norm_g,
              conv_w_pw1, conv_b_pw1, conv_w_dw, conv_b_dw, conv_ln_g, conv_ln_b, conv_w_pw2, conv_b_pw2,
              nsa_w_in, nsa_q_norm, nsa_kc_norm, nsa_ks_norm, nsa_kw_norm, nsa_pe_k, nsa_pe_v,
              nsa_ck_w1, nsa_ck_w2, nsa_cv_w1, nsa_cv_w2, nsa_w_out,
              ffn_w_up, ffn_w_dw, ffn_b_dw, ffn_w_down):
    for i in range(DEPTH_2):
        h = rmsnorm_2(x, mix_norm_g[i])
        j = i // N_MIXERS
        if i % N_MIXERS == 0:
            x = x + conformer_conv(h, conv_w_pw1[j], conv_b_pw1[j], conv_w_dw[j], conv_b_dw[j],
                                   conv_ln_g[j], conv_ln_b[j], conv_w_pw2[j], conv_b_pw2[j])
        else:
            x = x + nsa_attention(h, nsa_w_in[j], nsa_q_norm[j], nsa_kc_norm[j], nsa_ks_norm[j], nsa_kw_norm[j],
                                  nsa_pe_k[j], nsa_pe_v[j], nsa_ck_w1[j], nsa_ck_w2[j], nsa_cv_w1[j], nsa_cv_w2[j],
                                  nsa_w_out[j])
        x = x + conv_ffn(rmsnorm_2(x, ffn_norm_g[i]), ffn_w_up[i], ffn_w_dw[i], ffn_b_dw[i], ffn_w_down[i])
    return x


def setup_inputs(seed=0):
    out = dict(first_inputs(seed))
    for name, value in second_inputs(seed + 1).items():
        if name != "x":
            out[name + "_2"] = value
    return out


def reference(
    x, mem, norm_mix_g, w_in, conv_w, conv_b, dt_bias, a_log, d_skip, ssd_norm_g, sb_norm_g,
    w_out, norm_xa_g, norm_mem_g, w_xq, w_xk, w_xv, w_xo, norm_ff_g, w_ff1, w_ff2, final_g,
    mix_norm_g_2, ffn_norm_g_2, conv_w_pw1_2, conv_b_pw1_2, conv_w_dw_2, conv_b_dw_2,
    conv_ln_g_2, conv_ln_b_2, conv_w_pw2_2, conv_b_pw2_2, nsa_w_in_2, nsa_q_norm_2,
    nsa_kc_norm_2, nsa_ks_norm_2, nsa_kw_norm_2, nsa_pe_k_2, nsa_pe_v_2, nsa_ck_w1_2,
    nsa_ck_w2_2, nsa_cv_w1_2, nsa_cv_w2_2, nsa_w_out_2, ffn_w_up_2, ffn_w_dw_2, ffn_b_dw_2,
    ffn_w_down_2,
):
    x = first_block(
        x, mem, norm_mix_g, w_in, conv_w, conv_b, dt_bias, a_log, d_skip, ssd_norm_g, sb_norm_g,
        w_out, norm_xa_g, norm_mem_g, w_xq, w_xk, w_xv, w_xo, norm_ff_g, w_ff1, w_ff2, final_g,
    )
    return second_block(
        x, mix_norm_g_2, ffn_norm_g_2, conv_w_pw1_2, conv_b_pw1_2, conv_w_dw_2, conv_b_dw_2,
        conv_ln_g_2, conv_ln_b_2, conv_w_pw2_2, conv_b_pw2_2, nsa_w_in_2, nsa_q_norm_2,
        nsa_kc_norm_2, nsa_ks_norm_2, nsa_kw_norm_2, nsa_pe_k_2, nsa_pe_v_2, nsa_ck_w1_2,
        nsa_ck_w2_2, nsa_cv_w1_2, nsa_cv_w2_2, nsa_w_out_2, ffn_w_up_2, ffn_w_dw_2, ffn_b_dw_2,
        ffn_w_down_2,
    )


_drawn_inputs = setup_inputs


def setup_inputs(seed=0):
    import zlib

    import numpy as np

    out = dict(_drawn_inputs(seed))
    spreads = {}
    factors = {'conv_b': 3.416,
     'ssd_norm_g': 4.237,
     'sb_norm_g': 4.076,
     'norm_xa_g': 8.0,
     'norm_mem_g': 8.0,
     'norm_ff_g': 3.09,
     'conv_b_pw1_2': 3.88,
     'conv_ln_b_2': 4.075,
     'nsa_q_norm_2': 8.0,
     'nsa_kc_norm_2': 8.0,
     'nsa_ks_norm_2': 8.0,
     'nsa_kw_norm_2': 8.0,
     'nsa_pe_k_2': 8.0,
     'ffn_b_dw_2': 4.377}
    for name, (base, spread) in spreads.items():
        noise = np.random.default_rng([zlib.crc32(name.encode()), seed]).standard_normal(out[name].shape)
        drawn = base * np.exp(spread * noise) if base else spread * noise
        out[name] = __import__('jax').numpy.asarray(drawn.astype(out[name].dtype))
    for name, factor in factors.items():
        out[name] = (out[name] * factor).astype(out[name].dtype)
    return out
```

```python
from contextlib import ExitStack

import numpy as np

import concourse.bass as bass
from concourse import mybir

P = 128
T = 256
TT = T // P
D = 1024
KD = D // P
CH = 1024
RAW = 6
SPL = 3
AHEAD = 2
LO_DVE = 3 * P

SSD_TILES, SSD_HEADS, SB_HEADS = 4, 8, 8
XA_HEADS = 4
FF_TILES = 4096 // P
UP_TILES = 2816 // P
CONV_W = 31
N_CMP = (T - 32) // 16 + 1
EPS1, EPS2 = 1e-5, 1e-6
MASKED = -float(2 ** 100)

F32 = mybir.dt.float32
F32R = mybir.dt.float32r
ALU = mybir.AluOpType
ACT = mybir.ActivationFunctionType
AX = mybir.AxisListType.X

LAYERS = [("xbc", 6), ("q", 4), ("k", 4), ("z", 4), ("v", 4), ("mem_k", 4), ("mem_v", 4), ("w_out", 8),
          ("xq", 4), ("xo", 4), ("ff", 2 * FF_TILES), ("pw1", 16), ("pw2", 8), ("ffn0", 3 * UP_TILES),
          ("nsa_kc", 2), ("nsa_vc", 2), ("nsa_ks", 2), ("nsa_kw", 2), ("nsa_q", 8), ("nsa_v", 4),
          ("ck_w1", 4), ("cv_w1", 4), ("nsa_out", 8), ("ffn1", 3 * UP_TILES)]
START = {}
_n = 0
for _name, _count in LAYERS:
    START[_name] = _n
    _n += _count
N_CHUNKS = _n

VECTORS = [("mix_g", 8), ("conv_w", 24), ("conv_b", 6), ("d_skip", 4), ("ssd_g", 4), ("sb_g", 4), ("xa_g", 8),
           ("mem_g", 8), ("ff_g", 8), ("final_g", 8), ("mix2_g", 16), ("ffn2_g", 16), ("b_pw1", 16),
           ("w_dw", 8 * CONV_W), ("b_dw", 8), ("ln_g", 8), ("ln_b", 8), ("b_pw2", 8),
           ("q_g", 1), ("kc_g", 1), ("ks_g", 1), ("kw_g", 1), ("fconv", 2 * UP_TILES * 4),
           ("pe_k", 16), ("pe_v", 16), ("dt_bias", 8), ("a_log", 8)]
VCOL = {}
_n = 0
for _name, _count in VECTORS:
    VCOL[_name] = _n
    _n += _count
N_VEC = _n

CONSTS = [("ident", 128), ("ones", 128), ("neg_ones", 128), ("neg_upto", 128), ("tri", 128), ("strict", 128),
          ("block_ones", 128), ("rope", 128), ("neg_causal", 128), ("cmp_neg", 32), ("cmp_01", 32),
          ("v_mask", 128), ("cos", T), ("sin", T), ("eps", 2)]
CCOL = {}
_n = 0
for _name, _count in CONSTS:
    CCOL[_name] = _n
    _n += _count
N_CONST = _n

SMALLS = [("w_dt", 8 * 8), ("w_gate", 8 * 48), ("ck_w2", 2 * P), ("cv_w2", 2 * P)]
SCOL = {}
_n = 0
for _name, _count in SMALLS:
    SCOL[_name] = _n
    _n += _count
N_SMALL = _n

NORMS = ["mix", "mem", "ssd", "sb", "xa", "ff", "final", "mix2_0", "ln", "ffn2_0", "mix2_1", "ffn2_1"]
NORM = {n: i for i, n in enumerate(NORMS)}
NORM_DIM = {"ssd": 512, "sb": 512}
SQ_COUNT = {"ssd": 4, "sb": 4}
SQ_BASE = {}
_n = 0
for _name in NORMS:
    SQ_BASE[_name] = _n
    _n += SQ_COUNT.get(_name, 8)
PREPS = ["mix", "xa", "ff", "mix2_0", "ffn2_0", "mix2_1", "ffn2_1"]
PREP = {n: i for i, n in enumerate(PREPS)}
GAIN = {"mix": "mix_g", "xa": "xa_g", "ff": "ff_g", "mix2_0": "mix2_g", "mix2_1": "mix2_g",
        "ffn2_0": "ffn2_g", "ffn2_1": "ffn2_g"}
GY_BASE = {"mem": 0, "mixer": 8, "pw2": 16}
Y_BASE = {"mem": 0, "mixer": 8, "xa": 16, "pw2": 20, "nsa": 28}


def program(nc, x_d, mem_d, stream_d, vec_d, const_d, small_d, out_d):
    stack = ExitStack()
    with stack:
        def sb(name, shape, dt=F32, where=stack):
            return where.enter_context(nc.sbuf_tensor(name, shape, dt))

        sems = {}

        def sem(name):
            if name not in sems:
                sems[name] = stack.enter_context(nc.semaphore(name))
            return sems[name]

        X = sb("X", [P, KD, T])
        G = sb("G", [P, KD, T])
        GY = sb("GY", [P, KD, T])
        SQ = sb("SQ", [P, KD, T])
        XH, XL = sb("XH", [P, KD, T], F32R), sb("XL", [P, KD, T], F32R)
        YH, YL = sb("YH", [P, KD, T], F32R), sb("YL", [P, KD, T], F32R)
        WR = sb("WR", [P, RAW, CH])
        WH, WL = sb("WH", [P, SPL, CH], F32R), sb("WL", [P, SPL, CH], F32R)
        VEC = sb("VEC", [P, N_VEC])
        CON = sb("CON", [P, N_CONST])
        SML = sb("SML", [P, N_SMALL])
        SSUM = sb("SSUM", [P, T])
        LNV = sb("LNV", [P, T])
        RS = sb("RS", [P, T])
        RS2 = sb("RS2", [P, T])
        RST = sb("RST", [P, 2, TT])

        def group(specs):
            inner = ExitStack()
            got = {n: sb(n, s, dt, inner) for n, s, dt in specs}
            inner.close()
            return got

        A = group([("XP", [P, 6, T + 4], F32), ("CV", [P, 6, T], F32), ("XB", [P, 6, T], F32),
                   ("ZT", [P, 4, T], F32), ("QT", [P, 4, T], F32), ("KT", [P, 4, T], F32),
                   ("V", [P, TT, 512], F32), ("MEM", [P, KD, T], F32),
                   ("MK", [P, 4, T], F32), ("MV", [P, TT, 512], F32),
                   ("DTR", [P, TT, 8], F32), ("DT", [P, TT, 8], F32), ("DTE", [P, TT, 8], F32), ("AN", [P, TT, 8], F32),
                   ("EAL", [P, 8], F32), ("ABC", [P, TT, 8, P], F32), ("SEG", [P, 8, P], F32),
                   ("MM", [P, TT, 8, P], F32), ("CE", [P, 4, P], F32),
                   ("BT", [P, P], F32),
                   ("CBM", [P, 4, P], F32), ("ACL", [P, 3, 8], F32), ("DS", [P, 8], F32), ("DSX", [P, 12], F32), ("ST", [P, 256], F32)])
        XP, CV, XB, ZT, QT, KT, V, MEM = (A[n] for n in ("XP", "CV", "XB", "ZT", "QT", "KT", "V", "MEM"))
        MK, MV, DTR, DT, DTE, AN, EAL = (A[n] for n in ("MK", "MV", "DTR", "DT", "DTE", "AN", "EAL"))
        ABC, SEG, MM, CE, BT = (A[n] for n in ("ABC", "SEG", "MM", "CE", "BT"))
        EA = ABC[:, 0]
        XC = MEM[:, 4:8, :].rearrange("p k t -> p (k t)").rearrange("p (a n) -> p a n", a=2)
        XCD = CV[:, 4:6, :].rearrange("p k t -> p (k t)")
        CBM, ACL, DS, ST, DSX = (A[n] for n in ("CBM", "ACL", "DS", "ST", "DSX"))
        SBE = MEM[:, 0:4, :].rearrange("p k t -> p (k t)").rearrange("p (a n) -> p a n", a=2)
        SBP = MEM[:, 4:8, :].rearrange("p k t -> p (k t)").rearrange("p (a n) -> p a n", a=2)
        SBW = CV[:, 0:4, :].rearrange("p k t -> p (k t)").rearrange("p (a n) -> p a n", a=2)
        OS = QT

        B = group([("SG", [P, 2, T], F32), ("AT", [P, 2, T], F32), ("UP", [P, KD, T + CONV_W - 1], F32),
                   ("CX", [P, KD, T], F32), ("MU", [P, T], F32)])
        SG, AT, UPAD, CX, MU = (B[n] for n in ("SG", "AT", "UP", "CX", "MU"))
        C = group([("GU", [P, 2, T], F32), ("UH", [P, 2, T], F32R), ("UL", [P, 2, T], F32R),
                   ("TA", [P, 2, T], F32), ("AP_", [P, 2, T + 2], F32), ("CA", [P, 2, T], F32),
                   ("SA", [P, 2, T], F32), ("VA", [P, 2, T], F32)])
        GU, UH, UL, TA, APD, CA, SA, VA = (C[n] for n in ("GU", "UH", "UL", "TA", "AP_", "CA", "SA", "VA"))
        E = group([("HS", [P, 6, 2, T], F32),
                   ("QN", [P, 8, T], F32), ("QP", [P, 8, T], F32), ("KN", [P, 2, T], F32), ("KP", [P, 4, T], F32),
                   ("KCV", [P, 4, T], F32), ("CBUF", [P, 2, 4, T], F32),
                   ("NV", [P, TT, 512], F32), ("GT", [P, TT, 48], F32),
                   ("ZF", [P, 16, 60], F32), ("ZH", [P, 16, 60], F32R), ("ZL", [P, 16, 60], F32R),
                   ("H1", [P, 2, 2, 60], F32), ("HREP", [P, 2, 2, P], F32),
                   ("KC", [P, 3, 60], F32), ("VB", [P, 2, P], F32), ("GQ8", [P, 2], F32), ("KS", [P, 4, 64], F32),
                   ("SC", [P, 32, 16], F32), ("PC", [P, 32, 16], F32), ("CM", [P, 4, 32], F32),
                   ("PCT", [P, 2, T], F32), ("RM", [P, 2, 6, 4], F32), ("RM3", [P, 2, 2, 3], F32),
                   ("IDR", [P, P], F32R), ("NCR", [P, P], F32R)])

        acc = stack.enter_context(nc.psum_tensor("acc", [P, 2, 512], F32))
        big = stack.enter_context(nc.psum_tensor("big", [P, 4, 512], F32))
        mis = stack.enter_context(nc.psum_tensor("mis", [P, 2, 512], F32))

        raw_loaded = [sem(f"raw_loaded{i}") for i in range(RAW)]
        w_high, w_low_dve, w_low_pool, w_used = sem("w_high"), sem("w_low_dve"), sem("w_low_pool"), sem("w_used")
        acc_free = sem("acc_free")
        gx_ready, xh_ready, xl_ready = sem("gx_ready"), sem("xh_ready"), sem("xl_ready")
        gy_ready, yh_ready, yl_ready = sem("gy_ready"), sem("yh_ready"), sem("yl_ready")
        sq_ready, ssum_ready, nps_ready, rstd_ready = (sem("sq_ready"), sem("ssum_ready"), sem("nps_ready"),
                                                       sem("rstd_ready"))
        dve_chain, act_chain, pool_chain = sem("dve_chain"), sem("act_chain"), sem("pool_chain")

        def vec(name, i=0):
            return VEC[:, VCOL[name] + i:VCOL[name] + i + 1]

        def con(name, a=0, b=None):
            w = dict(CONSTS)[name]
            return CON[:, CCOL[name] + a:CCOL[name] + (w if b is None else b)]

        def small(name):
            return SML[:, SCOL[name]:SCOL[name] + dict(SMALLS)[name]]

        last_chunk = N_CHUNKS
        TILE = {}
        n = 0
        for name, count in [("xbc", 6), ("q", 4), ("k", 4), ("z", 4), ("v", 2), ("mem_k", 4), ("mem_v", 2), ("seg", 4),
                            ("w_out", 8), ("xq", 4), ("xo", 8), ("ff", FF_TILES), ("pw1", 16), ("pw2", 8),
                            ("ffn0", 2 * UP_TILES), ("nsa_kc", 2), ("nsa_vc", 2), ("nsa_ks", 2), ("nsa_kw", 2), ("nsa_q", 8),
                            ("nsa_v", 2), ("ck_w1", 2), ("cv_w1", 2), ("nsa_out", 8), ("ffn1", 2 * UP_TILES)]:
            TILE[name] = n
            n += count

        def ff_up(j):
            return START["ff"] + (0 if j == 0 else 2 * j - 1)

        def ff_down(j):
            return START["ff"] + (2 * j + 2 if j < FF_TILES - 1 else 2 * FF_TILES - 1)

        def last_k(name, i=0):
            return START[name] + i

        class Chain:

            def __init__(self, eng, sem_):
                self.eng, self.sem, self.base, self.k, self.turn, self.per = eng, sem_, 0, 0, None, 0

            def add(self, ins):
                self.k += 1
                ins.then_inc(self.sem, 1)
                return self.value()

            def value(self):
                v = self.base + self.k
                return v if self.turn is None else self.turn * self.per + v

            def link(self, ins):
                self.eng.wait_ge(self.sem, self.add(ins))

            def loop(self, turns, per):
                self.base += self.k
                self.k, self.per = 0, per
                with self.eng.Fori(0, turns) as t:
                    self.turn = t
                    yield t
                assert self.k == per, (self.k, per)
                self.base += turns * per
                self.k, self.turn = 0, None

        class Splitter:

            def __init__(self, one):
                self.one, self.issued = one, 0

            def to(self, n):
                while self.issued < min(n, last_chunk):
                    self.one(0, 0, self.issued)
                    self.issued += 1

            def in_loop(self, turn, per_turn, cs):
                self.one(turn, per_turn, cs)

            def ran(self, chunks):
                self.issued += chunks

        def plus(turn, per, n):
            return n if isinstance(turn, int) else turn * per + n

        XSTAT = DSX[:, :].rearrange("p (s a t) -> p s a t", s=3, a=2)

        def YS(p):
            return ZT[:, p]

        UP_TURNS = (UP_TILES - 4) // 2

        def turns_of_up(eng, chain=None, per=0):
            yield 0, 1
            if chain is None:
                with eng.Fori(0, UP_TURNS) as t:
                    yield t, 2
                    yield t, 3
            else:
                for t in chain.loop(UP_TURNS, per):
                    yield t, 2
                    yield t, 3
            yield 0, UP_TILES - 2
            yield 0, UP_TILES - 1

        def SEG_P(h):
            return XB[:, 2 * (h % 2):2 * (h % 2) + 2, :]

        def XO(h):
            return (big[:, 3, 0:T], mis[:, 1, 0:T])[h % 2]

        def XPT(h):
            return CV[:, 2 * (h % 2):2 * (h % 2) + 2, :]

        HS, QN, QP, KN, KP, KCV, CBUF, NV, GT = (E[n] for n in ("HS", "QN", "QP", "KN", "KP", "KCV", "CBUF", "NV", "GT"))
        ZF, ZH, ZL, H1, HREP, KC, VB, GQ8, KS = (E[n] for n in ("ZF", "ZH", "ZL", "H1", "HREP", "KC", "VB", "GQ8", "KS"))
        SC, PC, CM, PCT, RM, RM3, IDR, NCR = (E[n] for n in ("SC", "PC", "CM", "PCT", "RM", "RM3", "IDR", "NCR"))
        QR, RH, SH, LH, T1, T2 = (HS[:, i] for i in range(6))
        PP = CBUF.rearrange("p a g t -> p (a g t)")[:, 0:1536].rearrange("p (s b n) -> p s b n", s=2, b=2)
        PT = HS.rearrange("p a b t -> p (a b t)")[:, 0:1536].rearrange("p (s b n) -> p s b n", s=2, b=2)
        NORMED = 12
        N_HEADS2 = 16

        def pe_nsa(pe, tile, token_major, three, sum_squares, chunk_ready, acc_ready):
            def head_sums(n):
                pe.wait_ge(sem("hsq_done"), n + 1)
                if n >= 1:
                    pe.wait_ge(sem("hrs_done"), n)
                w = T if n < NORMED else 60
                pe.matmul(mis[:, 0, 0:w], con("block_ones"), SH[:, n % 2, 0:w], start=True, stop=True,
                          skip_group_check=True).then_inc(sem("hn_ps"), 1)

            def rotate(n):
                pe.wait_ge(sem("hqn_done"), n + 1)
                if n >= 1:
                    pe.wait_ge(sem("hrot_read"), n)
                x = KN[:, n % 2] if n < 4 else QN[:, n - 4]
                pe.matmul(mis[:, 1, 0:T], con("rope"), x, start=True, stop=True,
                          skip_group_check=True).then_inc(sem("rope_ps"), 1)

            for i in range(4):
                tile(START["nsa_kc"] + i, TILE["nsa_kc"] + i, XH, XL, base=(xl_ready, 8 * PREP["mix2_1"]) if i == 0 else None)
                if i == 0:
                    sum_squares("mix2_1")
                    for tt in range(TT):
                        ins = pe.matmul(big[:, 2, tt:tt + 1], SSUM[:, tt * P:tt * P + P], con("ones", 0, 1),
                                        start=True, stop=True, skip_group_check=True)
                    ins.then_inc(sem("rst_ps"), 1)
            for n in range(NORMED + 2):
                if n < NORMED:
                    tile(START["nsa_ks"] + n, TILE["nsa_ks"] + n, XH, XL)
                if 1 <= n <= NORMED:
                    head_sums(n - 1)
                if n >= 2:
                    rotate(n - 2)
            token_major(START["nsa_v"], TILE["nsa_v"], XH, XL)
            for tt in range(TT):
                for k in range(KD):
                    ins = pe.matmul(big[:, 3, 64 * tt:64 * tt + 48], G[:, k, tt * P:tt * P + P],
                                    small("w_gate")[:, k * 48:k * 48 + 48], start=k == 0, stop=k == KD - 1,
                                    skip_group_check=True)
            ins.then_inc(sem("gate_ps"), 1)
            for kv in range(2):
                pe.wait_ge(sem("zl_done"), kv + 1)
                for ht in range(2):
                    t = TILE["ck_w1"] + 2 * kv + ht
                    acc_ready(t)
                    for a in range(2):
                        c = START["ck_w1"] + 4 * kv + 2 * ht + a
                        chunk_ready(c)
                        for b in range(8):
                            ins = three(acc[:, t % 2, 0:60], c % SPL, b * P, ZH[:, 8 * a + b, :], ZL[:, 8 * a + b, :],
                                        a == 0 and b == 0, a == 1 and b == 7)
                        ins.then_inc(w_used, 1)
            pe.wait_ge(sem("h1_done"), 2)
            for ht in range(2):
                ins = pe.matmul(big[:, 0, 0:60], small("ck_w2")[:, P * ht:P * ht + P], H1[:, 0, ht, :], start=ht == 0,
                                stop=ht == 1, skip_group_check=True)
            ins.then_inc(sem("kc_ps"), 1)
            head_sums(NORMED)
            pe.wait_ge(sem("hrep_done"), 1)
            for s_ in range(2):
                for ht in range(2):
                    ins = pe.matmul(big[:, 1, P * s_:P * s_ + P], HREP[:, s_, ht, :], small("cv_w2")[:, P * ht:P * ht + P],
                                    start=ht == 0, stop=ht == 1, skip_group_check=True)
            ins.then_inc(sem("vb_ps"), 1)
            pe.wait_ge(sem("kc_done"), 1)
            pe.wait_ge(sem("vb_done"), 1)
            for e in range(2):
                half = slice(64 * e, 64 * e + 64)
                for tt in range(TT):
                    for j in range(8):
                        g = 2 * (j // 4) + e
                        at = (tt * 8 + j) * 16
                        ins = pe.matmul(big[:, e, at:at + N_CMP], QN[half, j, tt * P:tt * P + P],
                                        KC[half, 2, 15 * g:15 * g + 15], start=True, stop=True, skip_group_check=True)
            ins.then_inc(sem("sc_ps"), 1)
            pe.wait_ge(sem("pc_done"), 1)
            for s_ in range(2):
                for tt in range(TT):
                    ins = pe.transpose(big[:, 2, s_ * T + tt * P:s_ * T + tt * P + P],
                                       PC.rearrange("p (t j) n -> p t (j n)", t=2)[:, tt, s_ * P:s_ * P + P], con("ident"))
            ins.then_inc(sem("pct_ps"), 1)
            pe.wait_ge(sem("pct_done"), 1)
            pe.wait_ge(sem("consts_rounded"), 1)
            pe.wait_ge(sem("hp_done"), NORMED)

            def scores(hh):
                j, e = hh // 2, hh % 2
                half = slice(64 * e, 64 * e + 64)
                if hh >= 2:
                    pe.wait_ge(sem("at_exp"), hh - 1)
                for br in range(2):
                    o, k = big[:, 2 * e + br, :], KP[half, 2 * br + j // 4, :]
                    pe.matmul(o[:, 0:P], QP[half, j, 0:P], k[:, 0:P], start=True, stop=True, skip_group_check=True)
                    pe.matmul(o[:, P:P + T], QP[half, j, P:T], k, start=False, stop=True, skip_group_check=True)
                    for at in (0, T):
                        ins = pe.matmul(o[:, at:at + P], IDR[:, :], NCR[:, :], start=False, stop=True,
                                        skip_group_check=True)
                ins.then_inc(sem("at_s"), 1)

            def turn(hh):
                pe.wait_ge(sem("at_pn"), hh + 1)
                if hh >= 1:
                    pe.wait_ge(sem("at_pt_act"), hh)
                    pe.wait_ge(sem("at_pt_dve"), hh)
                for br in range(2):
                    for b in range(3):
                        ins = pe.transpose(mis[:, br, b * P:b * P + P], PP[:, hh % 2, br, b * P:b * P + P], con("ident"))
                ins.then_inc(sem("at_t"), 1)

            def outputs(hh):
                j, e = hh // 2, hh % 2
                s_, i = j // 4, j % 4
                o = acc[:, j % 2, 0:T]
                if e == 0:
                    if j >= 2:
                        pe.wait_ge(yl_ready, Y_BASE["nsa"] + j - 1)
                    q = slice(32 * i, 32 * i + 32)
                    pe.matmul(o, VB[q, s_, :], PCT[q, s_, :], start=True, stop=False, skip_group_check=True)
                pe.wait_ge(sem("at_pt_act"), hh + 1)
                pe.wait_ge(sem("at_pt_dve"), hh + 1)
                half = slice(64 * e, 64 * e + 64)
                g = 2 * s_ + e
                for br in range(2):
                    v = lambda m: NV[:, m, 256 * br + 64 * g:256 * br + 64 * g + 64]
                    pe.matmul(o[half, :], v(0), PT[:, hh % 2, br, 0:T], start=False, stop=False, skip_group_check=True)
                    ins = pe.matmul(o[half, P:T], v(1), PT[:, hh % 2, br, T:T + P], start=False, stop=br == 1,
                                    skip_group_check=True)
                ins.then_inc(sem("at_o"), 1)

            pe.wait_ge(acc_free, TILE["nsa_out"])
            for i in range(N_HEADS2 + 2):
                if i < N_HEADS2:
                    scores(i)
                if 1 <= i <= N_HEADS2:
                    turn(i - 1)
                if i >= 2:
                    outputs(i - 2)

        def act_nsa(act, ch, sp, rstd):
            link = ch.link

            def square(n, ready):
                act.wait_ge(acc_free, ready)
                act.activation(SH[:, n % 2], QR[:, n % 2], ACT.Square).then_inc(sem("hsq_done"), 1)

            def head_rstd(n):
                act.wait_ge(sem("hn_ps"), n + 1)
                w = T if n < NORMED else 60
                link(act.activation(LH[:, n % 2, 0:w], mis[:, 0, 0:w], ACT.Ln, bias=con("eps", 1, 2), scale=1.0 / 64))
                if n >= 2:
                    act.wait_ge(sem("hqn_done"), n - 1)
                act.activation(RH[:, n % 2, 0:w], LH[:, n % 2, 0:w], ACT.Exp, scale=-0.5).then_inc(sem("hrs_done"), 1)

            act.preload_act_table_set("natural_log_exp_and_others")
            sp.to(START["nsa_kc"] + 1 + AHEAD)
            rstd("mix2_1", RS)
            act.wait_ge(sem("rst_ps"), 2)
            link(act.activation(RST[:, 1, :], big[:, 2, 0:2], ACT.Ln, bias=con("eps", 1, 2), scale=1.0 / D))
            act.activation(RST[:, 0, :], RST[:, 1, :], ACT.Exp, scale=-0.5).then_inc(sem("rst_done"), 1)
            for kv in range(2):
                for i in range(2):
                    sp.to(START["nsa_kc"] + 2 * kv + i + 1 + AHEAD)
                act.wait_ge(acc_free, TILE["nsa_kc"] + 2 * kv + 2)
                for gp in range(2):
                    src = KCV[64 * gp:64 * gp + 64, 2 * kv:2 * kv + 2, :]
                    dst = CBUF[:, kv].rearrange("p (b a) t -> p b a t", a=2)[:, :, gp, :]
                    act.dma_start(dst[0:64], src).then_inc(sem(f"cbuf_loaded{kv}"), 16)
                    act.dma_start(dst[64:128, :, 0:T - 1], src[:, :, 1:T]).then_inc(sem(f"cbuf_loaded{kv}"), 16)
            for n in range(NORMED + 1):
                if n < NORMED:
                    sp.to(START["nsa_ks"] + n + 1 + AHEAD)
                    square(n, TILE["nsa_ks"] + n + 1)
                if n >= 1:
                    head_rstd(n - 1)
            sp.to(START["nsa_v"] + AHEAD)
            act.wait_ge(sem("zf_done"), 1)
            act.activation(ZH[:, :, :], ZF[:, :, :], ACT.Copy).then_inc(sem("zh_done"), 1)
            sp.to(START["ck_w1"] + AHEAD)
            act.wait_ge(sem("gate_done2"), 1)
            act.activation(GT[:, :, :], GT[:, :, :], ACT.Sigmoid).then_inc(sem("gates"), 1)
            for kv in range(2):
                if kv == 1:
                    act.wait_ge(sem("zf_done"), 2)
                    act.activation(ZH[:, :, :], ZF[:, :, :], ACT.Copy).then_inc(sem("zh_done"), 1)
                for ht in range(2):
                    c, t = START["ck_w1"] + 4 * kv + 2 * ht, TILE["ck_w1"] + 2 * kv + ht
                    sp.to(c + 1 + AHEAD)
                    sp.to(c + 2 + AHEAD)
                    act.wait_ge(w_used, c + 2)
                    act.wait_ge(acc_free, t)
                    link(act.activation(H1[:, kv, ht, :], acc[:, t % 2, 0:60], ACT.Silu))
                    act.sem_inc(acc_free, 1)
                act.sem_inc(sem("h1_done"), 1)
            act.preload_act_table_set("natural_log_exp_and_others")
            act.wait_ge(sem("kc_copied"), 1)
            act.activation(SH[:, NORMED % 2, 0:60], KC[:, 0, :], ACT.Square).then_inc(sem("hsq_done"), 1)
            head_rstd(NORMED)
            act.wait_ge(sem("sc_in"), 1)
            act.activation(SC[:, :, 0:N_CMP], SC[:, :, 0:N_CMP], ACT.Exp).then_inc(sem("sc_exp"), 1)
            act.wait_ge(sem("pct_ps"), 1)
            act.activation(PCT.rearrange("p s t -> p (s t)"), big[:, 2, :], ACT.Copy).then_inc(sem("pct_done"), 1)
            for i in range(N_HEADS2 + 2):
                if i < N_HEADS2:
                    act.wait_ge(sem("at_nm"), i + 1)
                    if i >= 2:
                        act.wait_ge(sem("at_t"), i - 1)
                    for br in range(2):
                        for tt, (a, b) in enumerate(((0, P), (P, P + T))):
                            ins = act.activation(PP[:, i % 2, br, a:b], big[:, 2 * (i % 2) + br, a:b], ACT.Exp,
                                                 bias=RM3[:, i % 2, br, tt:tt + 1],
                                                 accum_out=RM[:, i % 2, 0, 2 * br + tt:2 * br + tt + 1])
                            if (br, tt) != (1, 1):
                                ch.add(ins)
                    ins.then_inc(sem("at_exp"), 1)
                if 1 <= i <= N_HEADS2:
                    act.wait_ge(sem("at_t"), i)
                    if i >= 3:
                        act.wait_ge(sem("at_o"), i - 2)
                    act.activation(PT[:, (i - 1) % 2, 0, :], mis[:, 0, 0:384], ACT.Copy).then_inc(sem("at_pt_act"), 1)
                if i >= 3 and i % 2 == 1:
                    j = (i - 3) // 2
                    act.wait_ge(sem("at_o"), 2 * j + 2)
                    act.activation(YH[:, j], acc[:, j % 2, 0:T], ACT.Copy).then_inc(yh_ready, 1)

        def dve_nsa(dve, ch, sp, used, scaled, rstd_done):
            link = ch.link
            link(dve.tensor_scalar(GQ8[:, 0:1], vec("q_g"), 0.125, None, ALU.mult))
            link(dve.tensor_copy(IDR[:, :], con("ident")))
            dve.tensor_copy(NCR[:, :], con("neg_causal")).then_inc(sem("consts_rounded"), 1)
            rstd_done("mix2_1")
            for i in range(4):
                sp.to(START["nsa_kc"] + i + 1 + AHEAD)
                used(START["nsa_kc"] + i)
                scaled(KCV[:, i], TILE["nsa_kc"] + i, wait=False)

            def normed(n):
                dve.wait_ge(sem("hrs_done"), n + 1)
                x = KN[:, n % 2] if n < 4 else QN[:, n - 4]
                g = vec("ks_g") if n < 2 else vec("kw_g") if n < 4 else GQ8[:, 0:1]
                dve.scalar_tensor_tensor(x, QR[:, n % 2], g, RH[:, n % 2], ALU.mult, ALU.mult).then_inc(sem("hqn_done"), 1)

            def rotated(n):
                x = KN[:, n % 2] if n < 4 else QN[:, n - 4]
                if n >= 2:
                    dve.wait_ge(sem("hp_done"), n - 1)
                dve.wait_ge(sem("hqn_done"), n + 1)
                link(dve.tensor_tensor(T1[:, n % 2], x, con("cos"), ALU.mult))
                dve.wait_ge(sem("rope_ps"), n + 1)
                dve.tensor_tensor(T2[:, n % 2], mis[:, 1, 0:T], con("sin"), ALU.mult).then_inc(sem("hrot_read"), 1)

            for n in range(NORMED + 2):
                if n < NORMED:
                    sp.to(START["nsa_ks"] + n + 1 + AHEAD)
                    used(START["nsa_ks"] + n)
                    if n >= 2:
                        dve.wait_ge(sem("hqn_done"), n - 1)
                        dve.wait_ge(sem("hsq_done"), n - 1)
                    scaled(QR[:, n % 2], TILE["nsa_ks"] + n, wait=False)
                if 1 <= n <= NORMED:
                    normed(n - 1)
                if n >= 2:
                    rotated(n - 2)

            def positions(kv):
                dve.wait_ge(sem(f"cbuf_loaded{kv}"), 64)
                pe_ = "pe_k" if kv == 0 else "pe_v"
                for a in range(2):
                    x = CBUF[:, kv, :, 16 * a:16 * a + 240].rearrange("p g (n b two) -> p b g n two", b=8, two=2)[:, :, :, :, 0]
                    v = VEC[:, VCOL[pe_] + 8 * a:VCOL[pe_] + 8 * a + 8].unsqueeze(2).unsqueeze(2).broadcast_to([P, 8, 4, N_CMP])
                    link(dve.tensor_tensor(ZF[:, 8 * a:8 * a + 8, :].rearrange("p b (g n) -> p b g n", g=4), x, v, ALU.add))
                dve.sem_inc(sem("zf_done"), 1)

            def z_low(kv):
                dve.wait_ge(sem("zh_done"), kv + 1)
                dve.tensor_tensor(ZL[:, :, :], ZF[:, :, :], ZH[:, :, :].bitcast(F32), ALU.subtract).then_inc(
                    sem("zl_done"), 1)

            positions(0)
            sp.to(START["nsa_v"] + 1 + AHEAD)
            z_low(0)
            for i in range(4):
                sp.to(START["nsa_v"] + i + 1 + AHEAD)
            used(START["nsa_v"] + 3)
            dve.wait_ge(sem("rst_done"), 2)
            for tt in range(TT):
                dve.tensor_scalar(NV[:, tt], acc[:, (TILE["nsa_v"] + tt) % 2, :], RST[:, 0, tt:tt + 1], None,
                                  ALU.mult).then_inc(acc_free, 1)
            dve.wait_ge(sem("gate_ps"), 1)
            for tt in range(TT):
                link(dve.tensor_scalar(GT[:, tt], big[:, 3, 64 * tt:64 * tt + 48], RST[:, 0, tt:tt + 1], None, ALU.mult))
            dve.sem_inc(sem("gate_done2"), 1)
            link(dve.memset(HREP[:, :, :, :], 0.0))
            link(dve.memset(PC[:, :, :], 0.0))
            for i in range(2):
                sp.to(START["ck_w1"] + i + 1 + AHEAD)
            for i in range(2, 4):
                sp.to(START["ck_w1"] + i + 1 + AHEAD)
            used(START["ck_w1"] + 3)
            positions(1)
            z_low(1)
            for i in range(4):
                sp.to(START["cv_w1"] + i + 1 + AHEAD)
            dve.wait_ge(sem("kc_ps"), 1)
            link(dve.tensor_copy(KC[:, 0, :], big[:, 0, 0:60]))
            dve.sem_inc(sem("kc_copied"), 1)
            for s_ in range(2):
                for ht in range(2):
                    o = HREP[:, s_, ht, :].rearrange("p (i e n) -> p i e n", i=4, e=2)[:, :, :, 0:N_CMP]
                    x = H1[:, 1, ht, 30 * s_:30 * s_ + 30].rearrange("p (e n) -> p e n", e=2).unsqueeze(1).broadcast_to(
                        [P, 4, 2, N_CMP])
                    link(dve.tensor_copy(o, x))
            dve.sem_inc(sem("hrep_done"), 1)
            dve.wait_ge(sem("vb_ps"), 1)
            dve.tensor_tensor(VB[:, :, :], big[:, 1, 0:T].rearrange("p (s d) -> p s d", s=2),
                              con("v_mask").unsqueeze(1).broadcast_to([P, 2, P]), ALU.mult).then_inc(sem("vb_done"), 1)
            dve.wait_ge(sem("hrs_done"), NORMED + 1)
            dve.scalar_tensor_tensor(KC[:, 2, :], KC[:, 0, :], vec("kc_g"), RH[:, NORMED % 2, 0:60], ALU.mult,
                                     ALU.mult).then_inc(sem("kc_done"), 1)
            dve.wait_ge(sem("sc_ps"), 1)
            tj = lambda x: x.rearrange("p (t j) n -> p t j n", t=2)
            for e in range(2):
                s_ = SC[:, 16 * e:16 * e + 16, 0:N_CMP]
                link(dve.tensor_tensor(tj(s_), big[:, e, 0:T].rearrange("p (t j n) -> p t j n", t=2, j=8)[:, :, :, 0:N_CMP],
                                       con("cmp_neg").rearrange("p (t n) -> p t n", t=2)[:, :, 0:N_CMP].unsqueeze(2)
                                       .broadcast_to([P, 2, 8, N_CMP]), ALU.add))
            s_all = SC[:, :, 0:N_CMP]
            link(dve.tensor_reduce(CM[:, 0, :], s_all, AX, ALU.max))
            link(dve.tensor_tensor(s_all, s_all, CM[:, 0, :].unsqueeze(2).broadcast_to([P, 32, N_CMP]), ALU.subtract))
            dve.sem_inc(sem("sc_in"), 1)
            dve.wait_ge(sem("sc_exp"), 1)
            for e in range(2):
                s_ = tj(SC[:, 16 * e:16 * e + 16, 0:N_CMP])
                link(dve.tensor_tensor(s_, s_, con("cmp_01").rearrange("p (t n) -> p t n", t=2)[:, :, 0:N_CMP].unsqueeze(2)
                                       .broadcast_to([P, 2, 8, N_CMP]), ALU.mult))
            link(dve.tensor_reduce(CM[:, 1, :], s_all, AX, ALU.add))
            link(dve.tensor_scalar(CM[:, 1, :], CM[:, 1, :], 1e-30, None, ALU.max))
            link(dve.reciprocal(CM[:, 2, :], CM[:, 1, :]))
            dve.wait_ge(sem("gates"), 1)
            for e in range(2):
                gate = GT.rearrange("p t (j x) -> p t j x", x=6)[:, :, :, 3 * e]
                link(dve.tensor_tensor(CM[:, 3, 16 * e:16 * e + 16].rearrange("p (t j) -> p t j", t=2),
                                       CM[:, 2, 16 * e:16 * e + 16].rearrange("p (t j) -> p t j", t=2), gate, ALU.mult))
                o = PC.rearrange("p (m e) n -> p m e n", e=2)[:, :, e, 0:N_CMP]
                link(dve.tensor_tensor(o, SC[:, 16 * e:16 * e + 16, 0:N_CMP],
                                       CM[:, 3, 16 * e:16 * e + 16].unsqueeze(2).broadcast_to([P, 16, N_CMP]), ALU.mult))
            dve.sem_inc(sem("pc_done"), 1)

            def scale_rows(hh):
                r = RM[:, hh % 2]
                link(dve.reciprocal(r[:, 1, :], r[:, 0, :]))
                gate = GT[:, :, 3 * hh + 1:3 * hh + 3].rearrange("p t b -> p b t")
                link(dve.tensor_tensor(r[:, 2, :].rearrange("p (b t) -> p b t", b=2),
                                       r[:, 1, :].rearrange("p (b t) -> p b t", b=2), gate, ALU.mult))
                for br in range(2):
                    for tt, (a, b) in enumerate(((0, P), (P, P + T))):
                        p_ = PP[:, hh % 2, br, a:b]
                        ch.add(dve.tensor_scalar(p_, p_, r[:, 2, 2 * br + tt:2 * br + tt + 1], None, ALU.mult))
                dve.wait_ge(dve_chain, ch.value())
                dve.sem_inc(sem("at_pn"), 1)

            for i in range(N_HEADS2 + 2):
                if i < N_HEADS2:
                    dve.wait_ge(sem("at_s"), i + 1)
                    m = RM3[:, i % 2]
                    if i >= 2:
                        dve.wait_ge(sem("at_exp"), i - 1)
                    link(dve.tensor_reduce(m.rearrange("p b c -> p (b c)"),
                                           big[:, 2 * (i % 2):2 * (i % 2) + 2, 0:384].rearrange("p b (c n) -> p b c n", c=3),
                                           AX, ALU.max, negate=True))
                    dve.tensor_tensor(m[:, :, 1:2], m[:, :, 1:2], m[:, :, 2:3], ALU.min).then_inc(sem("at_nm"), 1)
                if 1 <= i <= N_HEADS2:
                    dve.wait_ge(sem("at_exp"), i)
                    scale_rows(i - 1)
                    dve.wait_ge(sem("at_t"), i)
                    if i >= 3:
                        dve.wait_ge(sem("at_o"), i - 2)
                    dve.tensor_copy(PT[:, (i - 1) % 2, 1, :], mis[:, 1, 0:384]).then_inc(sem("at_pt_dve"), 1)
                if i >= 3 and i % 2 == 1:
                    j = (i - 3) // 2
                    dve.wait_ge(yh_ready, Y_BASE["nsa"] + j + 1)
                    dve.tensor_tensor(YL[:, j], acc[:, j % 2, 0:T], YH[:, j].bitcast(F32), ALU.subtract).then_inc(yl_ready, 1)

        def pool_nsa(pool, sp):
            for n in range(NORMED):
                sp.to(START["nsa_ks"] + n + 1 + AHEAD)
                pool.wait_ge(sem("hrot_read"), n + 1)
                o = KP[:, n] if n < 4 else QP[:, n - 4]
                pool.tensor_tensor(o, T1[:, n % 2], T2[:, n % 2], ALU.add).then_inc(sem("hp_done"), 1)
            sp.to(START["nsa_out"] + AHEAD)

        block = stack.enter_context(nc.Block())

        @block.sync
        def _(sp):
            sp.dma_start(X[:], x_d).then_inc(sem("x_loaded"), 16)
            sp.dma_start(VEC[:], vec_d).then_inc(sem("vec_loaded"), 16)
            for c in range(RAW):
                sp.dma_start(WR[:, c], stream_d[c]).then_inc(raw_loaded[c], 16)
                if c == 1:
                    sp.dma_start(CON[:], const_d).then_inc(sem("const_loaded"), 16)
                if c == 2:
                    sp.dma_start(SML[:], small_d).then_inc(sem("small_loaded"), 16)
                    sp.dma_start(MEM[:], mem_d).then_inc(sem("mem_loaded"), 16)
            turns = (last_chunk - RAW) // RAW

            def load(c, slot, at):
                sp.wait_ge(w_low_dve, c - RAW + 1)
                sp.wait_ge(w_low_pool, c - RAW + 1)
                sp.dma_start(WR[:, slot], at).then_inc(raw_loaded[slot], 16)

            with sp.Fori(0, turns) as t:
                for s in range(RAW):
                    c = t * RAW + RAW + s
                    load(c, s, stream_d[bass.ds(c, 1)].rearrange("a p n -> p (a n)"))
            for c in range(RAW + turns * RAW, last_chunk):
                load(c, c % RAW, stream_d[c])
            sp.wait_ge(sem("result"), 1)
            sp.dma_start(out_d, X[:]).then_inc(sem("stored"), 16)
            sp.wait_ge(sem("stored"), 16)

        @block.tensor
        def _(pe):
            def chunk_ready(c):
                pe.wait_ge(w_low_dve, c + 1)
                pe.wait_ge(w_low_pool, c + 1)

            def acc_ready(t):
                pe.wait_ge(acc_free, t - 1)

            def three(out, slot, cols, hi, lo, start, stop, n=P):
                wh, wl = WH[:, slot, cols:cols + n], WL[:, slot, cols:cols + n]
                pe.matmul(out, wh, hi, start=start, stop=False, skip_group_check=True)
                pe.matmul(out, wh, lo, start=False, stop=False, skip_group_check=True)
                return pe.matmul(out, wl, hi, start=False, stop=stop, skip_group_check=True)

            def tile(c, t, hi, lo, base=None, slot=None, bank=None, first=False):
                slot = c % SPL if slot is None else slot
                bank = t % 2 if bank is None else bank
                chunk_ready(c)
                if not first:
                    acc_ready(t)
                for k in range(KD):
                    if base is not None:
                        pe.wait_ge(base[0], base[1] + k + 1)
                    ins = three(acc[:, bank, 0:T], slot, k * P, hi[:, k], lo[:, k], k == 0, k == KD - 1)
                ins.then_inc(w_used, 1)

            def token_major(c0, t0, hi, lo):
                acc_ready(t0)
                acc_ready(t0 + 1)
                for i in range(4):
                    c = c0 + i
                    chunk_ready(c)
                    for k in range(2):
                        kk = 2 * i + k
                        wh, wl = (w[:, c % SPL, k * 512:k * 512 + 512] for w in (WH, WL))
                        for tt in range(TT):
                            o = acc[:, (t0 + tt) % 2, :]
                            xh, xl = (x[:, kk, tt * P:tt * P + P] for x in (hi, lo))
                            pe.matmul(o, xh, wh, start=kk == 0, stop=False, skip_group_check=True)
                            pe.matmul(o, xh, wl, start=False, stop=False, skip_group_check=True)
                            ins = pe.matmul(o, xl, wh, start=False, stop=kk == KD - 1, skip_group_check=True)
                    ins.then_inc(w_used, 1)

            def sum_squares(name):
                pe.wait_ge(ssum_ready, NORM[name] + 1)
                pe.matmul(mis[:, 0, 0:T], con("ones"), SSUM[:, :], start=True, stop=True,
                          skip_group_check=True).then_inc(nps_ready, 1)

            def transpose_columns():
                for tt in range(TT):
                    pe.matmul(mis[:, 1, 16 + tt:17 + tt], SSUM[:, tt * P:tt * P + P], con("ones", 0, 1),
                              start=True, stop=True, skip_group_check=True)

            xl0 = (xl_ready, 8 * PREP["mix"])
            pe.wait_ge(sem("const_loaded"), 16)
            pe.wait_ge(sem("small_loaded"), 16)
            for j in range(6):
                c = START["xbc"] + j
                tile(c, j, XH, XL, base=xl0 if j == 0 else None, first=j < 2)
                if j == 0:
                    sum_squares("mix")
                    for tt in range(TT):
                        ins = pe.matmul(mis[:, 1, 16 + tt:17 + tt], SSUM[:, tt * P:tt * P + P], con("ones", 0, 1),
                                        start=True, stop=True, skip_group_check=True)
                    ins.then_inc(sem("rst_ps"), 1)
                if j == 3:
                    sum_squares("mem")
            for name in ("q", "k", "z"):
                for j in range(4):
                    tile(START[name] + j, TILE[name] + j, XH, XL)
            token_major(START["v"], TILE["v"], XH, XL)
            for tt in range(TT):
                for k in range(KD):
                    ins = pe.matmul(mis[:, 1, tt * 8:tt * 8 + 8], G[:, k, tt * P:tt * P + P],
                                    small("w_dt")[:, k * 8:k * 8 + 8], start=k == 0, stop=k == KD - 1,
                                    skip_group_check=True)
            ins.then_inc(sem("dt_ps"), 1)
            for j in range(4):
                tile(START["mem_k"] + j, TILE["mem_k"] + j, YH, YL, base=(yl_ready, Y_BASE["mem"]) if j == 0 else None)
            token_major(START["mem_v"], TILE["mem_v"], YH, YL)

            pe.wait_ge(sem("xb_done"), 6)
            for c in range(TT):
                for j in range(4):
                    ins = pe.transpose(big[:, c, j * P:j * P + P], XB[:, j, c * P:c * P + P], con("ident"))
                ins.then_inc(sem("xs_ps"), 1)
            for c in range(TT):
                for g in range(2):
                    h = slice(64 * g, 64 * g + 64)
                    ins = pe.matmul(big[:, 2 + g, c * P:c * P + P], XB[h, 4, c * P:c * P + P],
                                    XB[h, 5, c * P:c * P + P], start=True, stop=True, skip_group_check=True)
            ins.then_inc(sem("cb_ps"), 1)
            pe.transpose(big[:, 3, 256:384], XB[:, 4, 0:P], con("ident")).then_inc(sem("bt_ps"), 1)
            pe.wait_ge(sem("an_done"), 1)
            for c in range(TT):
                pe.matmul(mis[:, 1, 32 + 8 * c:40 + 8 * c], con("tri"), AN[:, c, :], start=True, stop=True,
                          skip_group_check=True)
            pe.matmul(mis[:, 1, 48:56], con("ones"), AN[:, 0, :], start=True, stop=True,
                      skip_group_check=True).then_inc(sem("acl_ps"), 1)
            pe.wait_ge(sem("abc_done"), 1)
            for c in range(TT):
                acc_ready(TILE["seg"] + 2 * c)
                acc_ready(TILE["seg"] + 2 * c + 1)
                for h in range(8):
                    ins = pe.matmul(acc[:, h // 4, (h % 4) * P:(h % 4 + 1) * P], ABC[:, c, h, :], con("tri"),
                                    start=True, stop=True, skip_group_check=True)
                ins.then_inc(sem("seg_ps"), 1)
            pe.wait_ge(sem("xcd_done"), 1)
            for g in range(2):
                ins = pe.matmul(big[64 * g:64 * g + 64, 3, 0:256], BT[:, 64 * g:64 * g + 64],
                                XCD[:, 256 * g:256 * g + 256], start=True, stop=True, skip_group_check=True)
            ins.then_inc(sem("st_ps"), 1)
            for c in range(TT):
                pe.wait_ge(sem("mm_done"), c + 1)
                if c == 1:
                    pe.wait_ge(sem("ce_done"), 1)
                for h in range(8):
                    p, g = h // 2, h // 4
                    half = slice(64 * (h % 2), 64 * (h % 2) + 64)
                    o = big[half, p // 2, (p % 2) * T + c * P:(p % 2) * T + c * P + P]
                    ins = pe.matmul(o, XC[:, c, 64 * h:64 * h + 64], MM[:, c, h, :], start=True, stop=c == 0,
                                    skip_group_check=True)
                    if c == 1:
                        gs = slice(64 * g, 64 * g + 64)
                        ins = pe.matmul(o, ST[gs, (h % 4) * 64:(h % 4) * 64 + 64], CE[gs, h % 4, :], start=False,
                                        stop=True, skip_group_check=True)
            ins.then_inc(sem("y_ps"), 1)

            pe.wait_ge(sem("y_read"), 1)
            def scores(h):
                half, p = slice(64 * (h % 2), 64 * (h % 2) + 64), h // 2
                if h >= 2:
                    pe.wait_ge(sem("sb_arg"), h - 1)
                z = big[:, h % 2, :]
                pe.matmul(z[:, 0:T], KT[half, p, 0:P], QT[half, p, :], start=True, stop=True, skip_group_check=True)
                pe.matmul(z[:, T:T + P], KT[half, p, P:T], QT[half, p, P:T], start=False, stop=True,
                          skip_group_check=True).then_inc(sem("sb_z"), 1)

            def later(h):
                pe.wait_ge(sem("sb_sp"), h + 1)
                z, s = big[:, h % 2, :], SBP[:, h % 2, :]
                pe.matmul(z[:, 0:T], con("neg_upto"), s[:, 0:T], start=False, stop=True, skip_group_check=True)
                pe.matmul(z[:, P:T], con("neg_ones"), s[:, T:T + P], start=False, stop=True, skip_group_check=True)
                pe.matmul(z[:, T:T + P], con("neg_upto"), s[:, T:T + P], start=False, stop=True,
                          skip_group_check=True).then_inc(sem("sb_c"), 1)

            def outputs(h):
                half, p = slice(64 * (h % 2), 64 * (h % 2) + 64), h // 2
                pe.wait_ge(sem("sb_w"), h + 1)
                if p >= 2:
                    pe.wait_ge(sem("os_done"), p - 1)
                o, w = big[half, 2 + p % 2, 0:T], SBW[:, h % 2, :]
                pe.matmul(o, V[:, 0, 64 * h:64 * h + 64], w[:, 0:T], start=True, stop=False, skip_group_check=True)
                pe.matmul(o[:, P:T], V[:, 1, 64 * h:64 * h + 64], w[:, T:T + P], start=False, stop=True,
                          skip_group_check=True).then_inc(sem("sb_o"), 1)

            for i in range(SB_HEADS + 1):
                if i < SB_HEADS:
                    scores(i)
                if i >= 1:
                    later(i - 1)
                    outputs(i - 1)
                if i == 2:
                    sum_squares("ssd")
            sum_squares("sb")

            for j in range(KD):
                tile(START["w_out"] + j, TILE["w_out"] + j, YH, YL, base=(yl_ready, Y_BASE["mixer"]) if j == 0 else None)
            for h in range(XA_HEADS):
                tile(START["xq"] + h, TILE["xq"] + h, XH, XL, base=(xl_ready, 8 * PREP["xa"]) if h == 0 else None)
                if h == 0:
                    sum_squares("xa")

            def xa_scores(h):
                pe.wait_ge(acc_free, TILE["xq"] + h + 1)
                if h >= 2:
                    pe.wait_ge(sem("xa_p"), h - 1)
                for tt in range(TT):
                    ins = pe.matmul(big[:, h % 2, tt * T:tt * T + T], QT[:, h, tt * P:tt * P + P], MK[:, h, :],
                                    start=True, stop=True, skip_group_check=True)
                ins.then_inc(sem("xa_s"), 1)

            def xa_turn(h):
                pe.wait_ge(sem("xa_pn"), h + 1)
                if h >= 1:
                    pe.wait_ge(sem("xa_pt"), h)
                for m in range(2):
                    for tt in range(TT):
                        ins = pe.transpose(big[:, 2, m * T + tt * P:m * T + tt * P + P],
                                           SEG_P(h)[:, tt, m * P:m * P + P], con("ident"))
                ins.then_inc(sem("xa_t"), 1)

            def xa_out(h):
                pe.wait_ge(sem("xa_pt"), h + 1)
                if h >= 2:
                    pe.wait_ge(yl_ready, Y_BASE["xa"] + h - 1)
                for m in range(2):
                    ins = pe.matmul(XO(h), MV[:, m, h * P:h * P + P],
                                    XPT(h)[:, m, :], start=m == 0, stop=m == 1, skip_group_check=True)
                ins.then_inc(sem("xa_o"), 1)

            for i in range(XA_HEADS + 1):
                if i < XA_HEADS:
                    xa_scores(i)
                if i >= 1:
                    xa_turn(i - 1)
                    xa_out(i - 1)
            for i in range(4):
                c = START["xo"] + i
                chunk_ready(c)
                for m in range(2):
                    t = TILE["xo"] + 2 * i + m
                    acc_ready(t)
                    for k in range(4):
                        if i == 0 and m == 0:
                            pe.wait_ge(yl_ready, Y_BASE["xa"] + k + 1)
                        ins = three(acc[:, t % 2, 0:T], c % SPL, (4 * m + k) * P, YH[:, k], YL[:, k], k == 0, k == 3)
                ins.then_inc(w_used, 1)

            def wide(c, slot, us, first, last):
                chunk_ready(c)
                for m in range(KD):
                    o = big[:, m // 2, (m % 2) * T:(m % 2) * T + T]
                    ins = three(o, slot, m * P, UH[:, us], UL[:, us], first and m % 2 == 0, last)
                ins.then_inc(w_used, 1)

            u_low = sem("u_low")
            C0, T0 = START["ff"], TILE["ff"]
            tile(C0, T0, XH, XL, base=(xl_ready, 8 * PREP["ff"]))
            sum_squares("ff")
            tile(C0 + 1, T0 + 1, XH, XL)
            pe.wait_ge(u_low, 1)
            wide(C0 + 2, (C0 + 2) % SPL, 0, True, False)
            S = 6
            with pe.Fori(0, 4) as t:
                for u in range(S):
                    j = 2 + u
                    tile(t * 12 + (C0 + 2 * j - 1), t * 6 + (T0 + j), XH, XL, slot=(C0 + 2 * j - 1) % SPL,
                         bank=(T0 + j) % 2)
                    pe.wait_ge(u_low, t * 6 + j)
                    wide(t * 12 + (C0 + 2 * j), (C0 + 2 * j) % SPL, (j - 1) % 2, False, False)
            for j in range(26, FF_TILES):
                tile(C0 + 2 * j - 1, T0 + j, XH, XL)
                pe.wait_ge(u_low, j)
                wide(C0 + 2 * j, (C0 + 2 * j) % SPL, (j - 1) % 2, False, False)
            pe.wait_ge(u_low, FF_TILES)
            wide(C0 + 2 * FF_TILES - 1, (C0 + 2 * FF_TILES - 1) % SPL, (FF_TILES - 1) % 2, False, True)
            sum_squares("final")
            for j in range(16):
                tile(START["pw1"] + j, TILE["pw1"] + j, XH, XL, base=(xl_ready, 8 * PREP["mix2_0"]) if j == 0 else None)
                if j == 0:
                    sum_squares("mix2_0")
            pe.wait_ge(sem("cx_sum"), 1)
            pe.matmul(mis[:, 1, 0:T], con("ones"), SSUM[:, :], start=True, stop=True,
                      skip_group_check=True).then_inc(sem("mean_ps"), 1)
            sum_squares("ln")
            for j in range(KD):
                tile(START["pw2"] + j, TILE["pw2"] + j, YH, YL, base=(yl_ready, Y_BASE["pw2"]) if j == 0 else None)

            def ffn(i):
                C0, T0 = START[f"ffn{i}"], TILE[f"ffn{i}"]
                base_u = FF_TILES + i * UP_TILES
                tile(C0, T0, XH, XL, base=(xl_ready, 8 * PREP[f"ffn2_{i}"]))
                sum_squares(f"ffn2_{i}")
                tile(C0 + 1, T0 + 1, XH, XL)

                def step(c, tl, uc, cs, ts, us, first):
                    tile(c, tl, XH, XL, slot=cs % SPL, bank=ts % 2)
                    tile(c + 1, tl + 1, XH, XL, slot=(cs + 1) % SPL, bank=(ts + 1) % 2)
                    pe.wait_ge(u_low, uc)
                    wide(c + 2, (cs + 2) % SPL, us % 2, first, False)

                for t, js in turns_of_up(pe):
                    cs, ts, us = C0 + 3 * js - 1, T0 + 2 * js, base_u + js
                    step(plus(t, 6, cs), plus(t, 4, ts), plus(t, 2, us), cs, ts, js - 1, js == 1)
                pe.wait_ge(u_low, base_u + UP_TILES)
                c = C0 + 3 * UP_TILES - 1
                wide(c, c % SPL, (UP_TILES - 1) % 2, False, True)

            ffn(0)
            pe_nsa(pe, tile, token_major, three, sum_squares, chunk_ready, acc_ready)
            for j in range(KD):
                tile(START["nsa_out"] + j, TILE["nsa_out"] + j, YH, YL, base=(yl_ready, Y_BASE["nsa"]) if j == 0 else None)
            ffn(1)

        @block.scalar
        def _(act):
            ch = Chain(act, act_chain)
            link = ch.link

            def high(turn, per, cs):
                act.wait_ge(raw_loaded[cs % RAW], plus(turn, 16 * per // RAW, 16 * (cs // RAW + 1)))
                if cs >= SPL:
                    act.wait_ge(w_used, plus(turn, per, cs - SPL + 1))
                act.activation(WH[:, cs % SPL], WR[:, cs % RAW], ACT.Copy).then_inc(w_high, 1)

            sp = Splitter(high)

            def prep_one(name, k):
                act.wait_ge(gx_ready, 8 * PREP[name] + k + 1)
                act.activation(XH[:, k], G[:, k], ACT.Copy).then_inc(xh_ready, 1)
                act.activation(SQ[:, k], X[:, k], ACT.Square).then_inc(sq_ready, 1)

            def prep(name):
                for k in range(KD):
                    prep_one(name, k)

            def rstd(name, out):
                act.wait_ge(nps_ready, NORM[name] + 1)
                e = con("eps", int(NORM[name] > NORM["final"]), int(NORM[name] > NORM["final"]) + 1)
                link(act.activation(LNV[:, :], mis[:, 0, 0:T], ACT.Ln, bias=e, scale=1.0 / NORM_DIM.get(name, D)))
                act.activation(out[:, :], LNV[:, :], ACT.Exp, scale=-0.5).then_inc(rstd_ready, 1)

            def y_high(stage, k):
                act.wait_ge(gy_ready, GY_BASE[stage] + k + 1)
                act.activation(YH[:, k], GY[:, k], ACT.Copy).then_inc(yh_ready, 1)

            sp.to(1)
            prep("mix")
            sp.to(2)
            act.wait_ge(sem("mem_loaded"), 16)
            act.wait_ge(sem("const_loaded"), 16)
            rstd("mix", RS)
            act.wait_ge(sem("rst_ps"), 1)
            link(act.activation(RST[:, 1, :], mis[:, 1, 16:18], ACT.Ln, bias=con("eps", 0, 1), scale=1.0 / D))
            act.activation(RST[:, 0, :], RST[:, 1, :], ACT.Exp, scale=-0.5).then_inc(sem("rst_done"), 1)
            link(act.activation(EAL[:, :], VEC[:, VCOL["a_log"]:VCOL["a_log"] + 8], ACT.Exp))
            sp.to(3)
            act.wait_ge(ssum_ready, 1)
            for k in range(KD):
                act.activation(SQ[:, k], MEM[:, k], ACT.Square).then_inc(sq_ready, 1)
            sp.to(6)
            rstd("mem", RS2)
            for j in range(6):
                act.wait_ge(sem("cv_done"), j + 1)
                act.activation(XB[:, j], CV[:, j], ACT.Silu).then_inc(sem("xb_done"), 1)
                sp.to(7 + j)
            for k in range(8):
                sp.to(13 + k)
                y_high("mem", k)
            act.wait_ge(acc_free, TILE["z"] + 4)
            act.activation(ZT[:, :, :], ZT[:, :, :], ACT.Silu).then_inc(sem("z_silu"), 1)
            sp.to(24)
            act.wait_ge(sem("dtr_done"), 1)
            link(act.activation(DTE[:, :, :], DTE[:, :, :], ACT.Exp))
            act.activation(DTE[:, :, :], DTE[:, :, :], ACT.Ln, bias=1.0).then_inc(sem("dte_done"), 1)
            sp.to(START["w_out"] + AHEAD)
            act.wait_ge(sem("ds_in"), 1)
            act.activation(DS[:, :], DS[:, :], ACT.Exp).then_inc(sem("ds_done"), 1)
            for c in range(TT):
                if c == 1:
                    act.wait_ge(sem("seg_ps"), 2)
                    act.activation(EA[:, :, :], acc[:, :, :].rearrange("p a (h l) -> p (a h) l", h=4),
                                   ACT.Exp).then_inc(sem("ea_done"), 1)
                act.wait_ge(sem("seg_done"), c + 1)
                act.activation(SEG[:, :, :], SEG[:, :, :], ACT.Exp).then_inc(sem("seg_exp"), 1)

            def sb_soft(h):
                act.wait_ge(sem("sb_z"), h + 1)
                e = SBE[:, h % 2, 0:384]
                link(act.activation(e, big[:, h % 2, 0:384], ACT.Abs))
                link(act.activation(e, e, ACT.Exp, scale=-1.0))
                act.activation(e, e, ACT.Ln, bias=1.0).then_inc(sem("sb_ln"), 1)

            def sb_exp(h):
                act.wait_ge(sem("sb_arg"), h + 1)
                w = SBW[:, h % 2, 0:384]
                act.activation(w, w, ACT.Exp).then_inc(sem("sb_we"), 1)

            for i in range(SB_HEADS + 1):
                if i < SB_HEADS:
                    sb_soft(i)
                if i >= 1:
                    sb_exp(i - 1)
                if i == 1:
                    for p in range(4):
                        act.wait_ge(sem("ys_done"), p + 1)
                        act.activation(SQ[:, p], YS(p), ACT.Square).then_inc(sq_ready, 1)
                if i == 3:
                    rstd("ssd", RS2)
                if i == 5:
                    for k in range(4):
                        y_high("mixer", k)
            for p in range(4):
                act.wait_ge(sem("os_done"), p + 1)
                act.activation(SQ[:, p], OS[:, p], ACT.Square).then_inc(sq_ready, 1)
            rstd("sb", RS2)
            for k in range(4, 8):
                y_high("mixer", k)
            for j in range(KD):
                sp.to(START["w_out"] + j + 1 + AHEAD)
                prep_one("xa", j)
            sp.to(START["xq"] + 1 + AHEAD)
            rstd("xa", RS)
            for j in range(4):
                sp.to(START["xq"] + j + 1 + AHEAD)

            def xa_exp(h):
                act.wait_ge(sem("xa_nm"), h + 1)
                for tt in range(TT):
                    ch.add(act.activation(SEG_P(h)[:, tt, :], big[:, h % 2, tt * T:tt * T + T], ACT.Exp,
                                          bias=XSTAT[:, 0, h % 2, tt:tt + 1], accum_out=XSTAT[:, 1, h % 2, tt:tt + 1]))
                act.wait_ge(act_chain, ch.value())
                act.sem_inc(sem("xa_p"), 1)

            for i in range(XA_HEADS + 1):
                if i < XA_HEADS:
                    xa_exp(i)
                if i >= 1:
                    h = i - 1
                    act.wait_ge(sem("xa_t"), h + 1)
                    act.activation(XPT(h).rearrange("p m t -> p (m t)"), big[:, 2, :],
                                   ACT.Copy).then_inc(sem("xa_pt"), 1)
                    act.wait_ge(sem("xa_o"), h + 1)
                    act.activation(YH[:, h], XO(h), ACT.Copy).then_inc(yh_ready, 1)
            for i in range(4):
                sp.to(START["xo"] + i + 1 + AHEAD)
                prep_one("ff", 2 * i)
                prep_one("ff", 2 * i + 1)

            gu_ready, u_high = sem("gu_ready"), sem("u_high")

            def u_split(turn, per, us):
                act.wait_ge(gu_ready, plus(turn, per, us + 1))
                act.activation(UH[:, us % 2], GU[:, us % 2], ACT.Copy).then_inc(u_high, 1)

            C0 = START["ff"]
            sp.to(C0 + 3)
            rstd("ff", RS)
            for j in range(2):
                u_split(0, 0, j)
                sp.to(C0 + 4 + j)
            with act.Fori(0, 4) as t:
                for u in range(6):
                    j = 2 + u
                    sp.in_loop(t, 12, C0 + 2 * j + 1)
                    u_split(t, 6, j)
                    sp.in_loop(t, 12, C0 + 2 * j + 2)
            sp.ran(48)
            for j in range(26, FF_TILES):
                sp.to(C0 + 2 * j + 2)
                u_split(0, 0, j)
                sp.to(C0 + 2 * j + 3)
            sp.to(START["pw1"] + AHEAD)
            act.wait_ge(sem("x_res"), 1)
            for k in range(KD):
                act.activation(SQ[:, k], X[:, k], ACT.Square).then_inc(sq_ready, 1)
            rstd("final", RS2)
            prep("mix2_0")

            C0 = START["pw1"]
            sp.to(C0 + 3)
            rstd("mix2_0", RS)
            for j in range(8):
                sp.to(C0 + 2 * j + 3)
                act.wait_ge(sem("gate_in"), j + 1)
                act.activation(SG[:, j % 2], SG[:, j % 2], ACT.Sigmoid,
                               bias=vec("b_pw1", 2 * j)).then_inc(sem("gate_done"), 1)
                sp.to(C0 + 2 * j + 4)
            act.wait_ge(sem("cx_centred"), 1)
            for k in range(KD):
                act.activation(SQ[:, k], CX[:, k], ACT.Square).then_inc(sq_ready, 1)
            rstd("ln", RS2)
            for k in range(KD):
                act.wait_ge(gy_ready, GY_BASE["pw2"] + k + 1)
                link(act.activation(GY[:, k], GY[:, k], ACT.Silu, bias=vec("ln_b", k), scale=vec("ln_g", k)))
                act.activation(YH[:, k], GY[:, k], ACT.Copy).then_inc(yh_ready, 1)
            for j in range(KD):
                sp.to(START["pw2"] + j + 1 + AHEAD)
                prep_one("ffn2_0", j)

            def ffn(i):
                C0 = START[f"ffn{i}"]
                base_u, base_s = FF_TILES + i * UP_TILES, i * UP_TILES

                def silu(turn, js):
                    act.wait_ge(sem("fconv_done"), plus(turn, 2, base_s + js + 1))
                    act.activation(SA[:, js % 2], CA[:, js % 2], ACT.Silu).then_inc(sem("fsilu_done"), 1)

                sp.to(C0 + 3)
                rstd(f"ffn2_{i}", RS)
                silu(0, 0)
                sp.to(C0 + 4)
                u_split(0, 0, base_u)
                for t, js in turns_of_up(act):
                    cs = C0 + 3 * js - 1
                    if isinstance(t, int):
                        sp.to(cs + 3)
                        silu(0, js)
                        sp.to(cs + 4)
                        u_split(0, 0, base_u + js)
                        sp.to(cs + 5)
                    else:
                        sp.in_loop(t, 6, cs + 2)
                        silu(t, js)
                        sp.in_loop(t, 6, cs + 3)
                        u_split(t, 2, base_u + js)
                        sp.in_loop(t, 6, cs + 4)
                        if js == 3:
                            sp.ran(6 * UP_TURNS)

            ffn(0)
            sp.to(START["nsa_kc"] + AHEAD)
            prep("mix2_1")
            act_nsa(act, ch, sp, rstd)
            for j in range(KD):
                sp.to(START["nsa_out"] + j + 1 + AHEAD)
                prep_one("ffn2_1", j)
            ffn(1)

        @block.vector
        def _(dve):
            ch = Chain(dve, dve_chain)
            link = ch.link

            def low(turn, per, cs):
                dve.wait_ge(w_high, plus(turn, per, cs + 1))
                dve.tensor_tensor(WL[:, cs % SPL, 0:LO_DVE], WR[:, cs % RAW, 0:LO_DVE],
                                  WH[:, cs % SPL, 0:LO_DVE].bitcast(F32), ALU.subtract).then_inc(w_low_dve, 1)

            sp = Splitter(low)

            def gx(name, k):
                i = int(name[-1]) if name[-2] == "_" else 0
                dve.tensor_scalar(G[:, k], X[:, k], vec(GAIN[name], 8 * i + k), None,
                                  ALU.mult).then_inc(gx_ready, 1)

            def reduce_squares(name):
                n = SQ_COUNT.get(name, 8)
                dve.wait_ge(sq_ready, SQ_BASE[name] + n)
                if NORM[name] > 0:
                    dve.wait_ge(nps_ready, NORM[name])
                dve.tensor_reduce(SSUM[:, :], SQ[:, 0:n, :].rearrange("p k t -> p t k"), AX, ALU.add).then_inc(
                    ssum_ready, 1)

            def used(c, turn=0, per=0):
                dve.wait_ge(w_used, plus(turn, per, c + 1))

            def scaled(out, ts, turn=0, per=0, wait=True):
                dve.tensor_tensor(out, acc[:, ts % 2, 0:T], RS[:, :], ALU.mult).then_inc(acc_free, 1)
                if wait:
                    dve.wait_ge(acc_free, plus(turn, per, ts + 1))

            def residual(ts, k, name):
                link(dve.tensor_tensor(X[:, k], acc[:, ts % 2, 0:T], X[:, k], ALU.add))
                dve.sem_inc(acc_free, 1)
                gx(name, k)

            def rstd_done(name):
                dve.wait_ge(rstd_ready, NORM[name] + 1)

            dve.memset(XP[:, :, 0:3], 0.0)
            dve.wait_ge(sem("x_loaded"), 16)
            dve.wait_ge(sem("vec_loaded"), 16)
            for k in range(KD):
                gx("mix", k)
            sp.to(2)
            reduce_squares("mix")
            rstd_done("mix")
            dve.wait_ge(sem("const_loaded"), 16)

            def conv_in(j):
                x = lambda i: XP[:, j, i:i + T]
                w = lambda i: vec("conv_w", 4 * j + i)
                link(dve.tensor_scalar(CV[:, j], x(0), w(0), vec("conv_b", j), ALU.mult, ALU.add))
                for i in range(1, 4):
                    ins = dve.scalar_tensor_tensor(CV[:, j], x(i), w(i), CV[:, j], ALU.mult, ALU.add)
                    if i < 3:
                        link(ins)
                ins.then_inc(sem("cv_done"), 1)

            for j in range(6):
                sp.to(j + 1 + AHEAD)
                used(START["xbc"] + j)
                scaled(XP[:, j, 3:3 + T], TILE["xbc"] + j)
                conv_in(j)
                if j == 2:
                    dve.wait_ge(sem("rst_ps"), 1)
                    reduce_squares("mem")
            for j in range(4):
                sp.to(START["q"] + j + 1 + AHEAD)
                used(START["q"] + j)
                t = TILE["q"] + j
                dve.scalar_tensor_tensor(QT[:, j], acc[:, t % 2, 0:T], 0.125, RS[:, :], ALU.mult,
                                         ALU.mult).then_inc(acc_free, 1)
            rstd_done("mem")
            for k in range(KD):
                dve.scalar_tensor_tensor(GY[:, k], MEM[:, k], vec("mem_g", k), RS2[:, :], ALU.mult,
                                         ALU.mult).then_inc(gy_ready, 1)
            for j in range(4):
                sp.to(START["k"] + j + 1 + AHEAD)
                used(START["k"] + j)
                scaled(KT[:, j], TILE["k"] + j, wait=False)
            for j in range(4):
                sp.to(START["z"] + j + 1 + AHEAD)
                used(START["z"] + j)
                scaled(ZT[:, j], TILE["z"] + j, wait=False)
            for i in range(4):
                sp.to(START["v"] + i + 1 + AHEAD)
            used(START["v"] + 3)
            dve.wait_ge(sem("rst_done"), 1)
            for tt in range(TT):
                dve.tensor_scalar(V[:, tt], acc[:, (TILE["v"] + tt) % 2, :], RST[:, 0, tt:tt + 1], None,
                                  ALU.mult).then_inc(acc_free, 1)
            dve.wait_ge(sem("dt_ps"), 1)
            for tt in range(TT):
                ins = dve.scalar_tensor_tensor(DTR[:, tt], mis[:, 1, tt * 8:tt * 8 + 8], RST[:, 0, tt:tt + 1],
                                               VEC[:, VCOL["dt_bias"]:VCOL["dt_bias"] + 8], ALU.mult, ALU.add)
                link(ins)
            dve.scalar_tensor_tensor(DTE[:, :, :], DTR[:, :, :], -1.0, DTR[:, :, :], ALU.mult,
                                     ALU.min).then_inc(sem("dtr_done"), 1)
            sp.to(START["mem_k"] + AHEAD)
            dve.wait_ge(sem("dte_done"), 1)
            link(dve.scalar_tensor_tensor(DT[:, :, :], DTR[:, :, :], 0.0, DTE[:, :, :], ALU.max, ALU.add))
            link(dve.scalar_tensor_tensor(AN[:, :, :], DT[:, :, :], -1.0,
                                          EAL[:, :].unsqueeze(1).broadcast_to([P, TT, 8]), ALU.mult, ALU.mult))
            dve.sem_inc(sem("an_done"), 1)
            dve.tensor_copy(ABC.rearrange("p c h l -> p (c h) l"),
                            AN.rearrange("p c h -> p (c h)").unsqueeze(2).broadcast_to([P, 16, P])).then_inc(
                sem("abc_done"), 1)
            for j in range(4):
                sp.to(START["mem_k"] + j + 1 + AHEAD)
                used(START["mem_k"] + j)
                dve.tensor_copy(MK[:, j], acc[:, (TILE["mem_k"] + j) % 2, 0:T]).then_inc(acc_free, 1)
            for i in range(4):
                sp.to(START["mem_v"] + i + 1 + AHEAD)
            used(START["mem_v"] + 3)
            for tt in range(TT):
                dve.tensor_copy(MV[:, tt], acc[:, (TILE["mem_v"] + tt) % 2, :]).then_inc(acc_free, 1)

            for c in range(TT):
                dve.wait_ge(sem("xs_ps"), c + 1)
                link(dve.tensor_tensor(XC[:, c].rearrange("p (h d) -> p h d", h=8),
                                       big[:, c, :].rearrange("p (h d) -> p h d", h=8),
                                       DT[:, c, :].unsqueeze(2).broadcast_to([P, 8, 64]), ALU.mult))
            dve.wait_ge(sem("bt_ps"), 1)
            dve.tensor_copy(BT[:, :], big[:, 3, 256:384])
            dve.wait_ge(sem("cb_ps"), 1)
            dve.tensor_tensor(CBM.rearrange("p (c g) s -> p g c s", c=2),
                              big[:, 2:4, 0:T].rearrange("p g (c s) -> p g c s", c=2),
                              con("tri").unsqueeze(1).unsqueeze(1).broadcast_to([P, 2, 2, P]), ALU.mult)
            dve.wait_ge(sem("acl_ps"), 1)
            link(dve.tensor_copy(ACL[:, :, :], mis[:, 1, 32:56].rearrange("p (c h) -> p c h", c=3)))
            dve.tensor_tensor(DS[:, :], ACL[:, 2, :], ACL[:, 0, :], ALU.subtract).then_inc(sem("ds_in"), 1)
            dve.wait_ge(sem("ds_done"), 1)
            dve.tensor_tensor(XCD[:, :].rearrange("p (h d) -> p h d", h=8), XC[:, 0].rearrange("p (h d) -> p h d", h=8),
                              DS[:, :].unsqueeze(2).broadcast_to([P, 8, 64]), ALU.mult).then_inc(sem("xcd_done"), 1)
            for c in range(TT):
                dve.wait_ge(sem("seg_ps"), c + 1)
                if c == 1:
                    dve.wait_ge(sem("ea_done"), 1)
                    dve.wait_ge(sem("mm_done"), 1)
                link(dve.tensor_tensor(SEG[:, :, :], acc[:, :, :].rearrange("p a (h l) -> p (a h) l", h=4),
                                       ACL[:, c, :].unsqueeze(2).broadcast_to([P, 8, P]), ALU.subtract))
                dve.sem_inc(acc_free, 2)
                dve.tensor_scalar(SEG[:, :, :], SEG[:, :, :], 0.0, None, ALU.min).then_inc(sem("seg_done"), 1)
                dve.wait_ge(sem("seg_exp"), c + 1)
                dve.tensor_tensor(MM[:, c].rearrange("p (g e) l -> p g e l", g=2),
                                  SEG[:, :, :].rearrange("p (g e) l -> p g e l", g=2),
                                  CBM[:, 2 * c:2 * c + 2, :].unsqueeze(2).broadcast_to([P, 2, 4, P]),
                                  ALU.mult).then_inc(sem("mm_done"), 1)
            for g in range(2):
                gs = slice(64 * g, 64 * g + 64)
                link(dve.tensor_tensor(CE[gs, :, :], XB[gs, 5, P:T].unsqueeze(1).broadcast_to([64, 4, P]),
                                       EA[gs, 4 * g:4 * g + 4, :], ALU.mult))
            dve.wait_ge(sem("st_ps"), 1)
            dve.tensor_copy(ST[:, :], big[:, 3, 0:256]).then_inc(sem("ce_done"), 1)
            dve.wait_ge(sem("y_ps"), 1)
            dve.wait_ge(sem("z_silu"), 1)
            for p in range(4):
                link(dve.scalar_tensor_tensor(XP[:, p, 0:T], XB[:, p], vec("d_skip", p),
                                              big[:, p // 2, (p % 2) * T:(p % 2) * T + T], ALU.mult, ALU.add))
                if p == 3:
                    dve.sem_inc(sem("y_read"), 1)
                dve.tensor_tensor(YS(p), XP[:, p, 0:T], ZT[:, p], ALU.mult).then_inc(sem("ys_done"), 1)

            def diagonal(x):
                return x.rearrange("p (a n) -> p a n", a=2)[:, :, 0:P]

            strict = con("strict").unsqueeze(1).broadcast_to([P, 2, P])

            def out_tile(p):
                dve.wait_ge(sem("sb_o"), 2 * p + 2)
                dve.tensor_copy(OS[:, p], big[:, 2 + p % 2, 0:T]).then_inc(sem("os_done"), 1)

            def arg(h):
                dve.wait_ge(sem("sb_c"), h + 1)
                dve.tensor_scalar(SBW[:, h % 2, 0:384], big[:, h % 2, 0:384], 0.0, None,
                                  ALU.min).then_inc(sem("sb_arg"), 1)

            def weights(h):
                dve.wait_ge(sem("sb_we"), h + 1)
                d = diagonal(SBW[:, h % 2, :])
                dve.tensor_tensor(d, d, strict, ALU.mult).then_inc(sem("sb_w"), 1)

            for i in range(SB_HEADS + 1):
                if i >= 1:
                    arg(i - 1)
                if i < SB_HEADS:
                    dve.wait_ge(sem("sb_ln"), i + 1)
                    s = SBP[:, i % 2, :]
                    link(dve.scalar_tensor_tensor(s[:, 0:384], big[:, i % 2, 0:384], 0.0, SBE[:, i % 2, 0:384],
                                                  ALU.max, ALU.add))
                    dve.tensor_tensor(diagonal(s), diagonal(s), strict, ALU.mult).then_inc(sem("sb_sp"), 1)
                if i >= 1:
                    weights(i - 1)
                if i == 1:
                    reduce_squares("ssd")
                if i >= 3 and i % 2 == 1:
                    out_tile((i - 3) // 2)
                if i == 4:
                    rstd_done("ssd")
                    for k in range(4):
                        dve.scalar_tensor_tensor(GY[:, k], YS(k), vec("ssd_g", k), RS2[:, :], ALU.mult,
                                                 ALU.mult).then_inc(gy_ready, 1)
            out_tile(3)
            reduce_squares("sb")
            rstd_done("sb")
            for k in range(4):
                dve.scalar_tensor_tensor(GY[:, 4 + k], OS[:, k], vec("sb_g", k), RS2[:, :], ALU.mult,
                                         ALU.mult).then_inc(gy_ready, 1)
            for j in range(KD):
                sp.to(START["w_out"] + j + 1 + AHEAD)
                used(START["w_out"] + j)
                residual(TILE["w_out"] + j, j, "xa")
            reduce_squares("xa")
            for h in range(XA_HEADS):
                sp.to(START["xq"] + h + 1 + AHEAD)
                used(START["xq"] + h)
                if h == 0:
                    rstd_done("xa")
                dve.scalar_tensor_tensor(QT[:, h], acc[:, (TILE["xq"] + h) % 2, 0:T], float(P) ** -0.5, RS[:, :],
                                         ALU.mult, ALU.mult).then_inc(acc_free, 1)
            for i in range(XA_HEADS + 1):
                if i < XA_HEADS:
                    dve.wait_ge(sem("xa_s"), i + 1)
                    dve.tensor_reduce(XSTAT[:, 0, i % 2, :], big[:, i % 2, :].rearrange("p (a m) -> p a m", a=2), AX,
                                      ALU.max, negate=True).then_inc(sem("xa_nm"), 1)
                    dve.wait_ge(sem("xa_p"), i + 1)
                    link(dve.reciprocal(XSTAT[:, 2, i % 2, :], XSTAT[:, 1, i % 2, :]))
                    dve.tensor_tensor(SEG_P(i), SEG_P(i), XSTAT[:, 2, i % 2, :].unsqueeze(2).broadcast_to([P, TT, T]),
                                      ALU.mult).then_inc(sem("xa_pn"), 1)
                if i >= 1:
                    h = i - 1
                    dve.wait_ge(yh_ready, Y_BASE["xa"] + h + 1)
                    dve.tensor_tensor(YL[:, h], XO(h), YH[:, h].bitcast(F32),
                                      ALU.subtract).then_inc(yl_ready, 1)
            for i in range(4):
                sp.to(START["xo"] + i + 1 + AHEAD)
                used(START["xo"] + i)
                residual(TILE["xo"] + 2 * i, 2 * i, "ff")
                residual(TILE["xo"] + 2 * i + 1, 2 * i + 1, "ff")
            reduce_squares("ff")

            gu_ready, u_low = sem("gu_ready"), sem("u_low")

            def hidden(turn, per, js):
                ts = TILE["ff"] + js
                scaled(TA[:, js % 2], ts, turn, per)
                if js >= 2:
                    dve.wait_ge(u_low, plus(turn, per, js - 1))
                dve.scalar_tensor_tensor(GU[:, js % 2], TA[:, js % 2], 0.0, TA[:, js % 2], ALU.max,
                                         ALU.mult).then_inc(gu_ready, 1)

            C0 = START["ff"]
            sp.to(C0 + 1 + AHEAD)
            rstd_done("ff")
            for j in range(2):
                used(C0 + j)
                hidden(0, 0, j)
                sp.to(C0 + 4 + j)
            with dve.Fori(0, 4) as t:
                for u in range(6):
                    j = 2 + u
                    sp.in_loop(t, 12, C0 + 2 * j + 1)
                    used(C0 + 2 * j - 1, t, 12)
                    hidden(t, 6, j)
                    sp.in_loop(t, 12, C0 + 2 * j + 2)
            sp.ran(48)
            for j in range(26, FF_TILES):
                sp.to(C0 + 2 * j + 2)
                used(C0 + 2 * j - 1)
                hidden(0, 0, j)
                sp.to(C0 + 2 * j + 3)
            sp.to(START["pw1"] + AHEAD)

            def add_wide(c):
                used(c)
                f = lambda x: x.rearrange("p k t -> p (k t)")
                link(dve.tensor_tensor(f(X[:, :, :]), f(big[:, :, :]), f(X[:, :, :]), ALU.add))

            add_wide(C0 + 2 * FF_TILES - 1)
            dve.sem_inc(sem("x_res"), 1)
            reduce_squares("final")
            rstd_done("final")
            for k in range(KD):
                link(dve.scalar_tensor_tensor(X[:, k], X[:, k], vec("final_g", k), RS2[:, :], ALU.mult, ALU.mult))
                gx("mix2_0", k)
            reduce_squares("mix2_0")

            dve.memset(UPAD[:, :, 0:CONV_W - 1], 0.0)
            sp.to(START["pw1"] + 1 + AHEAD)
            rstd_done("mix2_0")
            for j in range(KD):
                c, t = START["pw1"] + 2 * j, TILE["pw1"] + 2 * j
                sp.to(c + 1 + AHEAD)
                used(c)
                scaled(SG[:, j % 2], t)
                dve.sem_inc(sem("gate_in"), 1)
                sp.to(c + 2 + AHEAD)
                used(c + 1)
                scaled(AT[:, j % 2], t + 1)
                dve.wait_ge(sem("gate_done"), j + 1)
                link(dve.scalar_tensor_tensor(UPAD[:, j, CONV_W - 1:], AT[:, j % 2], vec("b_pw1", 2 * j + 1), SG[:, j % 2],
                                              ALU.add, ALU.mult))
                link(dve.tensor_scalar(CX[:, j], UPAD[:, j, 0:T], vec("w_dw", CONV_W * j), vec("b_dw", j), ALU.mult,
                                       ALU.add))
                for i in range(1, CONV_W):
                    link(dve.scalar_tensor_tensor(CX[:, j], UPAD[:, j, i:i + T], vec("w_dw", CONV_W * j + i), CX[:, j],
                                                  ALU.mult, ALU.add))
            dve.wait_ge(nps_ready, NORM["ln"])
            dve.tensor_reduce(SSUM[:, :], CX[:, :, :].rearrange("p k t -> p t k"), AX, ALU.add).then_inc(sem("cx_sum"), 1)
            dve.wait_ge(sem("mean_ps"), 1)
            link(dve.tensor_scalar(MU[:, :], mis[:, 1, 0:T], 1.0 / D, None, ALU.mult))
            link(dve.tensor_tensor(CX[:, :, :], CX[:, :, :], MU[:, :].unsqueeze(1).broadcast_to([P, KD, T]), ALU.subtract))
            dve.sem_inc(sem("cx_centred"), 1)
            reduce_squares("ln")
            rstd_done("ln")
            for k in range(KD):
                dve.tensor_tensor(GY[:, k], CX[:, k], RS2[:, :], ALU.mult).then_inc(gy_ready, 1)
            for j in range(KD):
                sp.to(START["pw2"] + j + 1 + AHEAD)
                used(START["pw2"] + j)
                t = TILE["pw2"] + j
                link(dve.scalar_tensor_tensor(X[:, j], acc[:, t % 2, 0:T], vec("b_pw2", j), X[:, j], ALU.add, ALU.add))
                dve.sem_inc(acc_free, 1)
                gx("ffn2_0", j)
            reduce_squares("ffn2_0")

            def ffn(i):
                C0, T0 = START[f"ffn{i}"], TILE[f"ffn{i}"]
                base_u, base_s = FF_TILES + i * UP_TILES, i * UP_TILES

                def step(turn, js, ca):
                    def w(q):
                        col = VCOL["fconv"] + 4 * (i * UP_TILES + js) + q
                        return VEC[:, col:col + 1] if isinstance(turn, int) else VEC[:, bass.ds(turn * 8 + col, 1)]

                    per_c, per_t = 6, 4
                    s = js % 2
                    if isinstance(turn, int):
                        sp.to(ca + 3)
                    else:
                        sp.in_loop(turn, 6, ca + 2)
                    used(ca, turn, per_c)
                    scaled(APD[:, s, 2:2 + T], T0 + 2 * js, turn, per_t)
                    ch.link(dve.tensor_scalar(CA[:, s], APD[:, s, 0:T], w(0), w(3), ALU.mult, ALU.add))
                    ch.link(dve.scalar_tensor_tensor(CA[:, s], APD[:, s, 1:1 + T], w(1), CA[:, s], ALU.mult, ALU.add))
                    dve.scalar_tensor_tensor(CA[:, s], APD[:, s, 2:2 + T], w(2), CA[:, s], ALU.mult,
                                             ALU.add).then_inc(sem("fconv_done"), 1)
                    if isinstance(turn, int):
                        sp.to(ca + 4)
                    else:
                        sp.in_loop(turn, 6, ca + 3)
                    used(ca + 1, turn, per_c)
                    scaled(VA[:, s], T0 + 2 * js + 1, turn, per_t)
                    dve.wait_ge(sem("fsilu_done"), plus(turn, 2, base_s + js + 1))
                    dve.wait_ge(u_low, plus(turn, 2, base_u + js - 1))
                    dve.tensor_tensor(GU[:, s], VA[:, s], SA[:, s], ALU.mult).then_inc(gu_ready, 1)
                    if js > 0:
                        if isinstance(turn, int):
                            sp.to(ca + 5)
                        else:
                            sp.in_loop(turn, 6, ca + 4)

                rstd_done(f"ffn2_{i}")
                step(0, 0, C0)
                for t, js in turns_of_up(dve, ch, 4):
                    step(t, js, C0 + 3 * js - 1)
                    if not isinstance(t, int) and js == 3:
                        sp.ran(6 * UP_TURNS)
                add_wide(C0 + 3 * UP_TILES - 1)

            dve.memset(APD[:, :, 0:2], 0.0)
            ffn(0)
            sp.to(START["nsa_kc"] + AHEAD)
            for k in range(KD):
                gx("mix2_1", k)
            reduce_squares("mix2_1")
            dve_nsa(dve, ch, sp, used, scaled, rstd_done)
            for j in range(KD):
                sp.to(START["nsa_out"] + j + 1 + AHEAD)
                used(START["nsa_out"] + j)
                residual(TILE["nsa_out"] + j, j, "ffn2_1")
            reduce_squares("ffn2_1")
            dve.memset(APD[:, :, 0:2], 0.0)
            ffn(1)
            dve.sem_inc(sem("result"), 1)

        @block.gpsimd
        def _(pool):
            def low(turn, per, cs):
                pool.wait_ge(w_high, plus(turn, per, cs + 1))
                pool.tensor_tensor(WL[:, cs % SPL, LO_DVE:], WR[:, cs % RAW, LO_DVE:],
                                   WH[:, cs % SPL, LO_DVE:].bitcast(F32), ALU.subtract).then_inc(w_low_pool, 1)

            sp = Splitter(low)

            def x_low(name, k):
                pool.wait_ge(xh_ready, 8 * PREP[name] + k + 1)
                pool.tensor_tensor(XL[:, k], G[:, k], XH[:, k].bitcast(F32), ALU.subtract).then_inc(xl_ready, 1)

            def y_low(stage, k):
                pool.wait_ge(yh_ready, Y_BASE[stage] + k + 1)
                pool.tensor_tensor(YL[:, k], GY[:, k], YH[:, k].bitcast(F32), ALU.subtract).then_inc(yl_ready, 1)

            def u_low_part(turn, per, us):
                pool.wait_ge(sem("u_high"), plus(turn, per, us + 1))
                pool.tensor_tensor(UL[:, us % 2], GU[:, us % 2], UH[:, us % 2].bitcast(F32),
                                   ALU.subtract).then_inc(sem("u_low"), 1)

            sp.to(1)
            for k in range(KD):
                x_low("mix", k)
            sp.to(12)
            for k in range(KD):
                sp.to(13 + k)
                y_low("mem", k)
            sp.to(START["w_out"] + AHEAD)
            for k in range(8):
                y_low("mixer", k)
            for j in range(KD):
                sp.to(START["w_out"] + j + 1 + AHEAD)
                x_low("xa", j)
            sp.to(START["xo"] + AHEAD)
            for i in range(4):
                sp.to(START["xo"] + i + 1 + AHEAD)
                x_low("ff", 2 * i)
                x_low("ff", 2 * i + 1)
            C0 = START["ff"]
            sp.to(C0 + 3)
            for j in range(2):
                u_low_part(0, 0, j)
                sp.to(C0 + 4 + j)
            with pool.Fori(0, 4) as t:
                for u in range(6):
                    j = 2 + u
                    sp.in_loop(t, 12, C0 + 2 * j + 1)
                    u_low_part(t, 6, j)
                    sp.in_loop(t, 12, C0 + 2 * j + 2)
            sp.ran(48)
            for j in range(26, FF_TILES):
                sp.to(C0 + 2 * j + 2)
                u_low_part(0, 0, j)
                sp.to(C0 + 2 * j + 3)
            sp.to(START["pw1"] + AHEAD)
            for k in range(KD):
                x_low("mix2_0", k)
            sp.to(START["pw2"] + AHEAD)
            for k in range(KD):
                y_low("pw2", k)
            for j in range(KD):
                sp.to(START["pw2"] + j + 1 + AHEAD)
                x_low("ffn2_0", j)

            def ffn(i):
                C0 = START[f"ffn{i}"]
                base_u = FF_TILES + i * UP_TILES
                sp.to(C0 + 4)
                u_low_part(0, 0, base_u)
                for t, js in turns_of_up(pool):
                    cs = C0 + 3 * js - 1
                    if isinstance(t, int):
                        sp.to(cs + 4)
                        u_low_part(0, 0, base_u + js)
                        sp.to(cs + 5)
                    else:
                        sp.in_loop(t, 6, cs + 2)
                        sp.in_loop(t, 6, cs + 3)
                        u_low_part(t, 2, base_u + js)
                        sp.in_loop(t, 6, cs + 4)
                        if js == 3:
                            sp.ran(6 * UP_TURNS)

            ffn(0)
            sp.to(START["nsa_kc"] + AHEAD)
            for k in range(KD):
                x_low("mix2_1", k)
            pool_nsa(pool, sp)
            for j in range(KD):
                sp.to(START["nsa_out"] + j + 1 + AHEAD)
                x_low("ffn2_1", j)
            ffn(1)


def _features(v, n):
    return np.ascontiguousarray(v).reshape(n, P).T


def _outer(w, tiles):
    k = w.shape[0] // P
    return w.reshape(k, P, tiles, P).transpose(2, 1, 0, 3).reshape(tiles, P, k * P)


def _token(w):
    return w.reshape(4, 2, P, 512).transpose(0, 2, 1, 3).reshape(4, P, CH)


def _rows(w):
    return w.reshape(-1, P, CH)


def _constants():
    i = np.arange(P)
    f = np.float32
    rope = np.zeros((P, P), f)
    for b in (0, 64):
        for d in range(8):
            rope[b + d + 8, b + d] = -1.0
            rope[b + d, b + d + 8] = 1.0
    half = 8
    inv = (500000.0 ** (-np.arange(half, dtype=f) * (2.0 / 16))).astype(f)
    ang = (np.arange(T, dtype=f)[:, None] * inv[None, :]).astype(f)
    cos, sin = np.ones((P, T), f), np.zeros((P, T), f)
    for b in (0, 64):
        for d in range(16):
            cos[b + d], sin[b + d] = np.cos(ang[:, d % 8]), np.sin(ang[:, d % 8])
    end = np.arange(16) * 16 + 31
    t = np.arange(T).reshape(TT, P).T
    ok = (end[None, None, :] <= t[:, :, None]) & (np.arange(16) < N_CMP)[None, None, :]
    parts = {
        "ident": np.eye(P), "ones": np.ones((P, P)), "neg_ones": -np.ones((P, P)),
        "neg_upto": -(i[:, None] >= i[None, :]).astype(f), "tri": (i[:, None] <= i[None, :]),
        "strict": (i[:, None] < i[None, :]), "block_ones": (i[:, None] // 64 == i[None, :] // 64),
        "rope": rope, "neg_causal": np.where(i[None, :] <= i[:, None], 0.0, MASKED),
        "cmp_neg": np.where(ok, 0.0, MASKED).reshape(P, 32), "cmp_01": ok.reshape(P, 32),
        "v_mask": ((i[:, None] % 32) // 16 == i[None, :] // 64) & (i[:, None] % 16 < N_CMP),
        "cos": cos, "sin": sin, "eps": np.tile(np.array([EPS1, EPS2]), (P, 1)),
    }
    return np.concatenate([np.asarray(parts[n], f) for n, _ in CONSTS], axis=1)


def kernel(**inputs):
    import concourse.bacc as bacc
    from concourse.bass_utils import run_bass_kernel_spmd

    a = {k: np.asarray(v) for k, v in inputs.items()}
    w_in = a["w_in"][0]
    z, xbc, dt, q, k, v = np.split(w_in, [512, 1280, 1288, 1800, 2312], axis=1)
    nsa = np.split(a["nsa_w_in_2"][0], list(np.cumsum([1024] + [256] * 6)), axis=1)
    order = [h for s in range(2) for i in range(4) for h in (8 * s + i, 8 * s + 4 + i)]
    heads = np.concatenate([np.arange(64 * h, 64 * h + 64) for h in order])
    pw1 = a["conv_w_pw1_2"][0]
    gate_then_a = np.concatenate([np.arange(P) + c for j in range(8) for c in (1024 + P * j, P * j)])

    def ff(w1, w2):
        up, down = _outer(w1, FF_TILES), _rows(w2)
        steps = [up[0:1]]
        for j in range(1, FF_TILES):
            steps += [up[j:j + 1], down[j - 1:j]]
        return np.concatenate(steps + [down[FF_TILES - 1:]])

    def ffn(w_up, w_down):
        up, down = _outer(w_up, 2 * UP_TILES), _rows(w_down)
        steps = [up[0:1], up[UP_TILES:UP_TILES + 1]]
        for j in range(1, UP_TILES):
            steps += [up[j:j + 1], up[UP_TILES + j:UP_TILES + j + 1], down[j - 1:j]]
        return np.concatenate(steps + [down[UP_TILES - 1:]])

    def cmp_w1(w):
        return w.reshape(2, 8, P, 2, P).transpose(3, 0, 2, 1, 4).reshape(4, P, CH)

    stream = [_outer(xbc, 6), _outer(q, 4), _outer(k, 4), _outer(z, 4), _token(v), _outer(a["w_xk"][0], 4),
              _token(a["w_xv"][0]), _outer(a["w_out"][0], 8), _outer(a["w_xq"][0], 4),
              _outer(a["w_xo"][0], 8).reshape(4, 2, P, 512).transpose(0, 2, 1, 3).reshape(4, P, CH),
              ff(a["w_ff1"][0], a["w_ff2"][0]), _outer(pw1[:, gate_then_a], 16), _outer(a["conv_w_pw2_2"][0], 8),
              ffn(a["ffn_w_up_2"][0], a["ffn_w_down_2"][0]),
              _outer(nsa[1], 2), _outer(nsa[2], 2), _outer(nsa[3], 2), _outer(nsa[5], 2), _outer(nsa[0][:, heads], 8),
              _token(np.concatenate([nsa[4], nsa[6]], axis=1)), cmp_w1(a["nsa_ck_w1_2"][0]), cmp_w1(a["nsa_cv_w1_2"][0]),
              _outer(a["nsa_w_out_2"][0][heads], 8), ffn(a["ffn_w_up_2"][1], a["ffn_w_down_2"][1])]
    stream = np.concatenate(stream)

    def taps(w, tiles):
        return w.reshape(w.shape[0], tiles, P).transpose(2, 1, 0).reshape(P, -1)

    def pairs(pe):
        return pe.reshape(16, P).T

    twice = lambda g: np.tile(g.reshape(64, 1), (2, 1))
    fconv = np.concatenate([np.concatenate([a["ffn_w_dw_2"][i], a["ffn_b_dw_2"][i][None]]) for i in range(2)])
    fconv = np.concatenate([taps(fconv[4 * i:4 * i + 4], UP_TILES) for i in range(2)], axis=1)
    columns = {
        "mix_g": _features(a["norm_mix_g"][0], 8), "conv_w": taps(a["conv_w"][0], 6), "conv_b": _features(a["conv_b"][0], 6),
        "d_skip": _features(np.repeat(a["d_skip"][0], 64), 4), "ssd_g": _features(a["ssd_norm_g"][0], 4),
        "sb_g": _features(a["sb_norm_g"][0], 4), "xa_g": _features(a["norm_xa_g"][0], 8),
        "mem_g": _features(a["norm_mem_g"][0], 8), "ff_g": _features(a["norm_ff_g"][0], 8),
        "final_g": _features(a["final_g"], 8), "mix2_g": _features(a["mix_norm_g_2"].reshape(-1), 16),
        "ffn2_g": _features(a["ffn_norm_g_2"].reshape(-1), 16),
        "b_pw1": _features(a["conv_b_pw1_2"][0][gate_then_a], 16),
        "w_dw": taps(a["conv_w_dw_2"][0], 8), "b_dw": _features(a["conv_b_dw_2"][0], 8),
        "ln_g": _features(a["conv_ln_g_2"][0], 8), "ln_b": _features(a["conv_ln_b_2"][0], 8),
        "b_pw2": _features(a["conv_b_pw2_2"][0], 8), "q_g": twice(a["nsa_q_norm_2"][0]), "kc_g": twice(a["nsa_kc_norm_2"][0]),
        "ks_g": twice(a["nsa_ks_norm_2"][0]), "kw_g": twice(a["nsa_kw_norm_2"][0]), "fconv": fconv,
        "pe_k": pairs(a["nsa_pe_k_2"][0]), "pe_v": pairs(a["nsa_pe_v_2"][0]),
        "dt_bias": np.tile(a["dt_bias"], (P, 1)), "a_log": np.tile(a["a_log"], (P, 1)),
    }
    vectors = np.concatenate([columns[n] for n, _ in VECTORS], axis=1)

    def by_tile(w):
        k = w.shape[0] // P
        return w.reshape(k, P, -1).transpose(1, 0, 2).reshape(P, -1)

    gate_cols = np.concatenate([nsa[7][:, 3 * h:3 * h + 3] for h in order], axis=1)
    smalls = np.concatenate([by_tile(dt), by_tile(gate_cols), by_tile(np.tile(a["nsa_ck_w2_2"][0], (1, 2))),
                             by_tile(np.tile(a["nsa_cv_w2_2"][0], (1, 2)))], axis=1)

    def feature_major(x):
        return x[0].T.reshape(KD, P, T).transpose(1, 0, 2)

    arrays = {"x_t": feature_major(a["x"]), "mem_t": feature_major(a["mem"]), "weights": stream, "vectors": vectors,
              "constants": _constants(), "small_weights": smalls}
    arrays = {n: np.ascontiguousarray(x) for n, x in arrays.items()}
    nc = bacc.Bacc("TRN2", target_bir_lowering=False, num_devices=1)
    args = [nc.dram_tensor(n, x.shape, F32, kind="ExternalInput").ap() for n, x in arrays.items()]
    args.append(nc.dram_tensor("result_t", (P, KD, T), F32, kind="ExternalOutput").ap())
    program(nc, *args)
    r = run_bass_kernel_spmd(nc, [arrays], core_ids=[0])
    got = r.results[0]["result_t"]
    return np.ascontiguousarray(got.transpose(1, 0, 2).reshape(D, T).T).reshape(1, T, D)
```

```python
from contextlib import ExitStack

import numpy as np

import concourse.bass as bass
from concourse import mybir

P = 128
T = 256
TT = T // P
D = 1024
KD = D // P
CH = 1024
RAW = 6
SPL = 4
AHEAD = 3
LO_DVE = 3 * P

SSD_TILES, SSD_HEADS, SB_HEADS = 4, 8, 8
XA_HEADS = 4
FF_TILES = 4096 // P
UP_TILES = 2816 // P
CONV_W = 31
PE_TAPS = 12
N_CMP = (T - 32) // 16 + 1
EPS1, EPS2 = 1e-5, 1e-6
MASKED = -float(2 ** 100)

F32 = mybir.dt.float32
F32R = mybir.dt.float32r
ALU = mybir.AluOpType
ACT = mybir.ActivationFunctionType
AX = mybir.AxisListType.X

LAYERS = [("xbc", 6), ("q", 4), ("k", 4), ("z", 4), ("v", 4), ("mem_k", 4), ("mem_v", 4), ("w_out", 8),
          ("xq", 4), ("xo", 4), ("ff", 2 * FF_TILES), ("pw1", 16), ("pw2", 8), ("ffn0", 3 * UP_TILES),
          ("nsa_kc", 2), ("nsa_vc", 2), ("nsa_ks", 2), ("nsa_kw", 2), ("nsa_q", 2),
          ("ck_w1", 4), ("cv_w1", 4), ("nsa_q2", 6), ("nsa_v", 4), ("nsa_out", 8), ("ffn1", 3 * UP_TILES)]
START = {}
_n = 0
for _name, _count in LAYERS:
    START[_name] = _n
    _n += _count
N_CHUNKS = _n

VECTORS = [("mix_g", 8), ("conv_w", 24), ("conv_b", 6), ("d_skip", 4), ("ssd_g", 4), ("sb_g", 4), ("xa_g", 8),
           ("mem_g", 8), ("ff_g", 8), ("final_g", 8), ("mix2_g", 16), ("ffn2_g", 16), ("b_pw1", 16),
           ("w_dw", 8 * CONV_W), ("b_dw", 8), ("ln_g", 8), ("ln_b", 8), ("b_pw2", 8),
           ("q_g", 1), ("kc_g", 1), ("ks_g", 1), ("kw_g", 1), ("fconv", 2 * UP_TILES * 4),
           ("pe_k", 16), ("pe_v", 16), ("dt_bias", 8), ("a_log", 8)]
VCOL = {}
_n = 0
for _name, _count in VECTORS:
    VCOL[_name] = _n
    _n += _count
N_VEC = _n

CONSTS = [("ident", 128), ("neg_ones", 128), ("neg_upto", 128), ("tri", 128), ("strict", 128),
          ("block_ones", 128), ("rope", 128), ("neg_causal", 128), ("cmp_neg", 32), ("cmp_01", 32),
          ("v_mask", 128), ("cos", T), ("sin", T)]
CCOL = {}
_n = 0
for _name, _count in CONSTS:
    CCOL[_name] = _n
    _n += _count
N_CONST = _n

SMALLS = [("w_dt", 8 * 8), ("w_gate", 8 * 48), ("ck_w2", 2 * P), ("cv_w2", 2 * P)]
SCOL = {}
_n = 0
for _name, _count in SMALLS:
    SCOL[_name] = _n
    _n += _count
N_SMALL = _n

NORMS = ["mix", "mem", "ssd", "sb", "xa", "ff", "final", "mix2_0", "ln", "ffn2_0", "mix2_1", "ffn2_1"]
NORM = {n: i for i, n in enumerate(NORMS)}
NORM_DIM = {"ssd": 512, "sb": 512}
SQ_COUNT = {"ssd": 4, "sb": 4}
SQ_BASE = {}
_n = 0
for _name in NORMS:
    SQ_BASE[_name] = _n
    _n += SQ_COUNT.get(_name, 8)
PREPS = ["mix", "xa", "ff", "mix2_0", "ffn2_0", "mix2_1", "ffn2_1"]
PREP = {n: i for i, n in enumerate(PREPS)}
GAIN = {"mix": "mix_g", "xa": "xa_g", "ff": "ff_g", "mix2_0": "mix2_g", "mix2_1": "mix2_g",
        "ffn2_0": "ffn2_g", "ffn2_1": "ffn2_g"}
GY_BASE = {"mem": 0, "mixer": 8, "pw2": 16}
Y_BASE = {"mem": 0, "mixer": 8, "xa": 16, "pw2": 20, "nsa": 28}
SUMMED = ["xa", "ff", "ffn2_0", "ffn2_1"]


def program(nc, x_d, mem_d, stream_d, vec_d, const_d, small_d, out_d):
    stack = ExitStack()
    with stack:
        def sb(name, shape, dt=F32, where=stack):
            return where.enter_context(nc.sbuf_tensor(name, shape, dt))

        sems = {}

        def sem(name):
            if name not in sems:
                sems[name] = stack.enter_context(nc.semaphore(name))
            return sems[name]

        X = sb("X", [P, KD, T])
        G = sb("G", [P, KD, T])
        GY = sb("GY", [P, KD, T])
        SQ = sb("SQ", [P, KD, T])
        XH, XL = sb("XH", [P, KD, T], F32R), sb("XL", [P, KD, T], F32R)
        YH, YL = sb("YH", [P, KD, T], F32R), sb("YL", [P, KD, T], F32R)
        WR = sb("WR", [P, RAW, CH])
        WH, WL = sb("WH", [P, SPL, CH], F32R), sb("WL", [P, SPL, CH], F32R)
        VEC = sb("VEC", [P, N_VEC])
        CON = sb("CON", [P, N_CONST])
        SML = sb("SML", [P, N_SMALL])
        LNV = sb("LNV", [P, T])
        RS = sb("RS", [P, T])
        RS2 = sb("RS2", [P, T])
        SSUM = sb("SSUM", [P, T])
        ONES = sb("ONES", [P, P])
        EPS = sb("EPS", [P, 2])
        RST = sb("RST", [P, TT])

        def group(specs):
            inner = ExitStack()
            got = {n: sb(n, s, dt, inner) for n, s, dt in specs}
            inner.close()
            return got

        A = group([("XP", [P, 6, T + 4], F32), ("CV", [P, 6, T], F32), ("XB", [P, 6, T], F32),
                   ("ZT", [P, 4, T], F32), ("QT", [P, 4, T], F32), ("KT", [P, 2, 4, T], F32),
                   ("V", [P, TT, 512], F32), ("MEM", [P, KD, T], F32),
                   ("MK", [P, 4, T], F32), ("MV", [P, TT, 512], F32),
                   ("DTR", [P, TT, 8], F32), ("DT", [P, TT, 8], F32), ("DTE", [P, TT, 8], F32), ("AN", [P, TT, 8], F32),
                   ("EAL", [P, 8], F32), ("ABC", [P, TT, 8, P], F32), ("MM0", [P, 8, P], F32),
                   ("BT", [P, P], F32),
                   ("CBM", [P, 4, P], F32), ("ACL", [P, 3, 8], F32), ("DS", [P, 8], F32), ("DSX", [P, 12], F32)])
        XP, CV, XB, ZT, QT, KT, V, MEM = (A[n] for n in ("XP", "CV", "XB", "ZT", "QT", "KT", "V", "MEM"))
        MK, MV, DTR, DT, DTE, AN, EAL = (A[n] for n in ("MK", "MV", "DTR", "DT", "DTE", "AN", "EAL"))
        ABC, BT = (A[n] for n in ("ABC", "BT"))
        CE = SQ[:, 4:6, :].rearrange("p k (h l) -> p (k h) l", h=2)
        MM = (A["MM0"], ABC[:, 1])
        SEG = (CV[:, 0:4, :].rearrange("p k (h l) -> p (k h) l", h=2),
               XP.rearrange("p k t -> p (k t)")[:, 0:1024].rearrange("p (h l) -> p h l", h=8))
        EA = ABC[:, 0]
        XC = MEM[:, 4:8, :].rearrange("p k t -> p (k t)").rearrange("p (a n) -> p a n", a=2)
        XCD = CV[:, 4:6, :].rearrange("p k t -> p (k t)")
        CBM, ACL, DS, DSX = (A[n] for n in ("CBM", "ACL", "DS", "DSX"))
        ST = SQ[:, 7]
        SBE = MEM[:, 0:4, :].rearrange("p k t -> p (k t)").rearrange("p (a n) -> p a n", a=2)
        SBP = MEM[:, 4:8, :].rearrange("p k t -> p (k t)").rearrange("p (a n) -> p a n", a=2)
        SBW = CV[:, 0:4, :].rearrange("p k t -> p (k t)").rearrange("p (a n) -> p a n", a=2)
        OS = QT

        B = group([("SG", [P, 2, T], F32), ("AT", [P, 2, T], F32), ("UP", [P, KD, T + CONV_W - 1], F32),
                   ("CX", [P, KD, T], F32), ("CB", [P, 2, T], F32), ("MU", [P, T], F32),
                   ("DG", [P, 2, PE_TAPS, P], F32)])
        SG, AT, UPAD, CX, CB, MU, DG = (B[n] for n in ("SG", "AT", "UP", "CX", "CB", "MU", "DG"))
        C = group([("GU", [P, 2, T], F32), ("UH", [P, 2, T], F32R), ("UL", [P, 2, T], F32R),
                   ("TA", [P, 2, T], F32), ("AP_", [P, 2, T + 2], F32), ("CA", [P, 2, T], F32),
                   ("SA", [P, 2, T], F32), ("VA", [P, 2, T], F32)])
        GU, UH, UL, TA, APD, CA, SA, VA = (C[n] for n in ("GU", "UH", "UL", "TA", "AP_", "CA", "SA", "VA"))
        E = group([("HS", [P, 6, 2, T], F32),
                   ("QN", [P, 8, T], F32), ("QP", [P, 8, T], F32), ("KN", [P, 2, T], F32), ("KZ", [P, 2, 4, T], F32),
                   ("KCV", [P, 4, T], F32), ("CBUF", [P, 2, 4, T], F32),
                   ("NV", [P, TT, 512 + 64], F32), ("GT", [P, TT, 48], F32),
                   ("ZF", [P, 2, 16, 60], F32),
                   ("H1T", [P, 2, T], F32), ("H1", [P, 2, 60], F32), ("KB", [P, 2, P], F32),
                   ("KC", [P, 60], F32), ("VB", [P, 2, P], F32), ("GQ8", [P, 2], F32),
                   ("CM", [P, 4, 32], F32),
                   ("RM", [P, 2, 6, 4], F32), ("RM3", [P, 2, 2, 3], F32),
                   ("IDR", [P, P], F32R), ("NCR", [P, P], F32R)])

        acc = stack.enter_context(nc.psum_tensor("acc", [P, 2, 512], F32))
        big = stack.enter_context(nc.psum_tensor("big", [P, 4, 512], F32))
        mis = stack.enter_context(nc.psum_tensor("mis", [P, 2, 512], F32))

        raw_loaded = [sem(f"raw_loaded{i}") for i in range(RAW)]
        w_high, w_low_dve, w_low_pool, w_used = sem("w_high"), sem("w_low_dve"), sem("w_low_pool"), sem("w_used")
        acc_free = sem("acc_free")
        gx_ready, xh_ready, xl_ready = sem("gx_ready"), sem("xh_ready"), sem("xl_ready")
        gy_ready, yh_ready, yl_ready = sem("gy_ready"), sem("yh_ready"), sem("yl_ready")
        sq_ready, nps_ready, rstd_ready = sem("sq_ready"), sem("nps_ready"), sem("rstd_ready")
        dve_chain, act_chain, pool_chain = sem("dve_chain"), sem("act_chain"), sem("pool_chain")

        def vec(name, i=0):
            return VEC[:, VCOL[name] + i:VCOL[name] + i + 1]

        def con(name, a=0, b=None):
            w = dict(CONSTS)[name]
            return CON[:, CCOL[name] + a:CCOL[name] + (w if b is None else b)]

        def small(name):
            return SML[:, SCOL[name]:SCOL[name] + dict(SMALLS)[name]]

        last_chunk = N_CHUNKS
        TILE = {}
        n = 0
        for name, count in [("xbc", 6), ("q", 4), ("k", 4), ("z", 4), ("v", 2), ("mem_k", 4), ("mem_v", 2),
                            ("w_out", 8), ("xq", 4), ("xo", 8), ("ff", FF_TILES), ("pw1", 16), ("pw2", 8),
                            ("ffn0", 2 * UP_TILES), ("nsa_kc", 2), ("nsa_vc", 2), ("nsa_ks", 2), ("nsa_kw", 2),
                            ("nsa_q", 2), ("ck_w1", 1), ("cv_w1", 1), ("nsa_q2", 6), ("nsa_v", 2), ("nsa_out", 8), ("ffn1", 2 * UP_TILES)]:
            TILE[name] = n
            n += count

        def ff_up(j):
            return START["ff"] + (0 if j == 0 else 2 * j - 1)

        def ff_down(j):
            return START["ff"] + (2 * j + 2 if j < FF_TILES - 1 else 2 * FF_TILES - 1)

        class Chain:

            def __init__(self, eng, sem_):
                self.eng, self.sem, self.base, self.k, self.turn, self.per = eng, sem_, 0, 0, None, 0

            def add(self, ins):
                self.k += 1
                ins.then_inc(self.sem, 1)
                return self.value()

            def value(self):
                v = self.base + self.k
                return v if self.turn is None else self.turn * self.per + v

            def link(self, ins):
                self.eng.wait_ge(self.sem, self.add(ins))

            def loop(self, turns, per):
                self.base += self.k
                self.k, self.per = 0, per
                with self.eng.Fori(0, turns) as t:
                    self.turn = t
                    yield t
                assert self.k == per, (self.k, per)
                self.base += turns * per
                self.k, self.turn = 0, None

        class Splitter:

            def __init__(self, one):
                self.one, self.issued = one, 0

            def to(self, n):
                while self.issued < min(n, last_chunk):
                    self.one(0, 0, self.issued)
                    self.issued += 1

            def in_loop(self, turn, per_turn, cs):
                self.one(turn, per_turn, cs)

            def ran(self, chunks):
                self.issued += chunks

        def plus(turn, per, n):
            return n if isinstance(turn, int) else turn * per + n

        XSTAT = DSX[:, :].rearrange("p (s a t) -> p s a t", s=3, a=2)

        def YS(p):
            return ZT[:, p]

        UP_STEPS = 4
        UP_TURNS = (UP_TILES - 4) // UP_STEPS

        def turns_of_up(eng, chain=None, per=0):
            yield 0, 1
            if chain is None:
                with eng.Fori(0, UP_TURNS) as t:
                    for u in range(UP_STEPS):
                        yield t, 2 + u
            else:
                for t in chain.loop(UP_TURNS, per):
                    for u in range(UP_STEPS):
                        yield t, 2 + u
            for j in range(2 + UP_STEPS * UP_TURNS, UP_TILES):
                yield 0, j

        def SEG_P(h):
            return XB[:, 2 * (h % 2):2 * (h % 2) + 2, :]

        def XO(h):
            return (big[:, 3, 0:T], mis[:, 1, 0:T])[h % 2]

        def XPT(h):
            return CV[:, 2 * (h % 2):2 * (h % 2) + 2, :]

        HS, QN, QP, KN, KZ, KCV, CBUF, NV, GT = (E[n] for n in ("HS", "QN", "QP", "KN", "KZ", "KCV", "CBUF", "NV", "GT"))
        ZF, H1T, H1, KB, KC, VB, GQ8 = (E[n] for n in ("ZF", "H1T", "H1", "KB", "KC", "VB", "GQ8"))
        ZH, ZL = (y.rearrange("p k t -> p (k t)")[:, 0:1920].rearrange("p (s b n) -> p s b n", s=2, b=16)
                  for y in (YH, YL))
        CM, RM, RM3, IDR, NCR = (E[n] for n in ("CM", "RM", "RM3", "IDR", "NCR"))
        PCT = H1T
        SC, PC = (GY[:, i:i + 2, :].rearrange("p k (a n) -> p (k a) n", n=16) for i in (0, 2))
        HREP = GY[:, 4:6, :].rearrange("p s (h m) -> p s h m", h=2)
        OT = GY[:, 6:8, :].rearrange("p s (t f) -> p s t f", t=2)
        HE = GY[:, 6:8, :]
        OB = KCV[:, 0:2, :].rearrange("p s (b t f) -> p s b t f", b=2, t=2)
        QR, RH, SH, LH, T1, T2 = (HS[:, i] for i in range(6))
        PP = CBUF.rearrange("p a g t -> p (a g t)")[:, 0:1536].rearrange("p (s b n) -> p s b n", s=2, b=2)
        PT = HS.rearrange("p a b t -> p (a b t)")[:, 0:1536].rearrange("p (s b n) -> p s b n", s=2, b=2)
        NORMED = 12
        N_HEADS2 = 16

        def normed_chunk(n):
            return START["nsa_ks"] + n if n < 6 else START["nsa_q2"] + n - 6

        def normed_tile(n):
            return TILE["nsa_ks"] + n if n < 6 else TILE["nsa_q2"] + n - 6

        def pe_nsa(pe, tile, token_major, three, rstd_columns, chunk_ready, acc_ready):
            def head_sums(n):
                pe.wait_ge(sem("hsq_done"), n + 1)
                if n >= 1:
                    pe.wait_ge(sem("hrs_done"), n)
                w = T if n < NORMED else 60
                pe.matmul(mis[:, 0, 0:w], con("block_ones"), SH[:, n % 2, 0:w], start=True, stop=True,
                          skip_group_check=True).then_inc(sem("hn_ps"), 1)

            def rotate(n):
                pe.wait_ge(sem("hqn_done"), n + 1)
                if n >= 1:
                    pe.wait_ge(sem("hrot_read"), n)
                x = KN[:, n % 2] if n < 4 else QN[:, n - 4]
                pe.matmul(mis[:, 1, 0:T], con("rope"), x, start=True, stop=True,
                          skip_group_check=True).then_inc(sem("rope_ps"), 1)

            for i in range(4):
                tile(START["nsa_kc"] + i, TILE["nsa_kc"] + i, XH, XL, base=(xl_ready, 8 * PREP["mix2_1"]) if i == 0 else None,
                     norm="mix2_1" if i == 0 else None)
            rstd_columns(big[:, 2, 0:2], "mix2_1")
            for tt in range(TT):
                for k in range(KD):
                    ins = pe.matmul(big[:, 3, 64 * tt:64 * tt + 48], G[:, k, tt * P:tt * P + P],
                                    small("w_gate")[:, k * 48:k * 48 + 48], start=k == 0, stop=k == KD - 1,
                                    skip_group_check=True)
            ins.then_inc(sem("gate_ps"), 1)

            def compress():
                for kv in range(2):
                    pe.wait_ge(sem("zl_done"), kv + 1)
                    t = TILE["ck_w1"] + kv
                    acc_ready(t)
                    for i in range(4):
                        c = START["ck_w1"] + 4 * kv + i
                        chunk_ready(c)
                        for b in range(4):
                            kb = 4 * i + b
                            o = acc[0:60, t % 2, 0:T]
                            wh, wl = (w[:, c % SPL, b * T:b * T + T] for w in (WH, WL))
                            pe.matmul(o, ZH[:, kv, kb], wh, start=kb == 0, stop=False, skip_group_check=True)
                            pe.matmul(o, ZH[:, kv, kb], wl, start=False, stop=False, skip_group_check=True)
                            ins = pe.matmul(o, ZL[:, kv, kb], wh, start=False, stop=kb == 15, skip_group_check=True)
                        ins.then_inc(w_used, 1)

            def turn_hidden():
                pe.wait_ge(sem("h1t_done"), 2)
                for i in range(4):
                    ins = pe.transpose(big[:, 0, P * i:P * i + 60], H1T[0:60, i // 2, P * (i % 2):P * (i % 2) + P],
                                       con("ident")[0:60, 0:60])
                ins.then_inc(sem("h1_ps"), 1)

            def compress_out():
                pe.wait_ge(sem("hrep_done"), 1)
                for ht in range(2):
                    ins = pe.matmul(big[:, 2, 0:60], small("ck_w2")[:, P * ht:P * ht + P], H1[:, ht, :], start=ht == 0,
                                    stop=ht == 1, skip_group_check=True)
                ins.then_inc(sem("kc_ps"), 1)
                for s_ in range(2):
                    for ht in range(2):
                        ins = pe.matmul(big[:, 1, P * s_:P * s_ + P], HREP[:, s_, ht, :],
                                        small("cv_w2")[:, P * ht:P * ht + P], start=ht == 0, stop=ht == 1,
                                        skip_group_check=True)
                ins.then_inc(sem("vb_ps"), 1)

            def cmp_scores():
                pe.wait_ge(sem("kb_done"), 4)
                pe.wait_ge(sem("vb_done"), 1)
                pe.wait_ge(sem("hqn_done"), NORMED)
                for tt in range(TT):
                    for j in range(8):
                        ins = pe.matmul(big[:, tt, 32 * j:32 * j + P], QN[:, j, tt * P:tt * P + P], KB[:, j // 4, :],
                                        start=True, stop=True, skip_group_check=True)
                ins.then_inc(sem("sc_ps"), 1)

            for n in range(NORMED + 2):
                if n < NORMED:
                    tile(normed_chunk(n), normed_tile(n), XH, XL)
                if 1 <= n <= NORMED:
                    head_sums(n - 1)
                if n >= 2:
                    rotate(n - 2)
                if n == 5:
                    compress()
                if n == 8:
                    turn_hidden()
                if n == 9:
                    compress_out()
            head_sums(NORMED)
            token_major(START["nsa_v"], TILE["nsa_v"], XH, XL, halfway=cmp_scores)
            pe.wait_ge(sem("sc_in"), 1)
            pe.wait_ge(sem("consts_rounded"), 1)
            pe.wait_ge(sem("hp_done"), 8)
            pe.wait_ge(sem("kz_done"), 8)

            def scores(hh):
                j, e = hh // 2, hh % 2
                if hh >= 2:
                    pe.wait_ge(sem("at_exp"), hh - 1)
                for br in range(2):
                    o, k = big[:, 2 * e + br, :], KZ[:, e, 2 * br + j // 4, :]
                    pe.matmul(o[:, 0:P], QP[:, j, 0:P], k[:, 0:P], start=True, stop=True, skip_group_check=True)
                    pe.matmul(o[:, P:P + T], QP[:, j, P:T], k, start=False, stop=True, skip_group_check=True)
                    ins = pe.matmul(o[:, 0:384].rearrange("p (c n) -> p c n", c=3)[:, 0:3:2, :], IDR[:, :],
                                    NCR[:, :].unsqueeze(1).broadcast_to([P, 2, P]), start=False, stop=True,
                                    skip_group_check=True)
                ins.then_inc(sem("at_s"), 1)

            def turn(hh):
                pe.wait_ge(sem("at_exp"), hh + 1)
                if hh >= 1:
                    pe.wait_ge(sem("at_pt_act"), hh)
                    pe.wait_ge(sem("at_pt_dve"), hh)
                for br in range(2):
                    for b in range(3):
                        ins = pe.transpose(mis[:, br, b * P:b * P + P], PP[:, hh % 2, br, b * P:b * P + P], con("ident"))
                ins.then_inc(sem("at_t"), 1)

            def outputs(hh):
                g = 2 * (hh // 8) + hh % 2
                pe.wait_ge(sem("at_pt_act"), hh + 1)
                pe.wait_ge(sem("at_pt_dve"), hh + 1)
                if hh >= 1:
                    pe.wait_ge(sem("at_scaled"), hh)
                for br in range(2):
                    for tt in range(TT):
                        for m in range(tt + 1):
                            b = tt + m
                            ins = pe.matmul(acc[:, 0, (2 * br + tt) * P:(2 * br + tt) * P + P],
                                            PT[:, hh % 2, br, b * P:b * P + P],
                                            NV[:, m, 128 * g + 64 * br:128 * g + 64 * br + P], start=m == 0, stop=m == tt,
                                            skip_group_check=True)
                ins.then_inc(sem("at_o"), 1)

            def pair(j):
                o, q = acc[:, 1, 0:T], slice(32 * (j % 4), 32 * (j % 4) + 32)
                if j == 0:
                    pe.wait_ge(sem("pct_done"), 1)
                else:
                    pe.wait_ge(yl_ready, Y_BASE["nsa"] + j)
                pe.matmul(o, VB[q, j // 4, :], PCT[q, j // 4, :], start=True, stop=False, skip_group_check=True)
                pe.wait_ge(sem("at_ot"), 2 * j + 2)
                for tt in range(TT):
                    ins = pe.matmul(o[:, tt * P:tt * P + P], OT[:, j % 2, tt, :], con("ident"), start=False, stop=tt == 1,
                                    skip_group_check=True)
                ins.then_inc(sem("at_pair"), 1)

            def turn_compressed():
                pe.wait_ge(acc_free, TILE["nsa_out"])
                pe.wait_ge(sem("pc_done"), 1)
                for s_ in range(2):
                    for tt in range(TT):
                        ins = pe.transpose(acc[:, 1, s_ * T + tt * P:s_ * T + tt * P + P],
                                           PC.rearrange("p (t j) n -> p t (j n)", t=2)[:, tt, s_ * P:s_ * P + P],
                                           con("ident"))
                ins.then_inc(sem("pct_ps"), 1)

            for i in range(N_HEADS2 + 3):
                if i < N_HEADS2:
                    scores(i)
                if 1 <= i <= N_HEADS2:
                    turn(i - 1)
                if i == 1:
                    turn_compressed()
                if 2 <= i <= N_HEADS2 + 1:
                    outputs(i - 2)
                if i >= 4 and i % 2 == 0:
                    pair((i - 4) // 2)

        def act_nsa(act, ch, sp, rstd):
            link = ch.link

            def square(n, ready):
                act.wait_ge(acc_free, ready)
                act.activation(SH[:, n % 2], QR[:, n % 2], ACT.Square).then_inc(sem("hsq_done"), 1)

            def head_rstd(n):
                act.wait_ge(sem("hn_ps"), n + 1)
                w = T if n < NORMED else 60
                link(act.activation(LH[:, n % 2, 0:w], mis[:, 0, 0:w], ACT.Ln, bias=EPS[:, 1:2], scale=1.0 / 64))
                if n >= 2:
                    act.wait_ge(sem("hqn_done"), n - 1)
                act.activation(RH[:, n % 2, 0:w], LH[:, n % 2, 0:w], ACT.Exp, scale=-0.5).then_inc(sem("hrs_done"), 1)

            act.preload_act_table_set("natural_log_exp_and_others")
            sp.to(START["nsa_kc"] + 1 + AHEAD)
            rstd("mix2_1", RS)
            for kv in range(2):
                for i in range(2):
                    sp.to(START["nsa_kc"] + 2 * kv + i + 1 + AHEAD)
                act.wait_ge(acc_free, TILE["nsa_kc"] + 2 * kv + 2)
                for gp in range(2):
                    src = KCV[64 * gp:64 * gp + 64, 2 * kv:2 * kv + 2, :]
                    dst = CBUF[:, kv].rearrange("p (b a) t -> p b a t", a=2)[:, :, gp, :]
                    act.dma_start(dst[0:64], src).then_inc(sem(f"cbuf_loaded{kv}"), 16)
                    act.dma_start(dst[64:128, :, 0:T - 1], src[:, :, 1:T]).then_inc(sem(f"cbuf_loaded{kv}"), 16)

            def z_high(kv):
                act.wait_ge(sem("zf_done"), kv + 1)
                act.activation(ZH[:, kv], ZF[:, kv], ACT.Copy).then_inc(sem("zh_done"), 1)

            for n in range(NORMED + 1):
                if n < NORMED:
                    sp.to(normed_chunk(n) + 1 + AHEAD)
                    square(n, normed_tile(n) + 1)
                if n >= 1:
                    head_rstd(n - 1)
                if n == 3:
                    z_high(0)
                if n == 4:
                    z_high(1)
                    act.wait_ge(sem("gate_done2"), 1)
                    act.activation(GT[:, :, :], GT[:, :, :], ACT.Exp, scale=-1.0).then_inc(sem("gate_exp"), 1)
                if n == 5:
                    sp.to(START["nsa_q2"] + AHEAD)
                    for kv in range(2):
                        act.wait_ge(acc_free, TILE["ck_w1"] + kv + 1)
                        act.activation(HE[0:60, kv], H1T[0:60, kv], ACT.Exp, scale=-1.0).then_inc(sem("h1_exp"), 1)
            act.wait_ge(sem("kc_copied"), 1)
            act.activation(SH[:, NORMED % 2, 0:60], KC[:, :], ACT.Square).then_inc(sem("hsq_done"), 1)
            head_rstd(NORMED)
            sp.to(START["nsa_v"] + 2 + 4)
            act.wait_ge(sem("sc_in"), 1)
            act.activation(SC[:, :, 0:N_CMP], SC[:, :, 0:N_CMP], ACT.Exp).then_inc(sem("sc_exp"), 1)
            sp.to(START["nsa_out"] + AHEAD)
            for i in range(N_HEADS2 + 3):
                if 1 <= i <= N_HEADS2:
                    act.wait_ge(sem("at_t"), i)
                    if i >= 3:
                        act.wait_ge(sem("at_o"), i - 2)
                    act.activation(PT[:, (i - 1) % 2, 0, :], mis[:, 0, 0:384], ACT.Copy).then_inc(sem("at_pt_act"), 1)
                if i < N_HEADS2:
                    act.wait_ge(sem("at_nm"), i + 1)
                    if i >= 2:
                        act.wait_ge(sem("at_t"), i - 1)
                    for br in range(2):
                        for tt, (a, b) in enumerate(((0, P), (P, P + T))):
                            ins = act.activation(PP[:, i % 2, br, a:b], big[:, 2 * (i % 2) + br, a:b], ACT.Exp,
                                                 bias=RM3[:, i % 2, br, tt:tt + 1],
                                                 accum_out=RM[:, i % 2, 0, 2 * br + tt:2 * br + tt + 1])
                            if (br, tt) != (1, 1):
                                ch.add(ins)
                    ins.then_inc(sem("at_exp"), 1)
                if i == 1:
                    act.wait_ge(sem("pct_ps"), 1)
                    act.activation(PCT.rearrange("p s t -> p (s t)"), acc[:, 1, :], ACT.Copy).then_inc(sem("pct_done"), 1)
                if i >= 4 and i % 2 == 0:
                    j = (i - 4) // 2
                    act.wait_ge(sem("at_pair"), j + 1)
                    act.activation(YH[:, j], acc[:, 1, 0:T], ACT.Copy).then_inc(yh_ready, 1)

        def dve_nsa(dve, ch, sp, used, scaled, rstd_done):
            link = ch.link
            link(dve.tensor_scalar(GQ8[:, 0:1], vec("q_g"), 0.125, None, ALU.mult))
            link(dve.tensor_copy(IDR[:, :], con("ident")))
            dve.tensor_copy(NCR[:, :], con("neg_causal")).then_inc(sem("consts_rounded"), 1)
            rstd_done("mix2_1")
            for i in range(4):
                used(START["nsa_kc"] + i)
                scaled(KCV[:, i], TILE["nsa_kc"] + i, wait=False)
                sp.to(START["nsa_kc"] + i + 1 + AHEAD)

            def normed(n):
                dve.wait_ge(sem("hrs_done"), n + 1)
                x = KN[:, n % 2] if n < 4 else QN[:, n - 4]
                g = vec("ks_g") if n < 2 else vec("kw_g") if n < 4 else GQ8[:, 0:1]
                dve.scalar_tensor_tensor(x, QR[:, n % 2], g, RH[:, n % 2], ALU.mult, ALU.mult).then_inc(sem("hqn_done"), 1)

            def rotated(n):
                x = KN[:, n % 2] if n < 4 else QN[:, n - 4]
                if n >= 6:
                    dve.wait_ge(sem("hp_done"), n - 5)
                dve.wait_ge(sem("hqn_done"), n + 1)
                link(dve.tensor_tensor(T1[:, n % 2], x, con("cos"), ALU.mult))
                dve.wait_ge(sem("rope_ps"), n + 1)
                dve.tensor_tensor(T2[:, n % 2], mis[:, 1, 0:T], con("sin"), ALU.mult).then_inc(sem("hrot_read"), 1)
                if n < 4:
                    dve.wait_ge(sem("hrot_read"), n + 1)
                    dve.wait_ge(sem("kz_zero"), 1)
                    for e in range(2):
                        h = slice(64 * e, 64 * e + 64)
                        dve.tensor_tensor(KZ[h, e, n], T1[h, n % 2], T2[h, n % 2], ALU.add).then_inc(sem("kz_done"), 1)

            def positions(kv):
                dve.wait_ge(sem(f"cbuf_loaded{kv}"), 64)
                pe_ = "pe_k" if kv == 0 else "pe_v"
                for a in range(2):
                    x = CBUF[:, kv, :, 16 * a:16 * a + 240].rearrange("p g (n b two) -> p b g n two", b=8, two=2)[:, :, :, :, 0]
                    v = VEC[:, VCOL[pe_] + 8 * a:VCOL[pe_] + 8 * a + 8].unsqueeze(2).unsqueeze(2).broadcast_to([P, 8, 4, N_CMP])
                    last = ch.add(dve.tensor_tensor(ZF[:, kv, 8 * a:8 * a + 8, :].rearrange("p b (g n) -> p b g n", g=4),
                                                    x, v, ALU.add))
                dve.wait_ge(dve_chain, last)
                dve.sem_inc(sem("zf_done"), 1)

            def z_low(kv):
                dve.wait_ge(sem("zh_done"), kv + 1)
                dve.tensor_tensor(ZL[:, kv], ZF[:, kv], ZH[:, kv].bitcast(F32), ALU.subtract).then_inc(sem("zl_done"), 1)

            def gate_inputs():
                dve.wait_ge(sem("rst_ps"), 2)
                link(dve.tensor_copy(RST[:, :], big[:, 2, 0:2]))
                dve.wait_ge(sem("gate_ps"), 1)
                for tt in range(TT):
                    last = ch.add(dve.tensor_scalar(GT[:, tt], big[:, 3, 64 * tt:64 * tt + 48], RST[:, tt:tt + 1], None,
                                                    ALU.mult))
                dve.wait_ge(dve_chain, last)
                dve.sem_inc(sem("gate_done2"), 1)
                link(dve.memset(NV[:, :, 512:576], 0.0))
                link(dve.memset(KB[:, :, :], 0.0))
                link(dve.memset(HREP[:, :, :, :], 0.0))
                link(dve.memset(PC[:, :, :], 0.0))

            def hidden_tiles():
                for kv in range(2):
                    c, t = START["ck_w1"] + 4 * kv, TILE["ck_w1"] + kv
                    sp.to(c + 4 + AHEAD)
                    used(c + 3)
                    dve.tensor_copy(H1T[0:60, kv], acc[0:60, t % 2, 0:T]).then_inc(acc_free, 1)

            def hidden_turned():
                dve.wait_ge(sem("h1_ps"), 1)
                h1 = big[:, 0, :].rearrange("p (v t n) -> p v t n", v=2, t=2)
                ch.add(dve.tensor_copy(H1[:, :, :], h1[:, 0, :, 0:60]))
                for s_ in range(2):
                    for ht in range(2):
                        o = HREP[:, s_, ht, :].rearrange("p (i e n) -> p i e n", i=4, e=2)[:, :, :, 0:N_CMP]
                        x = h1[:, 1, ht, 30 * s_:30 * s_ + 30].rearrange("p (e n) -> p e n", e=2).unsqueeze(1).broadcast_to(
                            [P, 4, 2, N_CMP])
                        last = ch.add(dve.tensor_copy(o, x))
                dve.wait_ge(dve_chain, last)
                dve.sem_inc(sem("hrep_done"), 1)

            def compressed():
                dve.wait_ge(sem("kc_ps"), 1)
                dve.tensor_copy(KC[:, :], big[:, 2, 0:60]).then_inc(sem("kc_copied"), 1)
                dve.wait_ge(sem("vb_ps"), 1)
                dve.tensor_tensor(VB[:, :, :], big[:, 1, 0:T].rearrange("p (s d) -> p s d", s=2),
                                  con("v_mask").unsqueeze(1).broadcast_to([P, 2, P]), ALU.mult).then_inc(sem("vb_done"), 1)

            for n in range(NORMED + 2):
                if n < NORMED:
                    used(normed_chunk(n))
                    if n >= 2:
                        dve.wait_ge(sem("hqn_done"), n - 1)
                        dve.wait_ge(sem("hsq_done"), n - 1)
                    scaled(QR[:, n % 2], normed_tile(n), wait=False)
                    sp.to(normed_chunk(n) + 1 + AHEAD)
                if n >= 2:
                    rotated(n - 2)
                if 1 <= n <= NORMED:
                    normed(n - 1)
                if n == 1:
                    gate_inputs()
                if n == 2:
                    positions(0)
                if n == 3:
                    positions(1)
                if n == 4:
                    z_low(0)
                    dve.wait_ge(sem("gate_exp"), 1)
                    link(dve.tensor_scalar(GT[:, :, :], GT[:, :, :], 1.0, None, ALU.add))
                    dve.reciprocal(GT[:, :, :], GT[:, :, :]).then_inc(sem("gates"), 1)
                if n == 5:
                    z_low(1)
                    hidden_tiles()
                if 6 <= n <= 7:
                    kv = n - 6
                    he = HE[0:60, kv]
                    dve.wait_ge(sem("h1_exp"), kv + 1)
                    link(dve.tensor_scalar(he, he, 1.0, None, ALU.add))
                    link(dve.reciprocal(he, he))
                    dve.tensor_tensor(H1T[0:60, kv], H1T[0:60, kv], he, ALU.mult).then_inc(sem("h1t_done"), 1)
                if n == 8:
                    hidden_turned()
                if n == 9:
                    compressed()
            dve.wait_ge(sem("hrs_done"), NORMED + 1)
            dve.wait_ge(sem("kc_copied"), 1)
            for s_ in range(2):
                for e in range(2):
                    h, g = slice(64 * e, 64 * e + 64), 2 * s_ + e
                    dve.scalar_tensor_tensor(KB[h, s_, 16 * e:16 * e + N_CMP], KC[h, 15 * g:15 * g + 15], vec("kc_g")[h],
                                             RH[h, NORMED % 2, 15 * g:15 * g + 15], ALU.mult,
                                             ALU.mult).then_inc(sem("kb_done"), 1)
            sp.to(START["nsa_v"] + 2 + 4)
            dve.wait_ge(sem("sc_ps"), 1)
            s_all = SC[:, :, 0:N_CMP]
            by_tile = s_all.rearrange("p (t h) n -> p t h n", t=2)
            mask = lambda name: con(name).rearrange("p (t n) -> p t n", t=2)[:, :, 0:N_CMP].unsqueeze(2).broadcast_to(
                [P, 2, 16, N_CMP])
            link(dve.tensor_tensor(by_tile, big[:, 0:2, 0:T].rearrange("p t (h n) -> p t h n", h=16)[:, :, :, 0:N_CMP],
                                   mask("cmp_neg"), ALU.add))
            link(dve.tensor_reduce(CM[:, 0, :], s_all, AX, ALU.max))
            link(dve.tensor_tensor(s_all, s_all, CM[:, 0, :].unsqueeze(2).broadcast_to([P, 32, N_CMP]), ALU.subtract))
            dve.sem_inc(sem("sc_in"), 1)
            def compressed_softmax():
                dve.wait_ge(sem("sc_exp"), 1)
                link(dve.tensor_tensor(by_tile, by_tile, mask("cmp_01"), ALU.mult))
                link(dve.tensor_reduce(CM[:, 1, :], s_all, AX, ALU.add))
                link(dve.tensor_scalar(CM[:, 1, :], CM[:, 1, :], 1e-30, None, ALU.max))
                link(dve.reciprocal(CM[:, 2, :], CM[:, 1, :]))
                dve.wait_ge(sem("gates"), 1)
                gate = GT.rearrange("p t (h x) -> p (t h) x", x=3)[:, :, 0]
                link(dve.tensor_tensor(CM[:, 3, :], CM[:, 2, :], gate, ALU.mult))
                dve.tensor_tensor(PC[:, :, 0:N_CMP], s_all, CM[:, 3, :].unsqueeze(2).broadcast_to([P, 32, N_CMP]),
                                  ALU.mult).then_inc(sem("pc_done"), 1)

            sp.to(START["nsa_out"] + AHEAD)
            used(START["nsa_v"] + 3)
            for tt in range(TT):
                dve.tensor_scalar(NV[:, tt, 0:512], acc[:, (TILE["nsa_v"] + tt) % 2, :], RST[:, tt:tt + 1], None,
                                  ALU.mult).then_inc(acc_free, 1)

            for i in range(N_HEADS2 + 3):
                if i < N_HEADS2:
                    dve.wait_ge(sem("at_s"), i + 1)
                    m = RM3[:, i % 2]
                    if i >= 2:
                        dve.wait_ge(sem("at_exp"), i - 1)
                    link(dve.tensor_reduce(m.rearrange("p b c -> p (b c)"),
                                           big[:, 2 * (i % 2):2 * (i % 2) + 2, 0:384].rearrange("p b (c n) -> p b c n", c=3),
                                           AX, ALU.max, negate=True))
                    dve.tensor_tensor(m[:, :, 1:2], m[:, :, 1:2], m[:, :, 2:3], ALU.min).then_inc(sem("at_nm"), 1)
                if i == 0:
                    compressed_softmax()
                if 1 <= i <= N_HEADS2:
                    hh = i - 1
                    r = RM[:, hh % 2]
                    dve.wait_ge(sem("at_exp"), i)
                    inverse = ch.add(dve.reciprocal(r[:, 1, :], r[:, 0, :]))
                    dve.wait_ge(sem("at_t"), i)
                    if i >= 3:
                        dve.wait_ge(sem("at_o"), i - 2)
                    dve.tensor_copy(PT[:, hh % 2, 1, :], mis[:, 1, 0:384]).then_inc(sem("at_pt_dve"), 1)
                    dve.wait_ge(dve_chain, inverse)
                    scales = ch.add(dve.tensor_tensor(r[:, 2, :].rearrange("p (b t) -> p b t", b=2),
                                                      r[:, 1, :].rearrange("p (b t) -> p b t", b=2),
                                                      GT[:, :, 3 * hh + 1:3 * hh + 3].rearrange("p t b -> p b t"), ALU.mult))
                if 2 <= i <= N_HEADS2 + 1:
                    hh = i - 2
                    ob = OB[:, hh % 2]
                    dve.wait_ge(sem("at_o"), hh + 1)
                    if i > N_HEADS2:
                        dve.wait_ge(dve_chain, scales)
                    dve.tensor_tensor(ob.rearrange("p b t f -> p (b t) f"),
                                      acc[:, 0, :].rearrange("p (a f) -> p a f", a=4)[:, :, 0:64],
                                      RM[:, hh % 2, 2, :].unsqueeze(2).broadcast_to([P, 4, 64]),
                                      ALU.mult).then_inc(sem("at_scaled"), 1)
                if i >= 4 and i % 2 == 0:
                    j = (i - 4) // 2
                    dve.wait_ge(yh_ready, Y_BASE["nsa"] + j + 1)
                    dve.tensor_tensor(YL[:, j], acc[:, 1, 0:T], YH[:, j].bitcast(F32), ALU.subtract).then_inc(yl_ready, 1)
                if 2 <= i <= N_HEADS2 + 1:
                    e, j = hh % 2, hh // 2
                    if j >= 2:
                        dve.wait_ge(sem("at_pair"), j - 1)
                    dve.wait_ge(sem("at_scaled"), hh + 1)
                    dve.tensor_tensor(OT[:, j % 2, :, 64 * e:64 * e + 64], ob[:, 0], ob[:, 1],
                                      ALU.add).then_inc(sem("at_ot"), 1)

        def pool_nsa(pool, sp):
            pool.memset(KZ[:, :, :, :], 0.0).then_inc(sem("kz_zero"), 1)
            sp.to(START["nsa_q2"] + AHEAD)
            for n in range(4, NORMED):
                sp.to(normed_chunk(n) + 1 + AHEAD)
                pool.wait_ge(sem("hrot_read"), n + 1)
                pool.tensor_tensor(QP[:, n - 4], T1[:, n % 2], T2[:, n % 2], ALU.add).then_inc(sem("hp_done"), 1)
            sp.to(START["nsa_out"] + AHEAD)

        block = stack.enter_context(nc.Block())

        @block.sync
        def _(sp):
            sp.dma_start(VEC[:], vec_d).then_inc(sem("vec_loaded"), 16)
            for i in range(4):
                if i == 1:
                    sp.dma_start(WR[:, 0], stream_d[0]).then_inc(raw_loaded[0], 16)
                sp.dma_start(X[:, 2 * i:2 * i + 2, :], x_d[:, 2 * i:2 * i + 2, :]).then_inc(sem(f"x_loaded{i}"), 16)
            for c in range(1, RAW):
                sp.dma_start(WR[:, c], stream_d[c]).then_inc(raw_loaded[c], 16)
                if c == 2:
                    sp.dma_start(MEM[:], mem_d).then_inc(sem("mem_loaded"), 16)
                if c == 3:
                    sp.dma_start(CON[:], const_d).then_inc(sem("const_loaded"), 16)
            sp.dma_start(SML[:], small_d).then_inc(sem("small_loaded"), 16)
            turns = (last_chunk - RAW) // RAW

            def load(c, slot, at):
                sp.wait_ge(w_low_dve, c - RAW + 1)
                sp.wait_ge(w_low_pool, c - RAW + 1)
                sp.dma_start(WR[:, slot], at).then_inc(raw_loaded[slot], 16)

            with sp.Fori(0, turns) as t:
                for s in range(RAW):
                    c = t * RAW + RAW + s
                    load(c, s, stream_d[bass.ds(c, 1)].rearrange("a p n -> p (a n)"))
            for c in range(RAW + turns * RAW, last_chunk):
                load(c, c % RAW, stream_d[c])
            for b in range(4):
                sp.wait_ge(sem("result"), b + 1)
                sp.dma_start(out_d[:, 2 * b:2 * b + 2, :], X[:, 2 * b:2 * b + 2, :]).then_inc(sem("stored"), 16)
            sp.wait_ge(sem("stored"), 64)

        @block.tensor
        def _(pe):
            def chunk_ready(c):
                pe.wait_ge(w_low_dve, c + 1)
                pe.wait_ge(w_low_pool, c + 1)

            def acc_ready(t):
                pe.wait_ge(acc_free, t - 1)

            def three(out, slot, cols, hi, lo, start, stop, n=P):
                wh, wl = WH[:, slot, cols:cols + n], WL[:, slot, cols:cols + n]
                pe.matmul(out, wh, hi, start=start, stop=False, skip_group_check=True)
                pe.matmul(out, wh, lo, start=False, stop=False, skip_group_check=True)
                return pe.matmul(out, wl, hi, start=False, stop=stop, skip_group_check=True)

            def sum_square(name, k):
                n = SQ_COUNT.get(name, 8)
                pe.wait_ge(sq_ready, SQ_BASE[name] + k + 1)
                ins = pe.matmul(mis[:, 0, 0:T], ONES[:, :], SQ[:, k], start=k == 0, stop=k == n - 1,
                                skip_group_check=True)
                if k == n - 1:
                    ins.then_inc(nps_ready, 1)

            def sum_squares(name):
                for k in range(SQ_COUNT.get(name, 8)):
                    sum_square(name, k)

            def summed_squares(name):
                pe.wait_ge(sem("ssum_ready"), SUMMED.index(name) + 1)
                pe.matmul(mis[:, 0, 0:T], ONES[:, :], SSUM[:, :], start=True, stop=True,
                          skip_group_check=True).then_inc(nps_ready, 1)

            def rstd_columns(out, name):
                pe.wait_ge(rstd_ready, NORM[name] + 1)
                for tt in range(TT):
                    ins = pe.matmul(out[:, tt:tt + 1], RS[:, tt * P:tt * P + P], con("ident", 0, 1), start=True, stop=True,
                                    skip_group_check=True)
                ins.then_inc(sem("rst_ps"), 1)

            def tile(c, t, hi, lo, base=None, slot=None, bank=None, first=False, norm=None):
                slot = c % SPL if slot is None else slot
                bank = t % 2 if bank is None else bank
                chunk_ready(c)
                if not first:
                    acc_ready(t)
                for k in range(KD):
                    if base is not None:
                        pe.wait_ge(base[0], base[1] + k + 1)
                    ins = three(acc[:, bank, 0:T], slot, k * P, hi[:, k], lo[:, k], k == 0, k == KD - 1)
                    if k == KD - 1:
                        ins.then_inc(w_used, 1)
                    if norm is not None:
                        sum_square(norm, k)

            def token_part(c0, t0, hi, lo, i, halves=range(2)):
                if i == 0 and 0 in halves:
                    acc_ready(t0)
                    acc_ready(t0 + 1)
                c = c0 + i
                if 0 in halves:
                    chunk_ready(c)
                for k in halves:
                    kk = 2 * i + k
                    wh, wl = (w[:, c % SPL, k * 512:k * 512 + 512] for w in (WH, WL))
                    for tt in range(TT):
                        o = acc[:, (t0 + tt) % 2, :]
                        xh, xl = (x[:, kk, tt * P:tt * P + P] for x in (hi, lo))
                        pe.matmul(o, xh, wh, start=kk == 0, stop=False, skip_group_check=True)
                        pe.matmul(o, xh, wl, start=False, stop=False, skip_group_check=True)
                        ins = pe.matmul(o, xl, wh, start=False, stop=kk == KD - 1, skip_group_check=True)
                if 1 in halves:
                    ins.then_inc(w_used, 1)

            def token_major(c0, t0, hi, lo, halfway=None):
                for i in range(4):
                    token_part(c0, t0, hi, lo, i)
                    if i == 1 and halfway is not None:
                        halfway()

            xl0 = (xl_ready, 8 * PREP["mix"])
            pe.wait_ge(sem("ones_done"), 3)
            for j in range(6):
                c = START["xbc"] + j
                tile(c, j, XH, XL, base=xl0 if j == 0 else None, first=j < 2, norm="mix" if j == 0 else None)
                if j == 3:
                    pe.wait_ge(sem("const_loaded"), 16)
                    rstd_columns(mis[:, 1, 16:18], "mix")
                    sum_squares("mem")
            for name in ("q", "k", "z"):
                for j in range(4):
                    tile(START[name] + j, TILE[name] + j, XH, XL)
            token_major(START["v"], TILE["v"], XH, XL)
            pe.wait_ge(sem("small_loaded"), 16)
            for tt in range(TT):
                for k in range(KD):
                    ins = pe.matmul(mis[:, 1, tt * 8:tt * 8 + 8], G[:, k, tt * P:tt * P + P],
                                    small("w_dt")[:, k * 8:k * 8 + 8], start=k == 0, stop=k == KD - 1,
                                    skip_group_check=True)
            ins.then_inc(sem("dt_ps"), 1)

            def mem_key(j):
                tile(START["mem_k"] + j, TILE["mem_k"] + j, YH, YL, base=(yl_ready, Y_BASE["mem"]) if j == 0 else None)

            pe.wait_ge(sem("xb_done"), 6)
            for c in range(TT):
                for j in range(4):
                    ins = pe.transpose(big[:, c, j * P:j * P + P], XB[:, j, c * P:c * P + P], con("ident"))
                ins.then_inc(sem("xs_ps"), 1)
            for c in range(TT):
                for g in range(2):
                    h = slice(64 * g, 64 * g + 64)
                    ins = pe.matmul(big[:, 2 + g, c * P:c * P + P], XB[h, 4, c * P:c * P + P],
                                    XB[h, 5, c * P:c * P + P], start=True, stop=True, skip_group_check=True)
            ins.then_inc(sem("cb_ps"), 1)
            pe.transpose(big[:, 3, 256:384], XB[:, 4, 0:P], con("ident")).then_inc(sem("bt_ps"), 1)
            mem_key(0)
            mem_key(1)
            pe.wait_ge(sem("an_done"), 1)
            for c in range(TT):
                pe.matmul(mis[:, 1, 32 + 8 * c:40 + 8 * c], con("tri"), AN[:, c, :], start=True, stop=True,
                          skip_group_check=True)
            pe.matmul(mis[:, 1, 48:56], ONES[:, :], AN[:, 0, :], start=True, stop=True,
                      skip_group_check=True).then_inc(sem("acl_ps"), 1)
            pe.wait_ge(sem("abc_done"), 1)
            pe.wait_ge(sem("xs_read"), 1)
            for c in range(TT):
                for h in range(8):
                    ins = pe.matmul(big[:, 2 * c + h // 4, (h % 4) * P:(h % 4 + 1) * P], ABC[:, c, h, :], con("tri"),
                                    start=True, stop=True, skip_group_check=True)
                ins.then_inc(sem("seg_ps"), 1)
            mem_key(2)
            pe.wait_ge(sem("xcd_done"), 1)
            for g in range(2):
                ins = pe.matmul(mis[64 * g:64 * g + 64, 0, 0:256], BT[:, 64 * g:64 * g + 64],
                                XCD[:, 256 * g:256 * g + 256], start=True, stop=True, skip_group_check=True)
            ins.then_inc(sem("st_ps"), 1)
            mem_key(3)
            def scores(h):
                p = h // 2
                if h >= 2:
                    pe.wait_ge(sem("sb_arg"), h - 1)
                z, k = big[:, h % 2, :], KT[:, h % 2, p, :]
                pe.matmul(z[:, 0:T], k[:, 0:P], QT[:, p, :], start=True, stop=True, skip_group_check=True)
                pe.matmul(z[:, T:T + P], k[:, P:T], QT[:, p, P:T], start=False, stop=True,
                          skip_group_check=True).then_inc(sem("sb_z"), 1)

            pe.wait_ge(sem("seg_done"), 16)
            scores(0)
            for c in range(TT):
                pe.wait_ge(sem("mm_done"), c + 1)
                if c == 1:
                    pe.wait_ge(sem("ce_done"), 1)
                for h in range(8):
                    p, g = h // 2, h // 4
                    half = slice(64 * (h % 2), 64 * (h % 2) + 64)
                    o = big[half, 2 + p // 2, (p % 2) * T + c * P:(p % 2) * T + c * P + P]
                    ins = pe.matmul(o, XC[:, c, 64 * h:64 * h + 64], MM[c][:, h, :], start=True, stop=c == 0,
                                    skip_group_check=True)
                    if c == 1:
                        gs = slice(64 * g, 64 * g + 64)
                        ins = pe.matmul(o, ST[gs, (h % 4) * 64:(h % 4) * 64 + 64], CE[gs, h % 4, :], start=False,
                                        stop=True, skip_group_check=True)
            ins.then_inc(sem("y_ps"), 1)

            def later(h):
                pe.wait_ge(sem("sb_sp"), h + 1)
                z, s = big[:, h % 2, :], SBP[:, h % 2, :]
                pe.matmul(z[:, 0:T], con("neg_upto"), s[:, 0:T], start=False, stop=True, skip_group_check=True)
                pe.matmul(z[:, P:T], con("neg_ones"), s[:, T:T + P], start=False, stop=True, skip_group_check=True)
                pe.matmul(z[:, T:T + P], con("neg_upto"), s[:, T:T + P], start=False, stop=True,
                          skip_group_check=True).then_inc(sem("sb_c"), 1)

            def outputs(h):
                half, p = slice(64 * (h % 2), 64 * (h % 2) + 64), h // 2
                pe.wait_ge(sem("sb_w"), h + 1)
                if p >= 2:
                    pe.wait_ge(sem("os_done"), p - 1)
                o, w = big[half, 2 + p % 2, 0:T], SBW[:, h % 2, :]
                pe.matmul(o, V[:, 0, 64 * h:64 * h + 64], w[:, 0:T], start=True, stop=False, skip_group_check=True)
                pe.matmul(o[:, P:T], V[:, 1, 64 * h:64 * h + 64], w[:, T:T + P], start=False, stop=True,
                          skip_group_check=True).then_inc(sem("sb_o"), 1)

            for i in range(SB_HEADS + 2):
                if 1 <= i < SB_HEADS:
                    scores(i)
                if 1 <= i <= SB_HEADS:
                    later(i - 1)
                if i < SB_HEADS:
                    token_part(START["mem_v"], TILE["mem_v"], YH, YL, i // 2, halves=[i % 2])
                if i == 2:
                    pe.wait_ge(sem("y_read"), 1)
                if i >= 2:
                    outputs(i - 2)
                if i == 3:
                    sum_squares("ssd")
            sum_squares("sb")

            for j in range(KD):
                tile(START["w_out"] + j, TILE["w_out"] + j, YH, YL, base=(yl_ready, Y_BASE["mixer"]) if j == 0 else None)
            def xa_scores(h):
                pe.wait_ge(acc_free, TILE["xq"] + h + 1)
                if h >= 2:
                    pe.wait_ge(sem("xa_p"), h - 1)
                for tt in range(TT):
                    ins = pe.matmul(big[:, h % 2, tt * T:tt * T + T], QT[:, h, tt * P:tt * P + P], MK[:, h, :],
                                    start=True, stop=True, skip_group_check=True)
                ins.then_inc(sem("xa_s"), 1)

            def xa_turn(h):
                pe.wait_ge(sem("xa_pn"), h + 1)
                if h >= 1:
                    pe.wait_ge(sem("xa_pt"), h)
                for m in range(2):
                    for tt in range(TT):
                        ins = pe.transpose(big[:, 2, m * T + tt * P:m * T + tt * P + P],
                                           SEG_P(h)[:, tt, m * P:m * P + P], con("ident"))
                ins.then_inc(sem("xa_t"), 1)

            def xa_out(h):
                pe.wait_ge(sem("xa_pt"), h + 1)
                if h >= 2:
                    pe.wait_ge(yl_ready, Y_BASE["xa"] + h - 1)
                for m in range(2):
                    ins = pe.matmul(XO(h), MV[:, m, h * P:h * P + P],
                                    XPT(h)[:, m, :], start=m == 0, stop=m == 1, skip_group_check=True)
                ins.then_inc(sem("xa_o"), 1)

            for i in range(XA_HEADS + 3):
                if i < XA_HEADS:
                    tile(START["xq"] + i, TILE["xq"] + i, XH, XL, base=(xl_ready, 8 * PREP["xa"]) if i == 0 else None)
                if i == 0:
                    summed_squares("xa")
                if 1 <= i <= XA_HEADS:
                    xa_scores(i - 1)
                if 2 <= i <= XA_HEADS + 1:
                    xa_turn(i - 2)
                if i >= 3:
                    xa_out(i - 3)
            for i in range(4):
                c = START["xo"] + i
                chunk_ready(c)
                for m in range(2):
                    t = TILE["xo"] + 2 * i + m
                    acc_ready(t)
                    for k in range(4):
                        if i == 0 and m == 0:
                            pe.wait_ge(yl_ready, Y_BASE["xa"] + k + 1)
                        ins = three(acc[:, t % 2, 0:T], c % SPL, (4 * m + k) * P, YH[:, k], YL[:, k], k == 0, k == 3)
                    ins.then_inc(sem("xo_half") if m == 0 else w_used, 1)

            def wide(c, slot, us, first, last):
                chunk_ready(c)
                for m in range(KD):
                    o = big[:, m // 2, (m % 2) * T:(m % 2) * T + T]
                    ins = three(o, slot, m * P, UH[:, us], UL[:, us], first and m % 2 == 0, last)
                ins.then_inc(w_used, 1)

            u_low = sem("u_low")
            C0, T0 = START["ff"], TILE["ff"]
            tile(C0, T0, XH, XL, base=(xl_ready, 8 * PREP["ff"]))
            summed_squares("ff")
            tile(C0 + 1, T0 + 1, XH, XL)
            pe.wait_ge(u_low, 1)
            wide(C0 + 2, (C0 + 2) % SPL, 0, True, False)
            S = 6
            with pe.Fori(0, 4) as t:
                for u in range(S):
                    j = 2 + u
                    tile(t * 12 + (C0 + 2 * j - 1), t * 6 + (T0 + j), XH, XL, slot=(C0 + 2 * j - 1) % SPL,
                         bank=(T0 + j) % 2)
                    pe.wait_ge(u_low, t * 6 + j)
                    wide(t * 12 + (C0 + 2 * j), (C0 + 2 * j) % SPL, (j - 1) % 2, False, False)
            for j in range(26, FF_TILES):
                tile(C0 + 2 * j - 1, T0 + j, XH, XL)
                pe.wait_ge(u_low, j)
                wide(C0 + 2 * j, (C0 + 2 * j) % SPL, (j - 1) % 2, False, False)
            pe.wait_ge(u_low, FF_TILES)
            wide(C0 + 2 * FF_TILES - 1, (C0 + 2 * FF_TILES - 1) % SPL, (FF_TILES - 1) % 2, False, True)
            sum_squares("final")
            def gated(j):
                for i in (2 * j, 2 * j + 1):
                    tile(START["pw1"] + i, TILE["pw1"] + i, XH, XL, base=(xl_ready, 8 * PREP["mix2_0"]) if i == 0 else None,
                         norm="mix2_0" if i == 0 else None)

            def taps(j):
                pe.wait_ge(sem("up_ready"), j + 1)
                pe.wait_ge(sem("diagonals"), j + 1)
                if j >= 4:
                    pe.wait_ge(sem("cx_whole"), j - 3)
                for i in range(PE_TAPS):
                    ins = pe.matmul(big[:, j % 4, 0:T], DG[:, j % 2, i, :], UPAD[:, j, i:i + T], start=i == 0,
                                    stop=i == PE_TAPS - 1, skip_group_check=True)
                ins.then_inc(sem("taps_ps"), 1)

            def sum_features(j):
                pe.wait_ge(sem("cx_whole"), j + 1)
                return pe.matmul(mis[:, 1, 0:T], ONES[:, :], CX[:, j], start=j == 0, stop=j == KD - 1,
                                 skip_group_check=True)

            gated(0)
            for j in range(KD):
                if j + 1 < KD:
                    gated(j + 1)
                taps(j)
                if j >= 1:
                    sum_features(j - 1)
            sum_features(KD - 1).then_inc(sem("mean_ps"), 1)
            sum_squares("ln")
            for j in range(KD):
                tile(START["pw2"] + j, TILE["pw2"] + j, YH, YL, base=(yl_ready, Y_BASE["pw2"]) if j == 0 else None)

            def ffn(i):
                C0, T0 = START[f"ffn{i}"], TILE[f"ffn{i}"]
                base_u = FF_TILES + i * UP_TILES
                tile(C0, T0, XH, XL, base=(xl_ready, 8 * PREP[f"ffn2_{i}"]))
                summed_squares(f"ffn2_{i}")
                tile(C0 + 1, T0 + 1, XH, XL)

                def step(c, tl, uc, cs, ts, us, first):
                    tile(c, tl, XH, XL, slot=cs % SPL, bank=ts % 2)
                    tile(c + 1, tl + 1, XH, XL, slot=(cs + 1) % SPL, bank=(ts + 1) % 2)
                    pe.wait_ge(u_low, uc)
                    wide(c + 2, (cs + 2) % SPL, us % 2, first, False)

                for t, js in turns_of_up(pe):
                    cs, ts, us = C0 + 3 * js - 1, T0 + 2 * js, base_u + js
                    step(plus(t, 12, cs), plus(t, 8, ts), plus(t, 4, us), cs, ts, js - 1, js == 1)
                pe.wait_ge(u_low, base_u + UP_TILES)
                c = C0 + 3 * UP_TILES - 1
                wide(c, c % SPL, (UP_TILES - 1) % 2, False, True)

            ffn(0)
            pe_nsa(pe, tile, token_major, three, rstd_columns, chunk_ready, acc_ready)
            for j in range(KD):
                tile(START["nsa_out"] + j, TILE["nsa_out"] + j, YH, YL, base=(yl_ready, Y_BASE["nsa"]) if j == 0 else None)
            ffn(1)

        @block.scalar
        def _(act):
            ch = Chain(act, act_chain)
            link = ch.link

            def high(turn, per, cs):
                act.wait_ge(raw_loaded[cs % RAW], plus(turn, 16 * per // RAW, 16 * (cs // RAW + 1)))
                if cs >= SPL:
                    act.wait_ge(w_used, plus(turn, per, cs - SPL + 1))
                act.activation(WH[:, cs % SPL], WR[:, cs % RAW], ACT.Copy).then_inc(w_high, 1)

            sp = Splitter(high)

            def prep_one(name, k):
                act.wait_ge(gx_ready, 8 * PREP[name] + k + 1)
                act.activation(XH[:, k], G[:, k], ACT.Copy).then_inc(xh_ready, 1)
                act.activation(SQ[:, k], X[:, k], ACT.Square).then_inc(sq_ready, 1)

            def prep(name):
                for k in range(KD):
                    prep_one(name, k)

            def rstd(name, out):
                act.wait_ge(nps_ready, NORM[name] + 1)
                e = EPS[:, int(NORM[name] > NORM["final"]):int(NORM[name] > NORM["final"]) + 1]
                link(act.activation(LNV[:, :], mis[:, 0, 0:T], ACT.Ln, bias=e, scale=1.0 / NORM_DIM.get(name, D)))
                act.activation(out[:, :], LNV[:, :], ACT.Exp, scale=-0.5).then_inc(rstd_ready, 1)

            def y_high(stage, k):
                act.wait_ge(gy_ready, GY_BASE[stage] + k + 1)
                act.activation(YH[:, k], GY[:, k], ACT.Copy).then_inc(yh_ready, 1)

            act.preload_act_table_set("natural_log_exp_and_others")
            sp.to(1)
            prep("mix")
            sp.to(3)
            act.wait_ge(sem("ones_done"), 3)
            rstd("mix", RS)
            link(act.activation(EAL[:, :], VEC[:, VCOL["a_log"]:VCOL["a_log"] + 8], ACT.Exp))
            sp.to(4)
            act.wait_ge(sem("mem_loaded"), 16)
            for k in range(KD):
                act.activation(SQ[:, k], MEM[:, k], ACT.Square).then_inc(sq_ready, 1)
            sp.to(4 + AHEAD)
            rstd("mem", RS2)
            for j in range(6):
                act.wait_ge(sem("cv_done"), j + 1)
                act.activation(XB[:, j], CV[:, j], ACT.Silu).then_inc(sem("xb_done"), 1)
                sp.to(5 + AHEAD + j)
            for k in range(8):
                sp.to(11 + AHEAD + k)
                y_high("mem", k)
            act.wait_ge(acc_free, TILE["z"] + 4)
            act.activation(ZT[:, :, :], ZT[:, :, :], ACT.Silu).then_inc(sem("z_silu"), 1)
            sp.to(START["mem_k"] + AHEAD)
            act.preload_act_table_set("natural_log_exp_and_others")
            act.wait_ge(sem("dtr_done"), 1)
            link(act.activation(DTE[:, :, :], DTE[:, :, :], ACT.Exp))
            act.activation(DTE[:, :, :], DTE[:, :, :], ACT.Ln, bias=1.0).then_inc(sem("dte_done"), 1)
            sp.to(START["mem_k"] + 2 + AHEAD)
            act.wait_ge(sem("ds_in"), 1)
            act.activation(DS[:, :], DS[:, :], ACT.Exp).then_inc(sem("ds_done"), 1)
            act.wait_ge(sem("seg_ps"), 2)
            act.activation(EA[:, :, :], big[:, 2:4, :].rearrange("p a (h l) -> p (a h) l", h=4),
                           ACT.Exp).then_inc(sem("ea_done"), 1)
            for c in range(TT):
                act.wait_ge(sem("seg_done"), 8 * c + 8)
                act.activation(SEG[c], SEG[c], ACT.Exp).then_inc(sem("seg_exp"), 1)
                sp.to(START["mem_k"] + 3 + c + AHEAD)

            def sb_soft(h):
                act.wait_ge(sem("sb_z"), h + 1)
                e = SBE[:, h % 2, 0:384]
                link(act.activation(e, big[:, h % 2, 0:384], ACT.Abs))
                link(act.activation(e, e, ACT.Exp, scale=-1.0))
                act.activation(e, e, ACT.Ln, bias=1.0).then_inc(sem("sb_ln"), 1)

            def sb_exp(h):
                act.wait_ge(sem("sb_arg"), h + 1)
                w = SBW[:, h % 2, 0:384]
                act.activation(w, w, ACT.Exp).then_inc(sem("sb_we"), 1)

            for i in range(SB_HEADS + 1):
                sp.to(START["mem_v"] + min(i // 2, 3) + 1 + AHEAD)
                if i < SB_HEADS:
                    sb_soft(i)
                if i >= 1:
                    sb_exp(i - 1)
                if i == 1:
                    for p in range(4):
                        act.wait_ge(sem("ys_done"), p + 1)
                        act.activation(SQ[:, p], YS(p), ACT.Square).then_inc(sq_ready, 1)
                if i == 4:
                    rstd("ssd", RS2)
            for k in range(4):
                y_high("mixer", k)
            for p in range(4):
                act.wait_ge(sem("os_done"), p + 1)
                act.activation(SQ[:, p], OS[:, p], ACT.Square).then_inc(sq_ready, 1)
            rstd("sb", RS2)
            for k in range(4, 8):
                y_high("mixer", k)
            for j in range(KD):
                sp.to(START["w_out"] + j + 1 + AHEAD)
                prep_one("xa", j)
            sp.to(START["xq"] + 1 + AHEAD)
            rstd("xa", RS)

            def xa_exp(h):
                act.wait_ge(sem("xa_nm"), h + 1)
                for tt in range(TT):
                    ch.add(act.activation(SEG_P(h)[:, tt, :], big[:, h % 2, tt * T:tt * T + T], ACT.Exp,
                                          bias=XSTAT[:, 0, h % 2, tt:tt + 1], accum_out=XSTAT[:, 1, h % 2, tt:tt + 1]))
                act.wait_ge(act_chain, ch.value())
                act.sem_inc(sem("xa_p"), 1)

            for i in range(XA_HEADS + 3):
                if i < XA_HEADS:
                    sp.to(START["xq"] + i + 1 + AHEAD)
                if 1 <= i <= XA_HEADS:
                    xa_exp(i - 1)
                if 2 <= i <= XA_HEADS + 1:
                    h = i - 2
                    act.wait_ge(sem("xa_t"), h + 1)
                    act.activation(XPT(h).rearrange("p m t -> p (m t)"), big[:, 2, :],
                                   ACT.Copy).then_inc(sem("xa_pt"), 1)
                if i >= 3:
                    h = i - 3
                    act.wait_ge(sem("xa_o"), h + 1)
                    act.activation(YH[:, h], XO(h), ACT.Copy).then_inc(yh_ready, 1)
            for i in range(4):
                sp.to(START["xo"] + i + 1 + AHEAD)
                prep_one("ff", 2 * i)
                prep_one("ff", 2 * i + 1)

            gu_ready, u_high = sem("gu_ready"), sem("u_high")

            def u_split(turn, per, us):
                act.wait_ge(gu_ready, plus(turn, per, us + 1))
                act.activation(UH[:, us % 2], GU[:, us % 2], ACT.Copy).then_inc(u_high, 1)

            C0 = START["ff"]
            sp.to(C0 + 1 + AHEAD)
            rstd("ff", RS)
            for j in range(2):
                u_split(0, 0, j)
                sp.to(C0 + 2 + j + AHEAD)
            with act.Fori(0, 4) as t:
                for u in range(6):
                    j = 2 + u
                    sp.in_loop(t, 12, C0 + 2 * j + 2)
                    u_split(t, 6, j)
                    sp.in_loop(t, 12, C0 + 2 * j + 3)
            sp.ran(48)
            for j in range(26, FF_TILES):
                sp.to(C0 + 2 * j + 0 + AHEAD)
                u_split(0, 0, j)
                sp.to(C0 + 2 * j + 1 + AHEAD)
            sp.to(START["pw1"] + AHEAD)
            for k in range(KD):
                if k % 2 == 0:
                    act.wait_ge(sem("x_res"), k // 2 + 1)
                act.activation(SQ[:, k], X[:, k], ACT.Square).then_inc(sq_ready, 1)
            rstd("final", RS2)
            prep("mix2_0")

            C0 = START["pw1"]
            sp.to(C0 + 1 + AHEAD)
            rstd("mix2_0", RS)
            for j in range(8):
                sp.to(C0 + 2 * j + 1 + AHEAD)
                act.wait_ge(acc_free, TILE["pw1"] + 2 * j + 1)
                act.activation(SG[:, j % 2], SG[:, j % 2], ACT.Sigmoid,
                               bias=vec("b_pw1", 2 * j)).then_inc(sem("gate_done"), 1)
                sp.to(C0 + 2 * j + 2 + AHEAD)
            act.preload_act_table_set("natural_log_exp_and_others")
            for k in range(KD):
                act.wait_ge(sem("cx_centred"), k + 1)
                act.activation(SQ[:, k], CX[:, k], ACT.Square).then_inc(sq_ready, 1)
            rstd("ln", RS2)
            for k in range(KD):
                act.wait_ge(gy_ready, GY_BASE["pw2"] + k + 1)
                silu = ch.add(act.activation(GY[:, k], GY[:, k], ACT.Silu, bias=vec("ln_b", k), scale=vec("ln_g", k)))
                if k >= 1:
                    act.wait_ge(act_chain, silu - 1)
                    act.activation(YH[:, k - 1], GY[:, k - 1], ACT.Copy).then_inc(yh_ready, 1)
            act.wait_ge(act_chain, silu)
            act.activation(YH[:, KD - 1], GY[:, KD - 1], ACT.Copy).then_inc(yh_ready, 1)
            for j in range(KD):
                sp.to(START["pw2"] + j + 1 + AHEAD)
                prep_one("ffn2_0", j)

            def ffn(i):
                C0 = START[f"ffn{i}"]
                base_u, base_s = FF_TILES + i * UP_TILES, i * UP_TILES

                def silu(turn, js):
                    act.wait_ge(sem("fconv_done"), plus(turn, 4, base_s + js + 1))
                    act.activation(SA[:, js % 2], CA[:, js % 2], ACT.Silu).then_inc(sem("fsilu_done"), 1)

                sp.to(C0 + 1 + AHEAD)
                act.preload_act_table_set("natural_log_exp_and_others")
                rstd(f"ffn2_{i}", RS)
                silu(0, 0)
                sp.to(C0 + 2 + AHEAD)
                u_split(0, 0, base_u)
                for t, js in turns_of_up(act):
                    cs = C0 + 3 * js - 1
                    if isinstance(t, int):
                        sp.to(cs + 2 + AHEAD)
                        silu(0, js)
                        u_split(0, 0, base_u + js)
                        sp.to(cs + 3 + AHEAD)
                    else:
                        sp.in_loop(t, 12, cs + 3)
                        sp.in_loop(t, 12, cs + 4)
                        silu(t, js)
                        u_split(t, 4, base_u + js)
                        sp.in_loop(t, 12, cs + 5)
                        if js == 1 + UP_STEPS:
                            sp.ran(12 * UP_TURNS)

            ffn(0)
            sp.to(START["nsa_kc"] + AHEAD)
            prep("mix2_1")
            act_nsa(act, ch, sp, rstd)
            for j in range(KD):
                sp.to(START["nsa_out"] + j + 1 + AHEAD)
                prep_one("ffn2_1", j)
            ffn(1)

        @block.vector
        def _(dve):
            ch = Chain(dve, dve_chain)
            link = ch.link

            def low(turn, per, cs):
                dve.wait_ge(w_high, plus(turn, per, cs + 1))
                dve.tensor_tensor(WL[:, cs % SPL, 0:LO_DVE], WR[:, cs % RAW, 0:LO_DVE],
                                  WH[:, cs % SPL, 0:LO_DVE].bitcast(F32), ALU.subtract).then_inc(w_low_dve, 1)

            sp = Splitter(low)

            def gx(name, k):
                i = int(name[-1]) if name[-2] == "_" else 0
                dve.tensor_scalar(G[:, k], X[:, k], vec(GAIN[name], 8 * i + k), None,
                                  ALU.mult).then_inc(gx_ready, 1)

            def used(c, turn=0, per=0):
                dve.wait_ge(w_used, plus(turn, per, c + 1))

            def scaled(out, ts, turn=0, per=0, wait=True):
                dve.tensor_tensor(out, acc[:, ts % 2, 0:T], RS[:, :], ALU.mult).then_inc(acc_free, 1)
                if wait:
                    dve.wait_ge(acc_free, plus(turn, per, ts + 1))

            def add_square(name, k, before=[0]):
                if k == 0:
                    return
                dve.wait_ge(sq_ready, SQ_BASE[name] + k + 1)
                if k > 1:
                    dve.wait_ge(dve_chain, before[0])
                ins = dve.tensor_tensor(SSUM[:, :], SQ[:, 0] if k == 1 else SSUM[:, :], SQ[:, k], ALU.add)
                if k < KD - 1:
                    before[0] = ch.add(ins)
                else:
                    ins.then_inc(sem("ssum_ready"), 1)

            def residual(ts, k, name):
                link(dve.tensor_tensor(X[:, k], acc[:, ts % 2, 0:T], X[:, k], ALU.add))
                dve.sem_inc(acc_free, 1)
                gx(name, k)
                if k > 0:
                    add_square(name, k - 1)
                if k == KD - 1:
                    add_square(name, k)

            def rstd_done(name):
                dve.wait_ge(rstd_ready, NORM[name] + 1)

            dve.memset(XP[:, :, 0:3], 0.0)
            for e in range(2):
                dve.memset(KT[64 * (1 - e):64 * (1 - e) + 64, e], 0.0)
            dve.wait_ge(sem("vec_loaded"), 16)
            for k in range(KD):
                if k % 2 == 0:
                    dve.wait_ge(sem(f"x_loaded{k // 2}"), 16)
                gx("mix", k)
            sp.to(2)
            rstd_done("mix")

            def conv_in(j):
                x = lambda i: XP[:, j, i:i + T]
                w = lambda i: vec("conv_w", 4 * j + i)
                link(dve.tensor_scalar(CV[:, j], x(0), w(0), vec("conv_b", j), ALU.mult, ALU.add))
                for i in range(1, 4):
                    ins = dve.scalar_tensor_tensor(CV[:, j], x(i), w(i), CV[:, j], ALU.mult, ALU.add)
                    if i < 3:
                        link(ins)
                ins.then_inc(sem("cv_done"), 1)

            for j in range(6):
                sp.to(j + 1 + AHEAD)
                used(START["xbc"] + j)
                scaled(XP[:, j, 3:3 + T], TILE["xbc"] + j)
                conv_in(j)
            for j in range(4):
                used(START["q"] + j)
                t = TILE["q"] + j
                dve.scalar_tensor_tensor(QT[:, j], acc[:, t % 2, 0:T], 0.125, RS[:, :], ALU.mult,
                                         ALU.mult).then_inc(acc_free, 1)
                sp.to(START["q"] + j + 1 + AHEAD)
            rstd_done("mem")
            dve.wait_ge(sem("mem_loaded"), 16)
            for k in range(KD):
                dve.scalar_tensor_tensor(GY[:, k], MEM[:, k], vec("mem_g", k), RS2[:, :], ALU.mult,
                                         ALU.mult).then_inc(gy_ready, 1)
            for j in range(4):
                sp.to(START["k"] + j + 1 + AHEAD)
                used(START["k"] + j)
                for e in range(2):
                    h = slice(64 * e, 64 * e + 64)
                    ins = dve.tensor_tensor(KT[h, e, j], acc[h, (TILE["k"] + j) % 2, 0:T], RS[h, :], ALU.mult)
                ins.then_inc(acc_free, 1)
            dve.wait_ge(sem("rst_ps"), 1)
            link(dve.tensor_copy(RST[:, :], mis[:, 1, 16:18]))
            for j in range(4):
                used(START["z"] + j)
                scaled(ZT[:, j], TILE["z"] + j, wait=False)
                sp.to(START["z"] + j + 1 + AHEAD)
            for i in range(4):
                sp.to(START["v"] + i + 1 + AHEAD)
            used(START["v"] + 3)
            for tt in range(TT):
                dve.tensor_scalar(V[:, tt], acc[:, (TILE["v"] + tt) % 2, :], RST[:, tt:tt + 1], None,
                                  ALU.mult).then_inc(acc_free, 1)
            dve.wait_ge(sem("dt_ps"), 1)
            for tt in range(TT):
                ins = dve.scalar_tensor_tensor(DTR[:, tt], mis[:, 1, tt * 8:tt * 8 + 8], RST[:, tt:tt + 1],
                                               VEC[:, VCOL["dt_bias"]:VCOL["dt_bias"] + 8], ALU.mult, ALU.add)
                link(ins)
            dve.scalar_tensor_tensor(DTE[:, :, :], DTR[:, :, :], -1.0, DTR[:, :, :], ALU.mult,
                                     ALU.min).then_inc(sem("dtr_done"), 1)
            sp.to(START["mem_k"] + AHEAD)
            dve.wait_ge(sem("dte_done"), 1)
            link(dve.scalar_tensor_tensor(DT[:, :, :], DTR[:, :, :], 0.0, DTE[:, :, :], ALU.max, ALU.add))
            link(dve.scalar_tensor_tensor(AN[:, :, :], DT[:, :, :], -1.0,
                                          EAL[:, :].unsqueeze(1).broadcast_to([P, TT, 8]), ALU.mult, ALU.mult))
            dve.sem_inc(sem("an_done"), 1)
            dve.tensor_copy(ABC.rearrange("p c h l -> p (c h) l"),
                            AN.rearrange("p c h -> p (c h)").unsqueeze(2).broadcast_to([P, 16, P])).then_inc(
                sem("abc_done"), 1)
            def mem_key(j):
                sp.to(START["mem_k"] + j + 1 + AHEAD)
                used(START["mem_k"] + j)
                dve.tensor_copy(MK[:, j], acc[:, (TILE["mem_k"] + j) % 2, 0:T]).then_inc(acc_free, 1)

            dve.wait_ge(sem("const_loaded"), 16)
            for c in range(TT):
                dve.wait_ge(sem("xs_ps"), c + 1)
                link(dve.tensor_tensor(XC[:, c].rearrange("p (h d) -> p h d", h=8),
                                       big[:, c, :].rearrange("p (h d) -> p h d", h=8),
                                       DT[:, c, :].unsqueeze(2).broadcast_to([P, 8, 64]), ALU.mult))
            dve.wait_ge(sem("bt_ps"), 1)
            dve.tensor_copy(BT[:, :], big[:, 3, 256:384])
            dve.wait_ge(sem("cb_ps"), 1)
            dve.tensor_tensor(CBM.rearrange("p (c g) s -> p g c s", c=2),
                              big[:, 2:4, 0:T].rearrange("p g (c s) -> p g c s", c=2),
                              con("tri").unsqueeze(1).unsqueeze(1).broadcast_to([P, 2, 2, P]),
                              ALU.mult).then_inc(sem("xs_read"), 1)
            dve.wait_ge(sem("acl_ps"), 1)
            link(dve.tensor_copy(ACL[:, :, :], mis[:, 1, 32:56].rearrange("p (c h) -> p c h", c=3)))
            dve.tensor_tensor(DS[:, :], ACL[:, 2, :], ACL[:, 0, :], ALU.subtract).then_inc(sem("ds_in"), 1)
            mem_key(0)
            mem_key(1)
            dve.wait_ge(sem("ds_done"), 1)
            dve.tensor_tensor(XCD[:, :].rearrange("p (h d) -> p h d", h=8), XC[:, 0].rearrange("p (h d) -> p h d", h=8),
                              DS[:, :].unsqueeze(2).broadcast_to([P, 8, 64]), ALU.mult).then_inc(sem("xcd_done"), 1)
            for c in range(TT):
                dve.wait_ge(sem("seg_ps"), c + 1)
                if c == 1:
                    dve.wait_ge(sem("ea_done"), 1)
                for h in range(8):
                    dve.tensor_scalar(SEG[c][:, h, :], big[:, 2 * c + h // 4, (h % 4) * P:(h % 4 + 1) * P],
                                      ACL[:, c, h:h + 1], 0.0, ALU.subtract, ALU.min).then_inc(sem("seg_done"), 1)
            for c in range(TT):
                mem_key(2 + c)
                dve.wait_ge(sem("seg_exp"), c + 1)
                dve.tensor_tensor(MM[c].rearrange("p (g e) l -> p g e l", g=2),
                                  SEG[c].rearrange("p (g e) l -> p g e l", g=2),
                                  CBM[:, 2 * c:2 * c + 2, :].unsqueeze(2).broadcast_to([P, 2, 4, P]),
                                  ALU.mult).then_inc(sem("mm_done"), 1)
            for g in range(2):
                gs = slice(64 * g, 64 * g + 64)
                link(dve.tensor_tensor(CE[gs, :, :], XB[gs, 5, P:T].unsqueeze(1).broadcast_to([64, 4, P]),
                                       EA[gs, 4 * g:4 * g + 4, :], ALU.mult))
            dve.wait_ge(sem("st_ps"), 1)
            dve.tensor_copy(ST[:, :], mis[:, 0, 0:256]).then_inc(sem("ce_done"), 1)
            dve.wait_ge(sem("y_ps"), 1)
            dve.wait_ge(sem("z_silu"), 1)
            for p in range(4):
                link(dve.scalar_tensor_tensor(XP[:, p, 0:T], XB[:, p], vec("d_skip", p),
                                              big[:, 2 + p // 2, (p % 2) * T:(p % 2) * T + T], ALU.mult, ALU.add))
                if p == 3:
                    dve.sem_inc(sem("y_read"), 1)
                dve.tensor_tensor(YS(p), XP[:, p, 0:T], ZT[:, p], ALU.mult).then_inc(sem("ys_done"), 1)

            def diagonal(x):
                return x.rearrange("p (a n) -> p a n", a=2)[:, :, 0:P]

            strict = con("strict").unsqueeze(1).broadcast_to([P, 2, P])

            def out_tile(p):
                dve.wait_ge(sem("sb_o"), 2 * p + 2)
                dve.tensor_copy(OS[:, p], big[:, 2 + p % 2, 0:T]).then_inc(sem("os_done"), 1)

            def arg(h):
                dve.wait_ge(sem("sb_c"), h + 1)
                if h >= 2:
                    dve.wait_ge(sem("sb_o"), h - 1)
                dve.tensor_scalar(SBW[:, h % 2, 0:384], big[:, h % 2, 0:384], 0.0, None,
                                  ALU.min).then_inc(sem("sb_arg"), 1)

            def weights(h):
                dve.wait_ge(sem("sb_we"), h + 1)
                d = diagonal(SBW[:, h % 2, :])
                dve.tensor_tensor(d, d, strict, ALU.mult).then_inc(sem("sb_w"), 1)

            for i in range(SB_HEADS + 1):
                sp.to(START["mem_v"] + min(i // 2, 3) + 1 + AHEAD)
                if i >= 1:
                    arg(i - 1)
                if i < SB_HEADS:
                    dve.wait_ge(sem("sb_ln"), i + 1)
                    s = SBP[:, i % 2, :]
                    link(dve.scalar_tensor_tensor(s[:, 0:384], big[:, i % 2, 0:384], 0.0, SBE[:, i % 2, 0:384],
                                                  ALU.max, ALU.add))
                    dve.tensor_tensor(diagonal(s), diagonal(s), strict, ALU.mult).then_inc(sem("sb_sp"), 1)
                if i >= 1:
                    weights(i - 1)
                if i == SB_HEADS:
                    used(START["mem_v"] + 3)
                    for tt in range(TT):
                        dve.tensor_copy(MV[:, tt], acc[:, (TILE["mem_v"] + tt) % 2, :]).then_inc(acc_free, 1)
                if i >= 4 and i % 2 == 0:
                    out_tile((i - 4) // 2)
                if i == 5:
                    rstd_done("ssd")
                    for k in range(4):
                        dve.scalar_tensor_tensor(GY[:, k], YS(k), vec("ssd_g", k), RS2[:, :], ALU.mult,
                                                 ALU.mult).then_inc(gy_ready, 1)
            out_tile(3)
            rstd_done("sb")
            for k in range(4):
                dve.scalar_tensor_tensor(GY[:, 4 + k], OS[:, k], vec("sb_g", k), RS2[:, :], ALU.mult,
                                         ALU.mult).then_inc(gy_ready, 1)
            for j in range(KD):
                used(START["w_out"] + j)
                residual(TILE["w_out"] + j, j, "xa")
                sp.to(START["w_out"] + j + 1 + AHEAD)
            for i in range(XA_HEADS + 3):
                if 2 <= i <= XA_HEADS + 1:
                    h = i - 2
                    dve.wait_ge(sem("xa_p"), h + 1)
                    link(dve.reciprocal(XSTAT[:, 2, h % 2, :], XSTAT[:, 1, h % 2, :]))
                    dve.tensor_tensor(SEG_P(h), SEG_P(h), XSTAT[:, 2, h % 2, :].unsqueeze(2).broadcast_to([P, TT, T]),
                                      ALU.mult).then_inc(sem("xa_pn"), 1)
                if i < XA_HEADS:
                    sp.to(START["xq"] + i + 1 + AHEAD)
                    used(START["xq"] + i)
                    if i == 0:
                        rstd_done("xa")
                    dve.scalar_tensor_tensor(QT[:, i], acc[:, (TILE["xq"] + i) % 2, 0:T], float(P) ** -0.5, RS[:, :],
                                             ALU.mult, ALU.mult).then_inc(acc_free, 1)
                if 1 <= i <= XA_HEADS:
                    h = i - 1
                    dve.wait_ge(sem("xa_s"), h + 1)
                    dve.tensor_reduce(XSTAT[:, 0, h % 2, :], big[:, h % 2, :].rearrange("p (a m) -> p a m", a=2), AX,
                                      ALU.max, negate=True).then_inc(sem("xa_nm"), 1)
                if i >= 3:
                    h = i - 3
                    dve.wait_ge(yh_ready, Y_BASE["xa"] + h + 1)
                    dve.tensor_tensor(YL[:, h], XO(h), YH[:, h].bitcast(F32),
                                      ALU.subtract).then_inc(yl_ready, 1)
            for i in range(4):
                dve.wait_ge(sem("xo_half"), i + 1)
                residual(TILE["xo"] + 2 * i, 2 * i, "ff")
                sp.to(START["xo"] + i + 1 + AHEAD)
                used(START["xo"] + i)
                residual(TILE["xo"] + 2 * i + 1, 2 * i + 1, "ff")

            gu_ready, u_low = sem("gu_ready"), sem("u_low")

            def hidden(turn, per, js):
                ts = TILE["ff"] + js
                scaled(TA[:, js % 2], ts, turn, per)
                if js >= 2:
                    dve.wait_ge(u_low, plus(turn, per, js - 1))
                dve.scalar_tensor_tensor(GU[:, js % 2], TA[:, js % 2], 0.0, TA[:, js % 2], ALU.max,
                                         ALU.mult).then_inc(gu_ready, 1)

            C0 = START["ff"]
            sp.to(C0 + 1 + AHEAD)
            rstd_done("ff")
            for j in range(2):
                used(C0 + j)
                hidden(0, 0, j)
                sp.to(C0 + 2 + j + AHEAD)
            with dve.Fori(0, 4) as t:
                for u in range(6):
                    j = 2 + u
                    sp.in_loop(t, 12, C0 + 2 * j + 2)
                    used(C0 + 2 * j - 1, t, 12)
                    hidden(t, 6, j)
                    sp.in_loop(t, 12, C0 + 2 * j + 3)
            sp.ran(48)
            for j in range(26, FF_TILES):
                sp.to(C0 + 2 * j + 0 + AHEAD)
                used(C0 + 2 * j - 1)
                hidden(0, 0, j)
                sp.to(C0 + 2 * j + 1 + AHEAD)
            sp.to(START["pw1"] + AHEAD)

            def add_wide(c, ready=None, norm=None):
                used(c)
                for b in range(4):
                    x = X[:, 2 * b:2 * b + 2, :].rearrange("p k t -> p (k t)")
                    link(dve.tensor_tensor(x, big[:, b, :], x, ALU.add))
                    if ready is not None:
                        dve.sem_inc(ready, 1)
                    if norm is not None:
                        gx(norm, 2 * b)
                        gx(norm, 2 * b + 1)

            add_wide(C0 + 2 * FF_TILES - 1, ready=sem("x_res"))
            rstd_done("final")
            for k in range(KD):
                link(dve.scalar_tensor_tensor(X[:, k], X[:, k], vec("final_g", k), RS2[:, :], ALU.mult, ALU.mult))
                gx("mix2_0", k)

            dve.memset(UPAD[:, :, 0:CONV_W - 1], 0.0)
            sp.to(START["pw1"] + 1 + AHEAD)
            rstd_done("mix2_0")

            def gate_half(j):
                used(START["pw1"] + 2 * j)
                scaled(SG[:, j % 2], TILE["pw1"] + 2 * j, wait=False)
                sp.to(START["pw1"] + 2 * j + 1 + AHEAD)

            def value_half(j):
                sp.to(START["pw1"] + 2 * j + 2 + AHEAD)
                used(START["pw1"] + 2 * j + 1)
                scaled(AT[:, j % 2], TILE["pw1"] + 2 * j + 1, wait=False)

            def gated(j):
                dve.wait_ge(acc_free, TILE["pw1"] + 2 * j + 2)
                dve.wait_ge(sem("gate_done"), j + 1)
                dve.scalar_tensor_tensor(UPAD[:, j, CONV_W - 1:], AT[:, j % 2], vec("b_pw1", 2 * j + 1), SG[:, j % 2],
                                         ALU.add, ALU.mult).then_inc(sem("up_ready"), 1)

            gate_half(0)
            value_half(0)
            gated(0)
            for j in range(KD + 1):
                even, odd = (CX[:, j], CB[:, j % 2]) if j < KD else (None, None)
                for n in range(CONV_W - PE_TAPS):
                    i = PE_TAPS + n
                    if j < KD:
                        x, w, o = UPAD[:, j, i:i + T], vec("w_dw", CONV_W * j + i), (even, odd)[n % 2]
                        if n == 0:
                            dve.wait_ge(sem("up_ready"), j + 1)
                            before = ch.add(dve.tensor_scalar(o, x, w, vec("b_dw", j), ALU.mult, ALU.add))
                        elif n == 1:
                            last = ch.add(dve.tensor_scalar(o, x, w, None, ALU.mult))
                        else:
                            dve.wait_ge(dve_chain, before)
                            before, last = last, ch.add(dve.scalar_tensor_tensor(o, x, w, o, ALU.mult, ALU.add))
                    if n == 2 and j >= 1:
                        if j == KD:
                            dve.wait_ge(dve_chain, last)
                        both = ch.add(dve.tensor_tensor(CX[:, j - 1], CX[:, j - 1], CB[:, (j - 1) % 2], ALU.add))
                    if n == 4 and j >= 1:
                        dve.wait_ge(sem("taps_ps"), j)
                        dve.wait_ge(dve_chain, both)
                        dve.tensor_tensor(CX[:, j - 1], CX[:, j - 1], big[:, (j - 1) % 4, 0:T],
                                          ALU.add).then_inc(sem("cx_whole"), 1)
                    if j + 1 < KD:
                        if n == 3:
                            gate_half(j + 1)
                        if n == 11:
                            value_half(j + 1)
                        if n == 12:
                            gated(j + 1)
            dve.wait_ge(sem("mean_ps"), 1)
            link(dve.tensor_scalar(MU[:, :], mis[:, 1, 0:T], 1.0 / D, None, ALU.mult))
            for k in range(KD):
                dve.tensor_tensor(CX[:, k], CX[:, k], MU[:, :], ALU.subtract).then_inc(sem("cx_centred"), 1)
            rstd_done("ln")
            for k in range(KD):
                dve.tensor_tensor(GY[:, k], CX[:, k], RS2[:, :], ALU.mult).then_inc(gy_ready, 1)
            for j in range(KD):
                used(START["pw2"] + j)
                t = TILE["pw2"] + j
                link(dve.scalar_tensor_tensor(X[:, j], acc[:, t % 2, 0:T], vec("b_pw2", j), X[:, j], ALU.add, ALU.add))
                dve.sem_inc(acc_free, 1)
                gx("ffn2_0", j)
                if j > 0:
                    add_square("ffn2_0", j - 1)
                sp.to(START["pw2"] + j + 1 + AHEAD)
            add_square("ffn2_0", KD - 1)

            def ffn(i):
                C0, T0 = START[f"ffn{i}"], TILE[f"ffn{i}"]
                base_u, base_s = FF_TILES + i * UP_TILES, i * UP_TILES

                def step(turn, js, ca):
                    def w(q):
                        col = VCOL["fconv"] + 4 * (i * UP_TILES + js) + q
                        return VEC[:, col:col + 1] if isinstance(turn, int) else VEC[:, bass.ds(turn * 16 + col, 1)]

                    per_c, per_t = 12, 8
                    s = js % 2
                    if isinstance(turn, int):
                        sp.to(ca + 1 + AHEAD)
                    else:
                        sp.in_loop(turn, 12, ca + 3)
                    used(ca, turn, per_c)
                    scaled(APD[:, s, 2:2 + T], T0 + 2 * js, turn, per_t)
                    ch.link(dve.tensor_scalar(CA[:, s], APD[:, s, 0:T], w(0), w(3), ALU.mult, ALU.add))
                    ch.link(dve.scalar_tensor_tensor(CA[:, s], APD[:, s, 1:1 + T], w(1), CA[:, s], ALU.mult, ALU.add))
                    dve.scalar_tensor_tensor(CA[:, s], APD[:, s, 2:2 + T], w(2), CA[:, s], ALU.mult,
                                             ALU.add).then_inc(sem("fconv_done"), 1)
                    if isinstance(turn, int):
                        sp.to(ca + 2 + AHEAD)
                    else:
                        sp.in_loop(turn, 12, ca + 4)
                    used(ca + 1, turn, per_c)
                    scaled(VA[:, s], T0 + 2 * js + 1, turn, per_t)
                    dve.wait_ge(sem("fsilu_done"), plus(turn, 4, base_s + js + 1))
                    dve.wait_ge(u_low, plus(turn, 4, base_u + js - 1))
                    dve.tensor_tensor(GU[:, s], VA[:, s], SA[:, s], ALU.mult).then_inc(gu_ready, 1)
                    if js > 0:
                        if isinstance(turn, int):
                            sp.to(ca + 3 + AHEAD)
                        else:
                            sp.in_loop(turn, 12, ca + 5)

                rstd_done(f"ffn2_{i}")
                step(0, 0, C0)
                for t, js in turns_of_up(dve, ch, 8):
                    step(t, js, C0 + 3 * js - 1)
                    if not isinstance(t, int) and js == 1 + UP_STEPS:
                        sp.ran(12 * UP_TURNS)
                add_wide(C0 + 3 * UP_TILES - 1, ready=sem("result") if i == 1 else None, norm="mix2_1" if i == 0 else None)

            dve.memset(APD[:, :, 0:2], 0.0)
            ffn(0)
            sp.to(START["nsa_kc"] + AHEAD)
            dve_nsa(dve, ch, sp, used, scaled, rstd_done)
            for j in range(KD):
                used(START["nsa_out"] + j)
                residual(TILE["nsa_out"] + j, j, "ffn2_1")
                sp.to(START["nsa_out"] + j + 1 + AHEAD)
            dve.memset(APD[:, :, 0:2], 0.0)
            ffn(1)

        @block.gpsimd
        def _(pool):
            def low(turn, per, cs):
                pool.wait_ge(w_high, plus(turn, per, cs + 1))
                pool.tensor_tensor(WL[:, cs % SPL, LO_DVE:], WR[:, cs % RAW, LO_DVE:],
                                   WH[:, cs % SPL, LO_DVE:].bitcast(F32), ALU.subtract).then_inc(w_low_pool, 1)

            sp = Splitter(low)

            def x_low(name, k):
                pool.wait_ge(xh_ready, 8 * PREP[name] + k + 1)
                pool.tensor_tensor(XL[:, k], G[:, k], XH[:, k].bitcast(F32), ALU.subtract).then_inc(xl_ready, 1)

            def y_low(stage, k):
                pool.wait_ge(yh_ready, Y_BASE[stage] + k + 1)
                pool.tensor_tensor(YL[:, k], GY[:, k], YH[:, k].bitcast(F32), ALU.subtract).then_inc(yl_ready, 1)

            def u_low_part(turn, per, us):
                pool.wait_ge(sem("u_high"), plus(turn, per, us + 1))
                pool.tensor_tensor(UL[:, us % 2], GU[:, us % 2], UH[:, us % 2].bitcast(F32),
                                   ALU.subtract).then_inc(sem("u_low"), 1)

            pool.memset(ONES[:, :], 1.0).then_inc(sem("ones_done"), 1)
            pool.memset(EPS[:, 0:1], EPS1).then_inc(sem("ones_done"), 1)
            pool.memset(EPS[:, 1:2], EPS2).then_inc(sem("ones_done"), 1)
            sp.to(1)
            for k in range(KD):
                x_low("mix", k)
            sp.to(10 + AHEAD)
            for k in range(KD):
                sp.to(11 + AHEAD + k)
                y_low("mem", k)
            sp.to(START["w_out"] + AHEAD)
            for k in range(8):
                y_low("mixer", k)
            for j in range(KD):
                sp.to(START["w_out"] + j + 1 + AHEAD)
                x_low("xa", j)
            sp.to(START["xo"] + AHEAD)
            for i in range(4):
                sp.to(START["xo"] + i + 1 + AHEAD)
                x_low("ff", 2 * i)
                x_low("ff", 2 * i + 1)
            C0 = START["ff"]
            sp.to(C0 + 1 + AHEAD)
            for j in range(2):
                u_low_part(0, 0, j)
                sp.to(C0 + 2 + j + AHEAD)
            with pool.Fori(0, 4) as t:
                for u in range(6):
                    j = 2 + u
                    sp.in_loop(t, 12, C0 + 2 * j + 2)
                    u_low_part(t, 6, j)
                    sp.in_loop(t, 12, C0 + 2 * j + 3)
            sp.ran(48)
            for j in range(26, FF_TILES):
                sp.to(C0 + 2 * j + 0 + AHEAD)
                u_low_part(0, 0, j)
                sp.to(C0 + 2 * j + 1 + AHEAD)
            sp.to(START["pw1"] + AHEAD)
            for k in range(KD):
                x_low("mix2_0", k)
            for j in range(KD):
                sp.to(START["pw1"] + 2 * j + AHEAD)
                if j >= 2:
                    pool.wait_ge(sem("taps_ps"), j - 1)
                w = VEC[:, VCOL["w_dw"] + CONV_W * j:VCOL["w_dw"] + CONV_W * j + PE_TAPS]
                pool.tensor_tensor(DG[:, j % 2], con("ident").unsqueeze(1).broadcast_to([P, PE_TAPS, P]),
                                   w.unsqueeze(2).broadcast_to([P, PE_TAPS, P]), ALU.mult).then_inc(sem("diagonals"), 1)
            sp.to(START["pw2"] + AHEAD)
            for k in range(KD):
                y_low("pw2", k)
            for j in range(KD):
                sp.to(START["pw2"] + j + 1 + AHEAD)
                x_low("ffn2_0", j)

            def ffn(i):
                C0 = START[f"ffn{i}"]
                base_u = FF_TILES + i * UP_TILES
                sp.to(C0 + 2 + AHEAD)
                u_low_part(0, 0, base_u)
                for t, js in turns_of_up(pool):
                    cs = C0 + 3 * js - 1
                    if isinstance(t, int):
                        sp.to(cs + 2 + AHEAD)
                        u_low_part(0, 0, base_u + js)
                        sp.to(cs + 3 + AHEAD)
                    else:
                        sp.in_loop(t, 12, cs + 3)
                        sp.in_loop(t, 12, cs + 4)
                        u_low_part(t, 4, base_u + js)
                        sp.in_loop(t, 12, cs + 5)
                        if js == 1 + UP_STEPS:
                            sp.ran(12 * UP_TURNS)

            ffn(0)
            sp.to(START["nsa_kc"] + AHEAD)
            for k in range(KD):
                x_low("mix2_1", k)
            pool_nsa(pool, sp)
            for j in range(KD):
                sp.to(START["nsa_out"] + j + 1 + AHEAD)
                x_low("ffn2_1", j)
            ffn(1)


def _features(v, n):
    return np.ascontiguousarray(v).reshape(n, P).T


def _outer(w, tiles):
    k = w.shape[0] // P
    return w.reshape(k, P, tiles, P).transpose(2, 1, 0, 3).reshape(tiles, P, k * P)


def _token(w):
    return w.reshape(4, 2, P, 512).transpose(0, 2, 1, 3).reshape(4, P, CH)


def _rows(w):
    return w.reshape(-1, P, CH)


def _constants():
    i = np.arange(P)
    f = np.float32
    rope = np.zeros((P, P), f)
    for b in (0, 64):
        for d in range(8):
            rope[b + d + 8, b + d] = -1.0
            rope[b + d, b + d + 8] = 1.0
    half = 8
    inv = (500000.0 ** (-np.arange(half, dtype=f) * (2.0 / 16))).astype(f)
    ang = (np.arange(T, dtype=f)[:, None] * inv[None, :]).astype(f)
    cos, sin = np.ones((P, T), f), np.zeros((P, T), f)
    for b in (0, 64):
        for d in range(16):
            cos[b + d], sin[b + d] = np.cos(ang[:, d % 8]), np.sin(ang[:, d % 8])
    end = np.arange(16) * 16 + 31
    t = np.arange(T).reshape(TT, P).T
    ok = (end[None, None, :] <= t[:, :, None]) & (np.arange(16) < N_CMP)[None, None, :]
    parts = {
        "ident": np.eye(P), "neg_ones": -np.ones((P, P)),
        "neg_upto": -(i[:, None] >= i[None, :]).astype(f), "tri": (i[:, None] <= i[None, :]),
        "strict": (i[:, None] < i[None, :]), "block_ones": (i[:, None] // 64 == i[None, :] // 64),
        "rope": rope, "neg_causal": np.where(i[None, :] <= i[:, None], 0.0, MASKED),
        "cmp_neg": np.where(ok, 0.0, MASKED).reshape(P, 32), "cmp_01": ok.reshape(P, 32),
        "v_mask": ((i[:, None] % 32) // 16 == i[None, :] // 64) & (i[:, None] % 16 < N_CMP),
        "cos": cos, "sin": sin,
    }
    return np.concatenate([np.asarray(parts[n], f) for n, _ in CONSTS], axis=1)


def kernel(**inputs):
    import concourse.bacc as bacc
    from concourse.bass_utils import run_bass_kernel_spmd

    a = {k: np.asarray(v) for k, v in inputs.items()}
    w_in = a["w_in"][0]
    z, xbc, dt, q, k, v = np.split(w_in, [512, 1280, 1288, 1800, 2312], axis=1)
    nsa = np.split(a["nsa_w_in_2"][0], list(np.cumsum([1024] + [256] * 6)), axis=1)
    order = [h for s in range(2) for i in range(4) for h in (8 * s + i, 8 * s + 4 + i)]
    heads = np.concatenate([np.arange(64 * h, 64 * h + 64) for h in order])
    pw1 = a["conv_w_pw1_2"][0]
    gate_then_a = np.concatenate([np.arange(P) + c for j in range(8) for c in (1024 + P * j, P * j)])

    def ff(w1, w2):
        up, down = _outer(w1, FF_TILES), _rows(w2)
        steps = [up[0:1]]
        for j in range(1, FF_TILES):
            steps += [up[j:j + 1], down[j - 1:j]]
        return np.concatenate(steps + [down[FF_TILES - 1:]])

    def ffn(w_up, w_down):
        up, down = _outer(w_up, 2 * UP_TILES), _rows(w_down)
        steps = [up[0:1], up[UP_TILES:UP_TILES + 1]]
        for j in range(1, UP_TILES):
            steps += [up[j:j + 1], up[UP_TILES + j:UP_TILES + j + 1], down[j - 1:j]]
        return np.concatenate(steps + [down[UP_TILES - 1:]])

    def cmp_w1(w):
        return w.reshape(4, 4, P, 256).transpose(0, 2, 1, 3).reshape(4, P, CH)

    values = np.stack([nsa[4].reshape(D, 4, 64), nsa[6].reshape(D, 4, 64)], axis=2).reshape(D, 512)
    queries = _outer(nsa[0][:, heads], 8)
    stream = [_outer(xbc, 6), _outer(q, 4), _outer(k, 4), _outer(z, 4), _token(v), _outer(a["w_xk"][0], 4),
              _token(a["w_xv"][0]), _outer(a["w_out"][0], 8), _outer(a["w_xq"][0], 4),
              _outer(a["w_xo"][0], 8).reshape(4, 2, P, 512).transpose(0, 2, 1, 3).reshape(4, P, CH),
              ff(a["w_ff1"][0], a["w_ff2"][0]), _outer(pw1[:, gate_then_a], 16), _outer(a["conv_w_pw2_2"][0], 8),
              ffn(a["ffn_w_up_2"][0], a["ffn_w_down_2"][0]),
              _outer(nsa[1], 2), _outer(nsa[2], 2), _outer(nsa[3], 2), _outer(nsa[5], 2), queries[:2],
              cmp_w1(a["nsa_ck_w1_2"][0]), cmp_w1(a["nsa_cv_w1_2"][0]), queries[2:], _token(values),
              _outer(a["nsa_w_out_2"][0][heads], 8), ffn(a["ffn_w_up_2"][1], a["ffn_w_down_2"][1])]
    stream = np.concatenate(stream)

    def taps(w, tiles):
        return w.reshape(w.shape[0], tiles, P).transpose(2, 1, 0).reshape(P, -1)

    def pairs(pe):
        return pe.reshape(16, P).T

    twice = lambda g: np.tile(g.reshape(64, 1), (2, 1))
    fconv = np.concatenate([np.concatenate([a["ffn_w_dw_2"][i], a["ffn_b_dw_2"][i][None]]) for i in range(2)])
    fconv = np.concatenate([taps(fconv[4 * i:4 * i + 4], UP_TILES) for i in range(2)], axis=1)
    columns = {
        "mix_g": _features(a["norm_mix_g"][0], 8), "conv_w": taps(a["conv_w"][0], 6), "conv_b": _features(a["conv_b"][0], 6),
        "d_skip": _features(np.repeat(a["d_skip"][0], 64), 4), "ssd_g": _features(a["ssd_norm_g"][0], 4),
        "sb_g": _features(a["sb_norm_g"][0], 4), "xa_g": _features(a["norm_xa_g"][0], 8),
        "mem_g": _features(a["norm_mem_g"][0], 8), "ff_g": _features(a["norm_ff_g"][0], 8),
        "final_g": _features(a["final_g"], 8), "mix2_g": _features(a["mix_norm_g_2"].reshape(-1), 16),
        "ffn2_g": _features(a["ffn_norm_g_2"].reshape(-1), 16),
        "b_pw1": _features(a["conv_b_pw1_2"][0][gate_then_a], 16),
        "w_dw": taps(a["conv_w_dw_2"][0], 8), "b_dw": _features(a["conv_b_dw_2"][0], 8),
        "ln_g": _features(a["conv_ln_g_2"][0], 8), "ln_b": _features(a["conv_ln_b_2"][0], 8),
        "b_pw2": _features(a["conv_b_pw2_2"][0], 8), "q_g": twice(a["nsa_q_norm_2"][0]), "kc_g": twice(a["nsa_kc_norm_2"][0]),
        "ks_g": twice(a["nsa_ks_norm_2"][0]), "kw_g": twice(a["nsa_kw_norm_2"][0]), "fconv": fconv,
        "pe_k": pairs(a["nsa_pe_k_2"][0]), "pe_v": pairs(a["nsa_pe_v_2"][0]),
        "dt_bias": np.tile(a["dt_bias"], (P, 1)), "a_log": np.tile(a["a_log"], (P, 1)),
    }
    vectors = np.concatenate([columns[n] for n, _ in VECTORS], axis=1)

    def by_tile(w):
        k = w.shape[0] // P
        return w.reshape(k, P, -1).transpose(1, 0, 2).reshape(P, -1)

    gate_cols = np.concatenate([nsa[7][:, 3 * h:3 * h + 3] for h in order], axis=1)
    smalls = np.concatenate([by_tile(dt), by_tile(gate_cols), by_tile(np.tile(a["nsa_ck_w2_2"][0], (1, 2))),
                             by_tile(np.tile(a["nsa_cv_w2_2"][0], (1, 2)))], axis=1)

    def feature_major(x):
        return x[0].T.reshape(KD, P, T).transpose(1, 0, 2)

    arrays = {"x_t": feature_major(a["x"]), "mem_t": feature_major(a["mem"]), "weights": stream, "vectors": vectors,
              "constants": _constants(), "small_weights": smalls}
    arrays = {n: np.ascontiguousarray(x) for n, x in arrays.items()}
    nc = bacc.Bacc("TRN2", target_bir_lowering=False, num_devices=1)
    args = [nc.dram_tensor(n, x.shape, F32, kind="ExternalInput").ap() for n, x in arrays.items()]
    args.append(nc.dram_tensor("result_t", (P, KD, T), F32, kind="ExternalOutput").ap())
    program(nc, *args)
    r = run_bass_kernel_spmd(nc, [arrays], core_ids=[0])
    got = r.results[0]["result_t"]
    return np.ascontiguousarray(got.transpose(1, 0, 2).reshape(D, T).T).reshape(1, T, D)
```
